# Optimizing a Trainium2 kernel written in Bass

```python
import math
import jax, jax.numpy as jnp
from jax import lax
import numpy as np

D_MODEL = 1024
BATCH = 1
SEQ = 512
DEPTH = 1
DEC_BATCH = 1
DEC_SEQ = 64
PAST_LEN = 1024

CHUNK = 64
Q_BLOCK = 128
HEAD_DIM = 64
GW = D_MODEL // 4
GROUP_HEADS = GW // HEAD_DIM
D_MIX = 4 * GW
CONV_WIDTH = 31
GDN_CONV_WIDTH = 4
RWKV_W_LORA = 16
RWKV_A_LORA = 16
RWKV_G_LORA = 32
N_EXPERT_GROUPS = 4
EXPERTS_PER_GROUP = 4
N_EXPERTS = N_EXPERT_GROUPS * EXPERTS_PER_GROUP
TOP_K_IN_GROUP = 2
D_EXPERT = 256
DN_ALPHA = (2 * DEPTH) ** 0.25
DN_BETA = (8 * DEPTH) ** -0.25
LN_EPS = 1e-5
GN_EPS = 64e-5
F32 = jnp.float32

CONV_COLS = 2 * GW
GDN_COLS = 4 * GW + 2 * GROUP_HEADS
RWKV_COLS = 3 * GW + RWKV_W_LORA + RWKV_A_LORA + RWKV_G_LORA
FOX_COLS = 3 * GW + GROUP_HEADS
N_IN = CONV_COLS + GDN_COLS + RWKV_COLS + FOX_COLS

kernel_name = 'hymba_conformer_gdn_rwkv7_fox_hmoe_step'

def layer_norm(x, g, b):
    xf = x.astype(F32)
    mu = jnp.mean(xf, -1, keepdims=True)
    var = jnp.mean(jnp.square(xf - mu), -1, keepdims=True)
    return ((xf - mu) * lax.rsqrt(var + LN_EPS) * g + b).astype(x.dtype)

def l2norm(x):
    xf = x.astype(F32)
    return xf * lax.rsqrt(jnp.sum(xf * xf, -1, keepdims=True) + 1e-6)

def causal_dwconv(buf, x, w):
    xp = jnp.concatenate([buf.astype(x.dtype), x], axis=1)
    out = lax.conv_general_dilated(xp, w[:, None, :].astype(x.dtype), window_strides=(1,), padding='VALID',
                                   dimension_numbers=('NWC', 'WIO', 'NWC'), feature_group_count=x.shape[-1])
    return out, xp[:, xp.shape[1] - (w.shape[0] - 1):]

def conv_module(hA, buf, conv_w, conv_b, ln_g, ln_b):
    val, gate = jnp.split(hA, 2, axis=-1)
    u = val * jax.nn.sigmoid(gate)
    c, new_buf = causal_dwconv(buf, u, conv_w)
    c = layer_norm(c + conv_b, ln_g, ln_b)
    return jax.nn.silu(c.astype(F32)), new_buf

def gdn_chunk(S, q, k, v, g, beta):
    L = q.shape[2]
    dv = v.shape[-1]
    G = jnp.cumsum(g, axis=-1)
    idx = jnp.arange(L)
    incl = idx[:, None] >= idx[None, :]
    strict = idx[:, None] > idx[None, :]
    decay = jnp.exp(jnp.where(incl, G[..., :, None] - G[..., None, :], -jnp.inf))
    kb = k * beta[..., None]
    A = jnp.where(strict, jnp.einsum('bhid,bhjd->bhij', kb, k) * decay, 0.0)
    eG = jnp.exp(G)[..., None]
    rhs = jnp.concatenate([v * beta[..., None], kb * eG], axis=-1)
    X = lax.linalg.triangular_solve(A, rhs, left_side=True, lower=True, unit_diagonal=True)
    u = X[..., :dv] - jnp.einsum('bhlk,bhkv->bhlv', X[..., dv:], S)
    o = (jnp.einsum('bhlk,bhkv->bhlv', q * eG, S)
         + jnp.einsum('bhij,bhjv->bhiv', jnp.einsum('bhid,bhjd->bhij', q, k) * decay, u))
    gl = G[..., -1:]
    S = S * jnp.exp(gl)[..., None] + jnp.einsum('bhjk,bhjv->bhkv', k * jnp.exp(gl - G)[..., None], u)
    return S, o

def gdn_mixer(hB, conv_buf, S0, conv_w, a_log, dt_bias, norm_w):
    B_, L, _ = hB.shape
    qkv, z, a, b = jnp.split(hB, [3 * GW, 4 * GW, 4 * GW + GROUP_HEADS], axis=-1)
    qkv, new_buf = causal_dwconv(conv_buf, qkv, conv_w)
    q, k, v = jnp.split(jax.nn.silu(qkv).astype(F32), 3, axis=-1)
    to_heads = lambda t: t.reshape(B_, L, GROUP_HEADS, HEAD_DIM).transpose(0, 2, 1, 3)
    q = l2norm(to_heads(q)) * HEAD_DIM ** -0.5
    k = l2norm(to_heads(k))
    v = to_heads(v)
    g = (-jnp.exp(a_log.astype(F32)) * jax.nn.softplus(a.astype(F32) + dt_bias)).transpose(0, 2, 1)
    beta = jax.nn.sigmoid(b.astype(F32)).transpose(0, 2, 1)
    S0 = S0.astype(F32)
    if L <= CHUNK:
        S, o = gdn_chunk(S0, q, k, v, g, beta)
    else:
        n = L // CHUNK
        to_c = lambda t: jnp.moveaxis(t.reshape(t.shape[:2] + (n, CHUNK) + t.shape[3:]), 2, 0)
        S, oc = lax.scan(lambda s, xs: gdn_chunk(s, *xs), S0, tuple(to_c(t) for t in (q, k, v, g, beta)))
        o = jnp.moveaxis(oc, 0, 2).reshape(B_, GROUP_HEADS, L, HEAD_DIM)
    o = o.transpose(0, 2, 1, 3)
    o = o * lax.rsqrt(jnp.mean(o * o, -1, keepdims=True) + 1e-6) * norm_w
    o = o * jax.nn.silu(z.astype(F32)).reshape(B_, L, GROUP_HEADS, HEAD_DIM)
    return o.reshape(B_, L, GW), new_buf, S

def rwkv7_scan(S0, r, w, k, v, a, b):
    def step(S, inp):
        r_t, w_t, k_t, v_t, a_t, b_t = inp
        Sa = jnp.einsum('bhvk,bhk->bhv', S, a_t)
        S = S * w_t[:, :, None, :] + Sa[..., None] * b_t[:, :, None, :] + v_t[..., None] * k_t[:, :, None, :]
        return S, jnp.einsum('bhvk,bhk->bhv', S, r_t)
    xs = tuple(jnp.moveaxis(t.astype(F32), 1, 0) for t in (r, w, k, v, a, b))
    S, y = lax.scan(step, S0.astype(F32), xs)
    return jnp.moveaxis(y, 0, 1), S

def rwkv_mixer(hC, shift_buf, S0, mu, w0, w_up, a0, a_up, g_up, k_k, k_a, r_k, lnx_g, lnx_b):
    B_, L, _ = hC.shape
    hf = hC.astype(F32)
    prev = jnp.concatenate([shift_buf[:, None].astype(F32), hf[:, :-1]], axis=1)
    xm = hf + (prev - hf) * mu
    r, k, v, xw, xa, xg = jnp.split(xm, [GW, 2 * GW, 3 * GW, 3 * GW + RWKV_W_LORA,
                                        3 * GW + RWKV_W_LORA + RWKV_A_LORA], axis=-1)
    w_pre = w0 + jnp.tanh(xw) @ w_up
    w = jnp.exp(-jnp.exp(-jax.nn.softplus(-w_pre) - 0.5))
    a = jax.nn.sigmoid(a0 + xa @ a_up)
    gate = jax.nn.sigmoid(xg) @ g_up
    heads = lambda t: t.reshape(B_, L, GROUP_HEADS, HEAD_DIM)
    kk = l2norm(heads(k * k_k))
    k = k * (1.0 + (a - 1.0) * k_a)
    r_h, k_h, v_h, a_h = heads(r), heads(k), heads(v), heads(a)
    y, S = rwkv7_scan(S0, r_h, heads(w), k_h, v_h, -kk, kk * a_h)
    mu_y = jnp.mean(y, -1, keepdims=True)
    var_y = jnp.mean(jnp.square(y - mu_y), -1, keepdims=True)
    yn = ((y - mu_y) * lax.rsqrt(var_y + GN_EPS)).reshape(B_, L, GW) * lnx_g + lnx_b
    bonus = jnp.sum(r_h * k_h * r_k, -1, keepdims=True) * v_h
    out = (yn + bonus.reshape(B_, L, GW)) * gate
    return out, hC[:, -1], S

def fox_attend(q, Fq, qpos, k, v, Fk, kpos):
    s = jnp.einsum('bqhd,bkhd->bhqk', q, k).astype(F32) * HEAD_DIM ** -0.5
    s = s + Fq.transpose(0, 2, 1)[..., :, None] - Fk.transpose(0, 2, 1)[..., None, :]
    s = jnp.where(kpos[None, None, None, :] <= qpos[None, None, :, None], s, -jnp.inf)
    p = jax.nn.softmax(s, axis=-1)
    return jnp.einsum('bhqk,bkhd->bqhd', p.astype(v.dtype), v)

def fox_prompt(q, k, v, logf):
    B_, S, H, d = q.shape
    F = jnp.cumsum(logf, axis=1)
    nb = S // Q_BLOCK
    qb = q.reshape(B_, nb, Q_BLOCK, H, d).transpose(1, 0, 2, 3, 4)
    Fb = F.reshape(B_, nb, Q_BLOCK, H).transpose(1, 0, 2, 3)
    pb = jnp.arange(S).reshape(nb, Q_BLOCK)
    kpos = jnp.arange(S)
    out = lax.map(lambda xs: fox_attend(xs[0], xs[1], xs[2], k, v, F, kpos), (qb, Fb, pb))
    return out.transpose(1, 0, 2, 3, 4).reshape(B_, S, H * d)

def fox_sample(q, k, v, logf, ck, cv, clogf):
    B_, L, H, d = q.shape
    P = ck.shape[1]
    k_all = jnp.concatenate([ck.astype(k.dtype), k], axis=1)
    v_all = jnp.concatenate([cv.astype(v.dtype), v], axis=1)
    F = jnp.cumsum(jnp.concatenate([clogf.astype(F32), logf], axis=1), axis=1)
    out = fox_attend(q, F[:, P:], P + jnp.arange(L), k_all, v_all, F, jnp.arange(P + L))
    return out.reshape(B_, L, H * d)

def hier_moe(x, wg, bg, we, be, w_gate, w_up, w_down):
    B_, L, D = x.shape
    xt = x.reshape(-1, D)
    T = xt.shape[0]
    pg = jax.nn.softmax((xt @ wg).astype(F32) + bg, axis=-1)
    gp, gi = lax.top_k(pg, 1)
    le = ((xt @ we).astype(F32) + be).reshape(T, N_EXPERT_GROUPS, EXPERTS_PER_GROUP)
    le = jnp.take_along_axis(le, gi[:, :, None], axis=1)[:, 0]
    ep, ei = lax.top_k(jax.nn.softmax(le, axis=-1), TOP_K_IN_GROUP)
    wts = gp * ep / jnp.sum(ep, -1, keepdims=True)
    eid = gi * EXPERTS_PER_GROUP + ei
    combine = jnp.sum(jax.nn.one_hot(eid, N_EXPERTS, dtype=F32) * wts[..., None], axis=1)
    y = jnp.zeros((T, D), F32)
    for e in range(N_EXPERTS):
        h = jax.nn.silu(xt @ w_gate[e]) * (xt @ w_up[e])
        y = y + combine[:, e:e + 1] * (h @ w_down[e]).astype(F32)
    return y.reshape(B_, L, D).astype(x.dtype)

def trunk_layer(x, lp, conv_buf, gdn_buf, gdn_S, rw_shift, rw_S, fox_cache):
    h = jnp.einsum('bld,dn->bln', x, lp['w_in'])
    hA, hB, hC, hD = jnp.split(h, [CONV_COLS, CONV_COLS + GDN_COLS, CONV_COLS + GDN_COLS + RWKV_COLS], axis=-1)
    oA, conv_buf = conv_module(hA, conv_buf, lp['conv_w'], lp['conv_b'], lp['conv_ln_g'], lp['conv_ln_b'])
    oB, gdn_buf, gdn_S = gdn_mixer(hB, gdn_buf, gdn_S, lp['gdn_conv_w'], lp['gdn_a_log'], lp['gdn_dt_bias'],
                                   lp['gdn_norm_w'])
    oC, rw_shift, rw_S = rwkv_mixer(hC, rw_shift, rw_S, lp['rwkv_mu'], lp['rwkv_w0'], lp['rwkv_w_up'],
                                    lp['rwkv_a0'], lp['rwkv_a_up'], lp['rwkv_g_up'], lp['rwkv_k_k'],
                                    lp['rwkv_k_a'], lp['rwkv_r_k'], lp['rwkv_lnx_g'], lp['rwkv_lnx_b'])
    B_, L, _ = x.shape
    qD, kD, vD, fD = jnp.split(hD, [GW, 2 * GW, 3 * GW], axis=-1)
    heads = lambda t: t.reshape(B_, L, GROUP_HEADS, HEAD_DIM)
    qD, kD, vD = heads(qD), heads(kD), heads(vD)
    logf = jax.nn.log_sigmoid(fD.astype(F32) + lp['fox_b_f'])
    if fox_cache is None:
        oD = fox_prompt(qD, kD, vD, logf)
    else:
        oD = fox_sample(qD, kD, vD, logf, fox_cache[0], fox_cache[1], fox_cache[2])
    mix = jnp.concatenate([oA, oB, oC, oD.astype(F32)], axis=-1).astype(x.dtype)
    x = layer_norm(DN_ALPHA * x + mix @ lp['w_out'], lp['ln1_g'], lp['ln1_b'])
    m = hier_moe(x, lp['router_g_w'], lp['router_g_b'], lp['router_e_w'], lp['router_e_b'],
                 lp['exp_w_gate'], lp['exp_w_up'], lp['exp_w_down'])
    x = layer_norm(DN_ALPHA * x + m, lp['ln2_g'], lp['ln2_b'])
    return x, (conv_buf, gdn_buf, gdn_S, rw_shift, rw_S, kD, vD, logf)

def setup_inputs(seed: int = 0) -> dict:
    keys = iter(jax.random.split(jax.random.key(seed), 64))
    def nrm(shape, scale=1.0):
        return scale * jax.random.normal(next(keys), shape, F32)
    def uni(shape, lo, hi):
        return jax.random.uniform(next(keys), shape, F32, lo, hi)
    H, Dh, D, E, FF, G = GROUP_HEADS, HEAD_DIM, D_MODEL, N_EXPERTS, D_EXPERT, N_EXPERT_GROUPS
    fox_bias = jnp.linspace(1.0, 7.0, H, dtype=F32)
    dt = jnp.exp(uni((DEPTH, H), math.log(1e-3), math.log(1e-1)))
    return {
        'x_prompt': nrm((BATCH, SEQ, D)),
        'x_sample': nrm((DEC_BATCH, DEC_SEQ, D)),
        'cache_fox_k': nrm((DEPTH, DEC_BATCH, PAST_LEN, H, Dh)),
        'cache_fox_v': nrm((DEPTH, DEC_BATCH, PAST_LEN, H, Dh)),
        'cache_fox_logf': jax.nn.log_sigmoid(fox_bias + nrm((DEPTH, DEC_BATCH, PAST_LEN, H))),
        'state_conv': nrm((DEPTH, DEC_BATCH, CONV_WIDTH - 1, GW), 0.5),
        'state_gdn_conv': nrm((DEPTH, DEC_BATCH, GDN_CONV_WIDTH - 1, 3 * GW)),
        'state_gdn': nrm((DEPTH, DEC_BATCH, H, Dh, Dh), 0.1),
        'state_rwkv_shift': nrm((DEPTH, DEC_BATCH, RWKV_COLS)),
        'state_rwkv': nrm((DEPTH, DEC_BATCH, H, Dh, Dh), 0.1),
        'w_in': nrm((DEPTH, D, N_IN), D ** -0.5),
        'conv_w': nrm((DEPTH, CONV_WIDTH, GW), CONV_WIDTH ** -0.5),
        'conv_b': nrm((DEPTH, GW), 0.01),
        'conv_ln_g': 1.0 + nrm((DEPTH, GW), 0.01),
        'conv_ln_b': nrm((DEPTH, GW), 0.01),
        'gdn_conv_w': nrm((DEPTH, GDN_CONV_WIDTH, 3 * GW), GDN_CONV_WIDTH ** -0.5),
        'gdn_a_log': jnp.log(uni((DEPTH, H), 1.0, 16.0)),
        'gdn_dt_bias': jnp.log(jnp.expm1(dt)),
        'gdn_norm_w': 1.0 + nrm((DEPTH, Dh), 0.01),
        'rwkv_mu': uni((DEPTH, RWKV_COLS), 0.0, 1.0),
        'rwkv_w0': uni((DEPTH, GW), -6.0, -1.0),
        'rwkv_w_up': nrm((DEPTH, RWKV_W_LORA, GW), 0.1),
        'rwkv_a0': nrm((DEPTH, GW), 0.1),
        'rwkv_a_up': nrm((DEPTH, RWKV_A_LORA, GW), RWKV_A_LORA ** -0.5),
        'rwkv_g_up': nrm((DEPTH, RWKV_G_LORA, GW), RWKV_G_LORA ** -0.5),
        'rwkv_k_k': 0.85 + nrm((DEPTH, GW), 0.01),
        'rwkv_k_a': 1.0 + nrm((DEPTH, GW), 0.01),
        'rwkv_r_k': nrm((DEPTH, H, Dh), 0.1),
        'rwkv_lnx_g': 1.0 + nrm((DEPTH, GW), 0.01),
        'rwkv_lnx_b': nrm((DEPTH, GW), 0.01),
        'fox_b_f': fox_bias + nrm((DEPTH, H), 0.1),
        'w_out': nrm((DEPTH, D_MIX, D), DN_BETA * D_MIX ** -0.5),
        'ln1_g': 1.0 + nrm((DEPTH, D), 0.01),
        'ln1_b': nrm((DEPTH, D), 0.01),
        'router_g_w': nrm((DEPTH, D, G), D ** -0.5),
        'router_g_b': nrm((DEPTH, G), 0.01),
        'router_e_w': nrm((DEPTH, D, E), D ** -0.5),
        'router_e_b': nrm((DEPTH, E), 0.01),
        'exp_w_gate': nrm((DEPTH, E, D, FF), D ** -0.5),
        'exp_w_up': nrm((DEPTH, E, D, FF), D ** -0.5),
        'exp_w_down': nrm((DEPTH, E, FF, D), DN_BETA * FF ** -0.5),
        'ln2_g': 1.0 + nrm((DEPTH, D), 0.01),
        'ln2_b': nrm((DEPTH, D), 0.01),
    }

def reference(x_prompt, x_sample, cache_fox_k, cache_fox_v, cache_fox_logf, state_conv, state_gdn_conv,
              state_gdn, state_rwkv_shift, state_rwkv, w_in, conv_w, conv_b, conv_ln_g, conv_ln_b,
              gdn_conv_w, gdn_a_log, gdn_dt_bias, gdn_norm_w, rwkv_mu, rwkv_w0, rwkv_w_up, rwkv_a0,
              rwkv_a_up, rwkv_g_up, rwkv_k_k, rwkv_k_a, rwkv_r_k, rwkv_lnx_g, rwkv_lnx_b, fox_b_f,
              w_out, ln1_g, ln1_b, router_g_w, router_g_b, router_e_w, router_e_b,
              exp_w_gate, exp_w_up, exp_w_down, ln2_g, ln2_b):
    xp, xs = x_prompt, x_sample
    bp, dt = x_prompt.shape[0], x_prompt.dtype
    outs_p = [[] for _ in range(8)]
    outs_s = [[] for _ in range(8)]
    for l in range(DEPTH):
        lp = {'w_in': w_in[l], 'conv_w': conv_w[l], 'conv_b': conv_b[l], 'conv_ln_g': conv_ln_g[l],
              'conv_ln_b': conv_ln_b[l], 'gdn_conv_w': gdn_conv_w[l], 'gdn_a_log': gdn_a_log[l],
              'gdn_dt_bias': gdn_dt_bias[l], 'gdn_norm_w': gdn_norm_w[l], 'rwkv_mu': rwkv_mu[l],
              'rwkv_w0': rwkv_w0[l], 'rwkv_w_up': rwkv_w_up[l], 'rwkv_a0': rwkv_a0[l],
              'rwkv_a_up': rwkv_a_up[l], 'rwkv_g_up': rwkv_g_up[l], 'rwkv_k_k': rwkv_k_k[l],
              'rwkv_k_a': rwkv_k_a[l], 'rwkv_r_k': rwkv_r_k[l], 'rwkv_lnx_g': rwkv_lnx_g[l],
              'rwkv_lnx_b': rwkv_lnx_b[l], 'fox_b_f': fox_b_f[l], 'w_out': w_out[l],
              'ln1_g': ln1_g[l], 'ln1_b': ln1_b[l], 'router_g_w': router_g_w[l],
              'router_g_b': router_g_b[l], 'router_e_w': router_e_w[l], 'router_e_b': router_e_b[l],
              'exp_w_gate': exp_w_gate[l], 'exp_w_up': exp_w_up[l], 'exp_w_down': exp_w_down[l],
              'ln2_g': ln2_g[l], 'ln2_b': ln2_b[l]}
        xp, st_p = trunk_layer(xp, lp,
                               jnp.zeros((bp, CONV_WIDTH - 1, GW), dt),
                               jnp.zeros((bp, GDN_CONV_WIDTH - 1, 3 * GW), dt),
                               jnp.zeros((bp, GROUP_HEADS, HEAD_DIM, HEAD_DIM), F32),
                               jnp.zeros((bp, RWKV_COLS), dt),
                               jnp.zeros((bp, GROUP_HEADS, HEAD_DIM, HEAD_DIM), F32),
                               None)
        xs, st_s = trunk_layer(xs, lp, state_conv[l], state_gdn_conv[l], state_gdn[l],
                               state_rwkv_shift[l], state_rwkv[l],
                               (cache_fox_k[l], cache_fox_v[l], cache_fox_logf[l]))
        for i in range(8):
            outs_p[i].append(st_p[i])
            outs_s[i].append(st_s[i])
    p_conv, p_gdn_conv, p_gdn, p_rwkv_shift, p_rwkv, p_fox_k, p_fox_v, p_fox_logf = [jnp.stack(o) for o in outs_p]
    s_conv, s_gdn_conv, s_gdn, s_rwkv_shift, s_rwkv, s_fox_k, s_fox_v, s_fox_logf = [jnp.stack(o) for o in outs_s]
    return (xp, xs, p_conv, p_gdn_conv, p_gdn, p_rwkv_shift, p_rwkv, p_fox_k, p_fox_v, p_fox_logf,
            s_conv, s_gdn_conv, s_gdn, s_rwkv_shift, s_rwkv, s_fox_k, s_fox_v, s_fox_logf)


_drawn_inputs = setup_inputs


def setup_inputs(seed=0):
    import zlib

    import numpy as np

    out = dict(_drawn_inputs(seed))
    spreads = {}
    factors = {'cache_fox_k': 2.77,
     'cache_fox_v': 2.802,
     'state_rwkv': 2.726,
     'conv_b': 6.216,
     'conv_ln_g': 5.086,
     'conv_ln_b': 8.0,
     'gdn_norm_w': 8.0,
     'rwkv_w_up': 2.741,
     'rwkv_k_k': 5.133,
     'rwkv_k_a': 5.103,
     'rwkv_lnx_g': 8.0,
     'rwkv_lnx_b': 8.0,
     'ln1_g': 3.579,
     'ln1_b': 3.779,
     'router_g_b': 5.73,
     'router_e_b': 8.0,
     'ln2_g': 5.795,
     'ln2_b': 5.529}
    for name, (base, spread) in spreads.items():
        noise = np.random.default_rng([zlib.crc32(name.encode()), seed]).standard_normal(out[name].shape)
        drawn = base * np.exp(spread * noise) if base else spread * noise
        out[name] = __import__('jax').numpy.asarray(drawn.astype(out[name].dtype))
    for name, factor in factors.items():
        out[name] = (out[name] * factor).astype(out[name].dtype)
    return out
```

```python
from contextlib import ExitStack

import numpy as np

import concourse.bass as bass
from concourse import mybir

F32 = mybir.dt.float32
ALU = mybir.AluOpType
ACT = mybir.ActivationFunctionType
AX = mybir.AxisListType.X

P = 128
D = 1024
KD = D // P
TP, TS = 512, 64
T = TP + TS
HALF = T // 2
HEADS, HD = 4, 64
GW = HEADS * HD
CHUNK = 64
PAST = 1024
CW = 31
CPAD = CW - 1
GTAPS = 4
PAD = GTAPS - 1
HW = 2 * PAD + T
SCOL = 2 * PAD + TP
TILES = [(0, 128), (128, 128), (256, 128), (384, 128), (512, 64)]
PIECES = [(0, TP, PAD), (TP, TS, SCOL)]
NT = len(TILES)
EXPERTS, FF = 16, 256
GROUPS = 4
DECAY = float(np.exp(-0.5))
ALPHA = 2.0 ** 0.25
LN_EPS, GN_EPS, RMS_EPS, L2_EPS = 1e-5, 64e-5, 1e-6, 1e-6
NEG = -1e30

SMALL, BQ, BK, BV, BZ, CR, CK, CV, DQ, DK, DV, VAL, GATE = 0, 1, 3, 5, 7, 9, 11, 13, 15, 17, 19, 21, 23
NCH = 25
RING = 4
ROWS = slice(96, 108)
TOP, LOW = slice(64, 128), slice(0, 64)

CONST = ["ident", "strict_l", "strict_u", "incl_u", "neg_strict_l", "neg_incl_u", "first_l", "first_u",
         "join2", "join4", "join8", "join16", "join32", "neg_causal", "head_ones", "mean_ones", "shift0", "shift1"]
SEL_G, SEL_F, SEL_PAIR, NSEL = 0, 4, 8, 10
PARAMS = [("conv_w", 2 * CW), ("conv_b", 2), ("conv_g", 2), ("conv_lb", 2), ("gconv_w", 6 * GTAPS),
          ("gnorm", 1), ("mu", 6), ("mu_s", 1), ("w0", 2), ("a0", 2), ("k_k", 2), ("k_a", 2), ("r_k", 2),
          ("lnx_g", 2), ("lnx_b", 2), ("row_bias", 1), ("row_alog", 1), ("row_sign", 1)]
PCOL, NPC = {}, 0
for _n, _k in PARAMS:
    PCOL[_n] = NPC
    NPC += _k


def own_order(engine, own):
    count = {}

    def mark(instruction, sem=None):
        sem = own if sem is None else sem
        count[sem.name] = count.get(sem.name, 0) + 1
        instruction.then_inc(sem, 1)

    def o(instruction, sem=None):
        mark(instruction, sem)
        sem = own if sem is None else sem
        engine.wait_ge(sem, count[sem.name])

    return o, mark


def step_kernel(nc, a):
    ctx = ExitStack()
    with ctx:
        def sb(name, words):
            return ctx.enter_context(nc.sbuf_tensor(name, [P, words], F32))

        def sem(name):
            return ctx.enter_context(nc.semaphore(name))

        def carve(region, at, *shape):
            n = int(np.prod(shape))
            v = region[:, at:at + n]
            if len(shape) > 1:
                names = "abcd"[:len(shape)]
                v = v.rearrange(f"p ({' '.join(names)}) -> p {' '.join(names)}",
                                **dict(zip(names[1:], shape[1:])))
            assert at + n <= region.shape[1], (region.name, at + n)
            return v, at + n

        def carve_all(region, at, *shapes):
            out = []
            for shape in shapes:
                v, at = carve(region, at, *shape)
                out.append(v)
            return out + [at]

        rH = sb("r_proj", NCH * HW)
        rX = sb("r_x", KD * T + RING * KD * P)
        rU = sb("r_unit", 14600)
        rG = sb("r_gdn", 10 * T)
        mixT, _ = carve(sb("mix", 8 * T), 0, 8, T)
        consts, _ = carve(sb("consts", len(CONST) * P), 0, len(CONST), P)
        sel, _ = carve(sb("sel", NSEL * P), 0, NSEL, P)
        par = sb("par", NPC)
        lora = sb("lora", GW)
        ch_mask = sb("chunk_mask", T)
        small = sb("small", 160)
        ps = ctx.enter_context(nc.psum_tensor("ps", [P, 8, 512], F32))

        def C(name):
            return consts[:, CONST.index(name), :]

        def pp(name, i=0, rows=slice(0, P)):
            at = PCOL[name] + i
            return par[rows, at:at + 1]

        ident = C("ident")

        hb, _ = carve(rH, 0, NCH, HW)
        xT, wat = carve(rX, 0, KD, T)
        wring = [carve(rX, wat + i * KD * P, KD, P)[0] for i in range(RING)]
        (rowy, rowG, rowGL, toks, uat) = carve_all(rU, 0, [T], [T], [T], [NT, 3, 12])
        beta, tG, nG, nbeg, eGL, decG, decR, eL = [small[:, i * 20:(i + 1) * 20] for i in range(8)]
        beta, tG, nG, nbeg, eGL = [v.rearrange("p (i h) -> p i h", h=4) for v in (beta, tG, nG, nbeg, eGL)]
        dec = sb("dec", 90)
        decG, decR = [dec[:, i * 36:(i + 1) * 36].rearrange("p (h c) -> p h c", c=9) for i in range(2)]
        eL = dec[:, 72:90].rearrange("p (h c) -> p h c", c=9)
        (rowz, rowt, Fp, Fs, kcT, vc, sc0, sc1, pT, vtok, _) = carve_all(
            rU, uat, [T], [T], [TP], [PAST + TS], [2, PAST], [8, GW], [PAST + TS], [PAST + TS], [2, T], [NT, GW])
        sc = [sc0, sc1]
        stat = sb("stat", 64)
        mx, rs = stat[:, 0:2], stat[:, 2:4]
        ealog = stat[:, 4:5]
        (cu, cacc, csig, ccen, csq, crs, _) = carve_all(
            rX, 0, [2, 2 * CPAD + T], [2, CPAD + T], [2, HW], [2, T], [2, T], [T])
        (gacc, gsig, _) = carve_all(rX, 0, [6, PAD + T], [6, PAD + T])
        (gsq, grs, geG, gz, _) = carve_all(rX, 0, [4, T], [4, T], [2, T], [2, HW])
        (gq, gk, gv, gR, gzs, _) = carve_all(rG, 0, [2, T], [2, T], [2, T], [2, T], [2, T])
        (xm, wsig, wcum, ta, tb, _) = carve_all(rX, 0, [7, T], [2, T], [2, T], [2, T], [2, T])
        (ac, bc, kc, rc, Au, Ru, Bb, Kb, gate, hat) = carve_all(rH, 0, *[[2, T]] * 9)
        bonus = xm[:, 2:4, :]
        xmv = xm[:, 4:6, :]
        U = []
        at = uat
        (N, NTm, ED, T1, QP, TPQ, BA, OUT, IS, NB, DmT, at) = carve_all(
            rU, at, [4, P], [4, P], [2, 4, P], [4, P], [4, P], [4, P], [4, 256], [4, 256], [5, 4, HD], [4, P], [4, P])
        U.append(dict(N=N, NT=NTm, ED=ED, T1=T1, QP=QP, TPQ=TPQ, BA=BA, OUT=OUT, IS=IS))
        (N, NTm, ED, T1, QP, TPQ, Aak, V, at) = carve_all(
            rU, at, [4, P], [4, P], [2, 4, P], [4, P], [4, P], [4, P], [4, P], [4, HD])
        (BA, KA, OUT, hat) = carve_all(rH, hat, [4, 256], [4, 256], [4, 256])
        IS, _ = carve(rX, 7 * T, 5, 4, HD)
        U.append(dict(N=N, NT=NTm, ED=ED, T1=T1, QP=QP, TPQ=TPQ, BA=BA, OUT=OUT, IS=IS))
        dg = [small[:, 0:1]] * 2
        (wout, xtok, _) = carve_all(rU, 0, [8, D], [NT, D])
        (x1, yacc, hT, hg, wr, logit, _) = carve_all(rH, 0, [NT, D], [NT, D], [2, T], [2, T], [KD, 20], [NT, 20])
        (lnp, _) = carve_all(rG, 0, [4, D])
        (x1T, rt, _) = carve_all(rX, 0, [KD, T], [1200])
        wgu = [carve(rU, i * 6144, KD, 2 * FF)[0] for i in range(2)]
        wdn = [carve(rU, i * 6144 + 4096, 2, D)[0] for i in range(2)]
        lasts = sb("lasts", 14)[:, :].rearrange("p (k c) -> p k c", k=2)
        bst = stat[:, 8:24]

        names = """ld_x ld_const ld_param ld_pad ld_cache ld_state ld_wout ld_xtok ld_lnp ld_router shift_rows
            proj_done evac_act evac_vec pads_zero zeros_set
            rows_neg rows_log rows_exp rows_done
            vt_pe vt_act s_done s_max s_exp p_ready t_done pt_copied pv_done o_act
            c_gate c_glu c_taps c_mean c_cen c_sq c_var c_rstd c_lin c_sig c_done
            g_taps g_sig g_silu g_sq g_sum g_rs g_pairs g_eg g_tokp g_tok g_texp g_zsig g_prep
            w_mix w_lora w_wa w_sg w_gatep w_gate w_cum w_e w_k1 w_sq w_ksum w_krs w_cprev w_e5 w_bon w_bonp w_prep w_eL
            u_tr u_tok u_A u_dexp u_N u_diag u_P u_Pq u_NTp u_NTs u_E0 u_D0 u_T1p u_T1 u_EDp u_ED u_TPQp u_TPQ
            u_OUTp u_OUTs u_OUTv u_Sp u_S u_Op u_O u_dec u_mask
            p_gsq p_gsum p_grs p_rsum p_rcen p_rsq p_rvar p_rrs p_done
            o_y o_x o_var o_rstd o_x1 o_x1t o_x1T o_log o_lg o_eg o_w2 o_comb
            m_gu m_silu m_h m_dn m_acc f_var f_rstd f_y
            st_hb st_rows st_conv st_state st_y pe_step vec_step act_step pool_step""".split()
        S = {n: sem(n) for n in names}
        ld_w = [sem(f"ld_w{i}") for i in range(RING)]
        ld_e = [sem(f"ld_e{i}") for i in range(2)]

        HEADP = [(h // 2, (h % 2) * HD) for h in range(HEADS)]
        mixer_bank = [0, 4]
        JOINS = ["join2", "join4", "join8", "join16", "join32"]

        def tile_cols(i):
            return PAD + TILES[i][0] if i < 4 else SCOL

        def bank4(b, n, rows=None):
            return ps[0:(rows or n), b, 0:4 * n].rearrange("p (h t) -> p h t", h=4)

        def par_pair(v):
            return v.rearrange("p (pair par) t -> p par pair t", par=2)

        def two_banks(b, n):
            return ps[:, b:b + 2, 0:n]

        def halves(v):
            return v.rearrange("p (u t) -> p u t", u=2)

        def chunks(v):
            return v.rearrange("p c (k t) -> p c k t", t=CHUNK)

        def bcast(v, shape):
            return v.to_broadcast(shape) if not isinstance(v, (int, float)) else v

        def bc_mid(v, k):
            return v.rearrange("p (o t) -> p o t", o=1).to_broadcast([v.shape[0], k, v.shape[1]])

        block = ctx.enter_context(nc.Block())

        @block.sync
        def _(sp):
            sp.dma_start(xT, a["xT"]).then_inc(S["ld_x"], 16)
            for j in range(NCH):
                if j >= RING:
                    sp.wait_ge(S["proj_done"], j - RING + 1)
                sp.dma_start(wring[j % RING], a["w_in"][j]).then_inc(ld_w[j % RING], 16)
            sp.wait_ge(S["evac_act"], NCH)
            sp.wait_ge(S["evac_vec"], NCH)
            sp.wait_ge(S["ld_pad"], 16)
            for k, end in enumerate((PAD + TP, HW)):
                sp.dma_start(a["o_gconv"][:, k], hb[:, BQ:BQ + 6, end - PAD:end]).then_inc(S["st_hb"], 16)
            sp.wait_ge(S["shift_rows"], 1)
            sp.dma_start(a["o_shift"], lasts).then_inc(S["st_hb"], 16)
            for t0, n, c0 in PIECES:
                sp.dma_start(a["o_kv"][:, :, t0:t0 + n], hb[:, DK:DK + 4, c0:c0 + n]).then_inc(S["st_hb"], 16)
            sp.wait_ge(S["rows_done"], 1)
            sp.dma_start(a["o_logf"], rowy[104:108, :]).then_inc(S["st_rows"], 16)
            sp.wait_ge(S["c_glu"], 1)
            for k, end in enumerate((CPAD + TP, 2 * CPAD + T)):
                sp.dma_start(a["o_conv"][:, k], cu[:, :, end - CPAD:end]).then_inc(S["st_conv"], 16)
            for m in range(2):
                sp.wait_ge(S["u_S"], 2 * 7 + 2 + m + 1 if m == 0 else 18)
            sp.wait_ge(S["u_S"], 18)
            for m in range(2):
                for k, slot in enumerate((2, 4)):
                    sp.dma_start(a["o_state"][m, k], U[m]["IS"][TOP, slot]).then_inc(S["st_state"], 16)
            sp.wait_ge(S["st_state"], 64)
            sp.wait_ge(S["u_O"], 2 * NT)
            sp.dma_start(wout, a["w_out"]).then_inc(S["ld_wout"], 16)
            for i, (t0, n) in enumerate(TILES):
                sp.dma_start(xtok[0:n, i], a["x_tok"][t0:t0 + n]).then_inc(S["ld_xtok"], 16)
            sp.wait_ge(S["p_done"], 1)
            for i in range(4):
                sp.dma_start(lnp[:, i], a["ln"][i:i + 1, :].to_broadcast([P, D])).then_inc(S["ld_lnp"], 16)
            sp.dma_start(wr, a["w_router"]).then_inc(S["ld_router"], 16)
            sp.dma_start(rt[:, 0:20], a["b_router"].to_broadcast([P, 20])).then_inc(S["ld_router"], 16)
            sp.wait_ge(S["o_x"], NT)
            for e in range(EXPERTS):
                if e >= 2:
                    sp.wait_ge(S["m_dn"], (e - 1) * NT)
                sp.dma_start(wgu[e % 2], a["w_gu"][e]).then_inc(ld_e[e % 2], 16)
                sp.dma_start(wdn[e % 2], a["w_dn"][e]).then_inc(ld_e[e % 2], 16)
            for i, (t0, n) in enumerate(TILES):
                sp.wait_ge(S["f_y"], i + 1)
                sp.dma_start(a["o_y"][t0:t0 + n], x1[0:n, i]).then_inc(S["st_y"], 16)
            sp.wait_ge(S["st_y"], 16 * NT)
            sp.wait_ge(S["st_hb"], 80)
            sp.wait_ge(S["st_rows"], 16)
            sp.wait_ge(S["st_conv"], 32)

        @block.gpsimd
        def _(pool):
            o, mark = own_order(pool, S["pool_step"])
            nc.gpsimd.memset(hb[:, :, 0:PAD], 0.0).then_inc(S["pads_zero"], 1)
            nc.gpsimd.memset(Fp, 0.0)
            nc.gpsimd.memset(Fs, 0.0)
            nc.gpsimd.memset(toks, 0.0).then_inc(S["zeros_set"], 1)
            pool.wait_ge(S["o_act"], 20)
            pool.wait_ge(S["w_mix"], 1)
            pool.wait_ge(S["st_hb"], 80)
            pool.wait_ge(S["w_prep"], 1)
            for u in U:
                nc.gpsimd.memset(u["BA"], 0.0)
                o(nc.gpsimd.memset(u["IS"], 0.0))
                for c in range(5):
                    for h in range(HEADS):
                        nc.gpsimd.affine_select(out=u["IS"][LOW, c, h], in_=u["IS"][LOW, c, h],
                                                compare_op=ALU.not_equal, fill=1.0, base=0,
                                                pattern=[[-1, HD]], channel_multiplier=1)
            nc.gpsimd.memset(KA, 0.0).then_inc(S["u_mask"], 1)
            for i, (t0, n) in enumerate(TILES):
                for m, u in enumerate(U):
                    k = 2 * i + m + 1
                    pool.wait_ge(S["u_N"], k)
                    d = u["N"][0:n, :, 0:n]
                    nc.gpsimd.affine_select(out=d, in_=d, compare_op=ALU.not_equal, fill=1.0, base=0,
                                            pattern=[[0, 4], [-1, n]], channel_multiplier=1).then_inc(S["u_diag"], 1)
                for m, u in enumerate(U):
                    k = 2 * i + m + 1
                    pool.wait_ge(S["u_diag"], k)
                    nc.gpsimd.tensor_tensor(u["ED"][0:n, 1, :, 0:n], u["N"][0:n, :, 0:n],
                                            bc_mid(C("first_l")[0:n, 0:n], 4), ALU.mult).then_inc(S["u_D0"], 1)

        @block.scalar
        def _(act):
            o, mark = own_order(act, S["act_step"])
            A = nc.scalar.activation
            act.dma_start(consts, a["consts"]).then_inc(S["ld_const"], 16)
            act.dma_start(sel, a["sel"]).then_inc(S["ld_const"], 16)
            act.dma_start(par[:, :], a["params"]).then_inc(S["ld_param"], 16)
            act.dma_start(lora[:, :], a["lora"]).then_inc(S["ld_param"], 16)
            act.dma_start(ch_mask[:, :], a["ch_mask"]).then_inc(S["ld_param"], 16)
            act.dma_start(hb[:, :, SCOL - PAD:SCOL], a["pads"]).then_inc(S["ld_pad"], 16)
            act.dma_start(kcT, a["k_cache"]).then_inc(S["ld_cache"], 16)
            act.dma_start(vc, a["v_cache"]).then_inc(S["ld_cache"], 16)
            act.dma_start(sc1[ROWS, 0:PAST], a["f_cache"]).then_inc(S["ld_cache"], 16)
            for j in range(NCH):
                act.wait_ge(S["proj_done"], j + 1)
                nc.scalar.copy(hb[:, j, PAD:PAD + HALF], ps[:, 2 * (j % RING), 0:HALF]).then_inc(S["evac_act"], 1)
            act.wait_ge(S["rows_neg"], 1)
            act.wait_ge(S["ld_param"], 48)
            o(A(rowt[ROWS, :], rowt[ROWS, :], ACT.Exp))
            A(ealog[ROWS, :], pp("row_alog", 0, ROWS), ACT.Exp)
            A(rowt[ROWS, :], rowt[ROWS, :], ACT.Ln, bias=1.0).then_inc(S["rows_log"], 1)
            for i, (t0, n) in enumerate(TILES):
                act.wait_ge(S["vt_pe"], i + 1)
                nc.scalar.copy(vtok[0:n, i], ps[0:n, 6 + i % 2, 0:GW]).then_inc(S["vt_act"], 1)
            units = [(i, h) for i in range(NT) for h in range(HEADS)]

            def exps(u):
                i, h = units[u]
                n = TILES[i][1]
                nk = P * (i + 1) if i < 4 else PAST + TS
                act.wait_ge(S["s_max"], u + 1)
                A(sc[u % 2][0:n, 0:nk], sc[u % 2][0:n, 0:nk], ACT.Exp, bias=mx[0:n, u % 2:u % 2 + 1],
                  accum_out=rs[0:n, u % 2:u % 2 + 1]).then_inc(S["s_exp"], 1)

            exps(0)
            for u, (i, h) in enumerate(units):
                n = TILES[i][1]
                pair, pb = HEADP[h]
                if u + 1 < len(units):
                    exps(u + 1)
                act.wait_ge(S["t_done"], u + 1)
                if i < 4:
                    nc.scalar.copy(pT[:, u % 2, 0:P * (i + 1)], ps[:, 6 + u % 2, 0:P * (i + 1)]).then_inc(S["pt_copied"], 1)
                else:
                    nc.scalar.copy(pT[:, u % 2, 0:512], ps[:, 6 + u % 2, :])
                    nc.scalar.copy(pT[LOW, u % 2, 512:T], ps[LOW, 3 * (u % 2) + 2, 64:128]).then_inc(S["pt_copied"], 1)
                act.wait_ge(S["pv_done"], u + 1)
                t0 = TILES[i][0]
                nc.scalar.copy(mixT[pb:pb + HD, 6 + pair, t0:t0 + n], ps[pb:pb + HD, 3 * (u % 2), 0:n]).then_inc(S["o_act"], 1)
            act.wait_ge(S["evac_vec"], NCH)
            act.dma_start(cu[:, :, CPAD + TP:2 * CPAD + TP], a["conv_state"]).then_inc(S["ld_state"], 16)
            A(csig, hb[:, GATE:GATE + 2, :], ACT.Sigmoid).then_inc(S["c_gate"], 1)
            act.wait_ge(S["c_cen"], 1)
            A(csq, ccen, ACT.Square).then_inc(S["c_sq"], 1)
            act.wait_ge(S["c_var"], 1)
            o(A(halves(crs), two_banks(2, HALF), ACT.Ln, bias=LN_EPS))
            A(crs, crs, ACT.Exp, scale=-0.5).then_inc(S["c_rstd"], 1)
            act.wait_ge(S["c_lin"], 1)
            A(csq, ccen, ACT.Sigmoid).then_inc(S["c_sig"], 1)
            act.wait_ge(S["g_taps"], 1)
            A(gsig, gacc, ACT.Sigmoid).then_inc(S["g_sig"], 1)
            act.wait_ge(S["g_silu"], 1)
            A(gsq, rG[:, 0:4 * T].rearrange("p (c t) -> p c t", c=4), ACT.Square).then_inc(S["g_sq"], 1)
            A(gz, hb[:, BZ:BZ + 2, :], ACT.Sigmoid).then_inc(S["g_zsig"], 1)
            act.wait_ge(S["g_sum"], 1)
            o(A(grs.rearrange("p c (u t) -> p (c u) t", u=2), ps[:, :, 0:HALF], ACT.Ln, bias=L2_EPS))
            A(grs, grs, ACT.Exp, scale=-0.5).then_inc(S["g_rs"], 1)
            act.wait_ge(S["g_pairs"], 1)
            A(geG.rearrange("p c (u t) -> p (c u) t", u=2), ps[:, 0:4, 0:HALF], ACT.Exp)
            A(decG[TOP], ps[TOP, 4, 0:36].rearrange("p (h c) -> p h c", c=9), ACT.Exp).then_inc(S["g_eg"], 1)
            act.wait_ge(S["g_tok"], 1)
            A(beta, toks[:, :, 0, 4:8], ACT.Exp)
            A(nbeg, tG, ACT.Exp)
            A(eGL, toks[:, :, 2, 0:4], ACT.Exp).then_inc(S["g_texp"], 1)
            act.wait_ge(S["w_mix"], 1)
            A(xm[0:16, 6], xm[0:16, 6], ACT.Tanh)
            A(xm[64:96, 6], xm[64:96, 6], ACT.Sigmoid).then_inc(S["w_lora"], 1)
            act.wait_ge(S["w_wa"], 1)
            for c in range(2):
                A(halves(wsig[:, c]), two_banks(2 * c, HALF), ACT.Sigmoid, bias=pp("w0", c))
                last = A(halves(ta[:, c]), two_banks(4 + 2 * c, HALF), ACT.Sigmoid, bias=pp("a0", c))
            last.then_inc(S["w_sg"], 1)
            act.wait_ge(S["w_gatep"], 1)
            act.wait_ge(S["st_hb"], 80)
            nc.scalar.copy(gate.rearrange("p c (u t) -> p (c u) t", u=2), ps[:, 0:4, 0:HALF]).then_inc(S["w_gate"], 1)
            act.wait_ge(S["w_cum"], 1)
            A(rc, tb, ACT.Exp, scale=-DECAY)
            A(kc, tb, ACT.Exp, scale=DECAY)
            A(Ru, wcum, ACT.Exp, scale=-DECAY)
            A(eL, eL, ACT.Exp, scale=-DECAY)
            for q in range(2):
                last = A(decR[TOP, q::2, :], wcum[q * HD:(q + 1) * HD, :, CHUNK - 1::CHUNK], ACT.Exp, scale=-DECAY)
            last.then_inc(S["w_e"], 1)
            act.wait_ge(S["w_cprev"], 1)
            A(ac, tb, ACT.Exp, scale=-DECAY)
            A(Au, wsig, ACT.Exp, scale=-DECAY).then_inc(S["w_e5"], 1)
            act.wait_ge(S["w_k1"], 1)
            A(tb, wsig, ACT.Square).then_inc(S["w_sq"], 1)
            act.wait_ge(S["w_ksum"], 1)
            o(A(tb.rearrange("p c (u t) -> p (c u) t", u=2), ps[:, 4:8, 0:HALF], ACT.Ln, bias=L2_EPS))
            A(tb, tb, ACT.Exp, scale=-0.5).then_inc(S["w_krs"], 1)
            act.wait_ge(S["u_mask"], 1)
            act.dma_start(U[0]["IS"][TOP, 3], a["s_gdn"]).then_inc(S["ld_state"], 16)
            act.dma_start(U[1]["IS"][TOP, 3], a["s_rwkv"]).then_inc(S["ld_state"], 16)
            act.wait_ge(S["w_prep"], 1)
            for i, (t0, n) in enumerate(TILES):
                nch = n // CHUNK
                k0 = 2 * i
                act.wait_ge(S["u_mask"], 2 + i)
                for h in range(HEADS):
                    A(NB[0:n, h, 0:n], NB[0:n, h, 0:n], ACT.Exp, bias=tG[0:n, i, h:h + 1])
                    last = A(DmT[0:n, h, 0:n], DmT[0:n, h, 0:n], ACT.Exp, bias=nG[0:n, i, h:h + 1])
                last.then_inc(S["u_dexp"], 1)
                act.wait_ge(S["u_tr"], k0 + 2)
                u = U[1]
                t4 = bank4(4, P, n)
                nc.scalar.copy(u["QP"][0:n, :, HD:P], ps[0:n, 4, 0:GW].rearrange("p (h t) -> p h t", h=4))
                nc.scalar.copy(V[0:n], ps[0:n, 4, GW:512].rearrange("p (h t) -> p h t", h=4))
                for c in range(nch):
                    r = slice(c * CHUNK, (c + 1) * CHUNK)
                    nc.scalar.copy(u["BA"][r, :, r], ps[r, 5, 0:GW].rearrange("p (h t) -> p h t", h=4))
                    last = nc.scalar.copy(KA[r, :, r], ps[r, 5, GW:512].rearrange("p (h t) -> p h t", h=4))
                last.then_inc(S["u_tok"], 1)
                for m, u in enumerate(U):
                    act.wait_ge(S["u_NTp"], k0 + m + 1)
                    nc.scalar.copy(u["NT"][0:n, :, 0:n], bank4(mixer_bank[m] + 1, n)).then_inc(S["u_NTs"], 1)
                for m, u in enumerate(U):
                    act.wait_ge(S["u_TPQp"], k0 + m + 1)
                    nc.scalar.copy(u["TPQ"][0:n], ps[0:n, mixer_bank[m] + 3, :].rearrange("p (h t) -> p h t", h=4)).then_inc(S["u_TPQ"], 1)
                for m, u in enumerate(U):
                    b = mixer_bank[m]
                    act.wait_ge(S["u_OUTp"], k0 + m + 1)
                    src = ps[:, b:b + 2, :].rearrange("p b (h t) -> p (b h) t", h=2)
                    nc.scalar.copy(u["OUT"][LOW, :, 0:P], src[LOW, :, 0:P])
                    nc.scalar.copy(u["OUT"][:, :, P:P + n], src[:, :, P:P + n]).then_inc(S["u_OUTs"], 1)
                for m, u in enumerate(U):
                    act.wait_ge(S["u_Op"], k0 + m + 1)
                    nc.scalar.copy(mixT[:, 2 + 2 * m:4 + 2 * m, t0:t0 + n],
                                   ps[:, mixer_bank[m] + 3, 0:2 * n].rearrange("p (c t) -> p c t", c=2)).then_inc(S["u_O"], 1)
            act.wait_ge(S["u_O"], 2 * NT)
            A(ta, mixT[:, 2:4], ACT.Square).then_inc(S["p_gsq"], 1)
            act.wait_ge(S["p_gsum"], 1)
            o(A(ta.rearrange("p c (u t) -> p (c u) t", u=2), ps[:, 0:4, 0:HALF], ACT.Ln, bias=RMS_EPS, scale=1.0 / HD))
            A(ta, ta, ACT.Exp, scale=-0.5).then_inc(S["p_grs"], 1)
            act.wait_ge(S["p_rcen"], 1)
            A(tb, mixT[:, 4:6], ACT.Square).then_inc(S["p_rsq"], 1)
            act.wait_ge(S["p_rvar"], 1)
            o(A(tb.rearrange("p c (u t) -> p (c u) t", u=2), ps[:, 0:4, 0:HALF], ACT.Ln, bias=GN_EPS, scale=1.0 / HD))
            A(tb, tb, ACT.Exp, scale=-0.5).then_inc(S["p_rrs"], 1)
            for i, (t0, n) in enumerate(TILES):
                act.wait_ge(S["o_var"], i + 1)
                o(A(stat[0:n, 24:25], stat[0:n, 21:22], ACT.Ln, bias=LN_EPS))
                A(stat[0:n, 24:25], stat[0:n, 24:25], ACT.Exp, scale=-0.5).then_inc(S["o_rstd"], 1)
                act.wait_ge(S["o_x1t"], i + 1)
                nc.scalar.copy(x1T[:, :, t0:t0 + n], ps[:, 4:6, 0:4 * n].rearrange("p b (k t) -> p b k t", t=n)).then_inc(S["o_x1T"], 1)
            act.wait_ge(S["o_lg"], 1)
            A(rt[:, 40:60], rt[:, 40:60], ACT.Exp).then_inc(S["o_eg"], 1)
            act.wait_ge(S["o_w2"], 1)
            A(rt[:, 60:65], rt[:, 60:65], ACT.Exp).then_inc(S["o_eg"], 1)
            for e in range(EXPERTS):
                for f in range(2):
                    act.wait_ge(S["m_gu"], 2 * e + f + 1)
                    if e >= 1:
                        act.wait_ge(S["m_h"], 2 * (e - 1) + f + 1)
                    A(halves(hg[:, f]), two_banks(4 * f, HALF), ACT.Silu).then_inc(S["m_silu"], 1)
            for i, (t0, n) in enumerate(TILES):
                act.wait_ge(S["f_var"], i + 1)
                o(A(stat[0:n, 24:25], stat[0:n, 21:22], ACT.Ln, bias=LN_EPS))
                A(stat[0:n, 24:25], stat[0:n, 24:25], ACT.Exp, scale=-0.5).then_inc(S["f_rstd"], 1)

        @block.vector
        def _(dve):
            o, mark = own_order(dve, S["vec_step"])
            v = nc.vector
            STT, TT, TSC = v.scalar_tensor_tensor, v.tensor_tensor, v.tensor_scalar
            for j in range(NCH):
                dve.wait_ge(S["proj_done"], j + 1)
                b = 2 * (j % RING) + 1
                k = TP - HALF
                v.tensor_copy(hb[:, j, PAD + HALF:PAD + TP], ps[:, b, 0:k])
                o(v.tensor_copy(hb[:, j, SCOL:SCOL + TS], ps[:, b, k:HALF]), S["evac_vec"])
            dve.wait_ge(S["evac_act"], NCH)
            for k, end in enumerate((PAD + TP, HW)):
                v.tensor_copy(lasts[:, k, 0:6], hb[:, CR:CR + 6, end - 1])
                last = v.tensor_copy(lasts[:, k, 6:7], hb[:, SMALL, end - 1:end])
            mark(last, S["shift_rows"])
            dve.wait_ge(S["evac_act"], NCH)
            dve.wait_ge(S["ld_param"], 48)
            dve.wait_ge(S["ld_cache"], 48)
            dve.wait_ge(S["zeros_set"], 1)
            for t0, n, c0 in PIECES:
                o(TSC(rowz[ROWS, t0:t0 + n], hb[ROWS, SMALL, c0:c0 + n], pp("row_bias", 0, ROWS),
                      pp("row_sign", 0, ROWS), ALU.add, ALU.mult))
            o(STT(rowt[ROWS, :], rowz[ROWS, :], -1.0, rowz[ROWS, :], ALU.mult, ALU.min), S["rows_neg"])
            dve.wait_ge(S["rows_log"], 1)
            o(STT(rowy[ROWS, :], rowz[ROWS, :], 0.0, rowt[ROWS, :], ALU.max, ALU.add))
            o(TSC(rowy[ROWS, :], rowy[ROWS, :], ealog[ROWS, :], -1.0, ALU.mult, ALU.mult))
            o(v.tensor_tensor_scan(rowG[ROWS, :], ch_mask[ROWS, :], rowy[ROWS, :], 0.0, ALU.mult, ALU.add))
            G3 = rowG[ROWS, :].rearrange("p (k t) -> p k t", t=CHUNK)
            o(TT(rowGL[ROWS, :].rearrange("p (k t) -> p k t", t=CHUNK),
                 G3[:, :, CHUNK - 1:CHUNK].to_broadcast([12, 9, CHUNK]), G3, ALU.subtract))
            SCAN = v.tensor_tensor_scan
            o(SCAN(Fp[ROWS, :], rowy[ROWS, 0:TP], rowy[ROWS, 0:TP], 0.0, ALU.add, ALU.min))
            o(SCAN(Fs[ROWS, 0:PAST], sc1[ROWS, 0:PAST], sc1[ROWS, 0:PAST], 0.0, ALU.add, ALU.min))
            o(SCAN(Fs[ROWS, PAST:], rowy[ROWS, TP:], rowy[ROWS, TP:], Fs[ROWS, PAST - 1:PAST], ALU.add, ALU.min),
              S["rows_done"])
            units = [(i, h) for i in range(NT) for h in range(HEADS)]

            def scores(u):
                i, h = units[u]
                n = TILES[i][1]
                nk = P * i if i < 4 else PAST
                b, s = 3 * (u % 2), sc[u % 2]
                dve.wait_ge(S["s_done"], u + 1)
                if u >= 2:
                    dve.wait_ge(S["t_done"], u - 1)
                if nk:
                    src = ps[0:n, b, 0:nk] if i < 4 else ps[0:n, b:b + 2, :].rearrange("p b t -> p (b t)")
                    o(TSC(s[0:n, 0:nk], src, HD ** -0.5, None, ALU.mult))
                diag = ps[0:n, b, nk:nk + n] if i < 4 else ps[0:n, b + 2, 0:n]
                o(STT(s[0:n, nk:nk + n], diag, HD ** -0.5, C("neg_causal")[0:n, 0:n], ALU.mult, ALU.add))
                o(v.reduce_max(mx[0:n, u % 2:u % 2 + 1], s[0:n, 0:nk + n], AX))
                o(TSC(mx[0:n, u % 2:u % 2 + 1], mx[0:n, u % 2:u % 2 + 1], -1.0, None, ALU.mult), S["s_max"])

            dve.wait_ge(S["ld_const"], 32)
            scores(0)
            for u, (i, h) in enumerate(units):
                if u + 1 < len(units):
                    scores(u + 1)
                n = TILES[i][1]
                nk = P * (i + 1) if i < 4 else PAST + TS
                dve.wait_ge(S["s_exp"], u + 1)
                o(v.reciprocal(rs[0:n, u % 2:u % 2 + 1], rs[0:n, u % 2:u % 2 + 1]))
                o(TSC(sc[u % 2][0:n, 0:nk], sc[u % 2][0:n, 0:nk], rs[0:n, u % 2:u % 2 + 1], None, ALU.mult), S["p_ready"])
            dve.wait_ge(S["proj_done"], NCH)
            o(v.memset(cu[:, :, 0:CPAD], 0.0))
            dve.wait_ge(S["ld_state"], 16)
            dve.wait_ge(S["c_gate"], 1)
            TT(cu[:, :, CPAD:CPAD + TP], csig[:, :, PAD:PAD + TP], hb[:, VAL:VAL + 2, PAD:PAD + TP], ALU.mult)
            o(TT(cu[:, :, 2 * CPAD + TP:], csig[:, :, SCOL:], hb[:, VAL:VAL + 2, SCOL:], ALU.mult), S["c_glu"])
            NC_ = CPAD + T
            for j in range(CW):
                for c in range(2):
                    w = pp("conv_w", c * CW + j)
                    if j == 0:
                        o(TSC(cacc[:, c], cu[:, c, 0:NC_], w, pp("conv_b", c), ALU.mult, ALU.add))
                    else:
                        o(STT(cacc[:, c], cu[:, c, j:j + NC_], w, cacc[:, c], ALU.mult, ALU.add),
                          S["c_taps"] if j == CW - 1 else None)
            dve.wait_ge(S["c_mean"], 1)
            TT(ccen[:, :, 0:TP], cacc[:, :, 0:TP], bc_mid(ps[:, 0, :], 2), ALU.subtract)
            o(TT(ccen[:, :, TP:], cacc[:, :, CPAD + TP:], bc_mid(ps[:, 1, 0:TS], 2), ALU.subtract), S["c_cen"])
            dve.wait_ge(S["c_rstd"], 1)
            o(TT(ccen, ccen, bc_mid(crs, 2), ALU.mult))
            for c in range(2):
                o(TSC(ccen[:, c], ccen[:, c], pp("conv_g", c), pp("conv_lb", c), ALU.mult, ALU.add))
            o(v.memset(stat[:, 30:31], 0.0), S["c_lin"])
            dve.wait_ge(S["c_sig"], 1)
            o(TT(mixT[:, 0:2], ccen, csq, ALU.mult), S["c_done"])
            dve.wait_ge(S["st_conv"], 32)
            dve.wait_ge(S["pads_zero"], 1)
            dve.wait_ge(S["ld_pad"], 16)
            for j in range(GTAPS):
                for c in range(6):
                    w = pp("gconv_w", c * GTAPS + j)
                    src = hb[:, BQ + c, j:j + PAD + T]
                    if j == 0:
                        o(TSC(gacc[:, c], src, w, None, ALU.mult))
                    else:
                        o(STT(gacc[:, c], src, w, gacc[:, c], ALU.mult, ALU.add))
            o(v.memset(stat[:, 30:31], 0.0), S["g_taps"])
            dve.wait_ge(S["g_sig"], 1)
            qkv = rG[:, 0:6 * T].rearrange("p (c t) -> p c t", c=6)
            TT(qkv[:, :, 0:TP], gacc[:, :, 0:TP], gsig[:, :, 0:TP], ALU.mult)
            o(TT(qkv[:, :, TP:], gacc[:, :, PAD + TP:], gsig[:, :, PAD + TP:], ALU.mult), S["g_silu"])
            dve.wait_ge(S["g_zsig"], 1)
            for t0, n, c0 in PIECES:
                o(TT(gzs[:, :, t0:t0 + n], hb[:, BZ:BZ + 2, c0:c0 + n], gz[:, :, c0:c0 + n], ALU.mult))
            dve.wait_ge(S["g_rs"], 1)
            o(STT(gq, gq, HD ** -0.5, grs[:, 0:2], ALU.mult, ALU.mult))
            o(TT(gk, gk, grs[:, 2:4], ALU.mult))
            dve.wait_ge(S["g_eg"], 1)
            o(TT(gR, gq, geG, ALU.mult))
            dve.wait_ge(S["g_tokp"], 1)
            tk = ps[:, 5, 0:NT * 36].rearrange("p (i k r) -> p i k r", k=3, r=12)
            v.tensor_copy(toks[:, 0:4], tk[:, 0:4])
            o(v.tensor_copy(toks[LOW, 4], tk[LOW, 4]))
            o(TT(tG, toks[:, :, 1, 0:4], toks[:, :, 0, 4:8], ALU.add))
            o(TSC(nG, toks[:, :, 1, 0:4], -1.0, None, ALU.mult), S["g_tok"])
            dve.wait_ge(S["g_texp"], 1)
            o(TSC(nbeg, nbeg, -1.0, None, ALU.mult), S["g_prep"])
            for c in range(7):
                src = hb[:, CR + c if c < 6 else SMALL]
                m = pp("mu", c) if c < 6 else pp("mu_s")
                d = wcum[:, :, :].rearrange("p c t -> p (c t)")[:, 0:PAD + T]
                o(TT(d, src[:, PAD - 1:HW - 1], src[:, PAD:HW], ALU.subtract))
                for t0, n, c0 in PIECES:
                    o(STT(xm[:, c, t0:t0 + n], d[:, c0 - PAD:c0 - PAD + n], m, src[:, c0:c0 + n], ALU.mult, ALU.add),
                      S["w_mix"] if (c, t0) == (6, TP) else None)
            dve.wait_ge(S["w_sg"], 1)
            for c in range(2):
                o(SCAN(wcum[:, c], ch_mask[:, :], wsig[:, c], 0.0, ALU.mult, ALU.add))
            W4 = chunks(wcum)
            for c in range(2):
                o(TT(chunks(tb)[:, c], W4[:, c], W4[:, c, :, 31:32].to_broadcast([P, 9, CHUNK]), ALU.subtract))
            o(TT(eL, W4[:, :, :, 63:64].rearrange("p c k o -> p c (k o)"),
                 W4[:, :, :, 31:32].rearrange("p c k o -> p c (k o)"), ALU.subtract), S["w_cum"])
            dve.wait_ge(S["w_e"], 1)
            o(TT(tb, tb, wsig, ALU.subtract))
            o(TT(wsig, wcum, wsig, ALU.subtract), S["w_cprev"])
            dve.wait_ge(S["w_e5"], 1)
            r, k = xm[:, 0:2], xm[:, 2:4]
            for c in range(2):
                o(TSC(wsig[:, c], k[:, c], pp("k_k", c), None, ALU.mult))
            o(v.memset(stat[:, 30:31], 0.0), S["w_k1"])
            dve.wait_ge(S["w_krs"], 1)
            o(TT(wsig, wsig, tb, ALU.mult))
            o(STT(ac, wsig, -1.0, ac, ALU.mult, ALU.mult))
            o(STT(Au, wsig, -1.0, Au, ALU.mult, ALU.mult))
            o(TT(tb, wsig, ta, ALU.mult))
            o(TT(bc, tb, kc, ALU.mult))
            for c in range(2):
                o(TSC(ta[:, c], ta[:, c], 1.0, pp("k_a", c), ALU.subtract, ALU.mult))
            o(STT(k, ta, 1.0, k, ALU.add, ALU.mult))
            for c in range(2):
                o(STT(tb[:, c], r[:, c], pp("r_k", c), k[:, c], ALU.mult, ALU.mult),
                  S["w_bon"] if c == 1 else None)
            o(TT(kc, k, kc, ALU.mult))
            o(TT(rc, r, rc, ALU.mult))
            o(TT(Ru, r, Ru, ALU.mult))
            for c in range(2):
                e = eL[:, c].rearrange("p (k o) -> p k o", o=1).to_broadcast([P, 9, CHUNK])
                o(TT(chunks(Bb)[:, c], chunks(bc)[:, c], e, ALU.mult))
                o(TT(chunks(Kb)[:, c], chunks(kc)[:, c], e, ALU.mult))
            dve.wait_ge(S["w_bonp"], 1)
            o(TT(bonus.rearrange("p c (u t) -> p (c u) t", u=2), xmv.rearrange("p c (u t) -> p (c u) t", u=2),
                 ps[:, 4:8, 0:HALF], ALU.mult), S["w_prep"])
            dve.wait_ge(S["u_mask"], 1)
            dve.wait_ge(S["ld_state"], 48)
            for i, (t0, n) in enumerate(TILES):
                k0 = 2 * i
                nch = n // CHUNK
                g, w = U
                dve.wait_ge(S["u_tr"], k0 + 1)
                Gb = bank4(1, n)
                STT(NB[0:n, :, 0:n], Gb, -1.0, bc_mid(C("neg_strict_l")[0:n, 0:n], 4), ALU.mult, ALU.add)
                mark(TT(DmT[0:n, :, 0:n], Gb, bc_mid(C("neg_incl_u")[0:n, 0:n], 4), ALU.add), S["u_mask"])
                kt = ps[0:n, 0, 0:GW].rearrange("p (h t) -> p h t", h=4)
                vt = ps[0:n, 0, GW:512].rearrange("p (h t) -> p h t", h=4)

                def per_token(x, rows, m=64):
                    return x[rows, i].rearrange("p (h o) -> p h o", o=1).to_broadcast([rows.stop - rows.start, 4, m])

                rn = slice(0, n)
                TT(g["QP"][0:n, :, 0:HD], vt, per_token(beta, rn), ALU.mult)
                TT(g["QP"][0:n, :, HD:P], kt, per_token(nbeg, rn), ALU.mult)
                for c in range(nch):
                    rr = slice(c * CHUNK, (c + 1) * CHUNK)
                    TT(g["BA"][rr, :, rr], kt[rr], per_token(eGL, rr), ALU.mult)
                dve.wait_ge(S["u_dexp"], i + 1)
                dve.wait_ge(S["u_A"], k0 + 1)
                for q in range(2):
                    blk = ps[0:n, 2 + q, 0:4 * n].rearrange("p (k c t) -> p k c t", k=2, c=2)
                    STT(g["N"][0:n, q::2, 0:n], blk[:, 0], -1.0, NB[0:n, q::2, 0:n], ALU.mult, ALU.mult)
                    last = TT(g["BA"][0:n, q::2, P:P + n], blk[:, 1], DmT[0:n, q::2, 0:n], ALU.mult)
                o(last, S["u_N"])
                dve.wait_ge(S["u_A"], k0 + 2)
                for q in range(2):
                    blk = ps[0:n, 4 + 2 * q, 0:4 * n].rearrange("p (k c t) -> p k c t", k=2, c=2)
                    blk2 = ps[0:n, 5 + 2 * q, 0:4 * n].rearrange("p (k c t) -> p k c t", k=2, c=2)
                    TT(w["N"][0:n, q::2, 0:n], blk[:, 0], bc_mid(C("strict_l")[0:n, 0:n], 2), ALU.mult)
                    TT(Aak[0:n, q::2, 0:n], blk[:, 1], bc_mid(C("strict_u")[0:n, 0:n], 2), ALU.mult)
                    TT(w["BA"][0:n, q::2, P:P + n], blk2[:, 0], bc_mid(C("incl_u")[0:n, 0:n], 2), ALU.mult)
                    last = TT(KA[0:n, q::2, P:P + n], blk2[:, 1], bc_mid(C("incl_u")[0:n, 0:n], 2), ALU.mult)
                o(last, S["u_N"])
                for m, u in enumerate(U):
                    dve.wait_ge(S["u_NTs"], k0 + m + 1)
                    mark(TT(u["ED"][0:n, 0, :, 0:n], u["NT"][0:n, :, 0:n],
                                bc_mid(C("first_u")[0:n, 0:n], 4), ALU.mult), S["u_E0"])
                dve.wait_ge(S["u_P"], i + 1)
                mark(v.tensor_copy(w["QP"][0:n, :, 0:HD], ps[0:n, 4, 0:GW].rearrange("p (h t) -> p h t", h=4)), S["u_Pq"])
                for m in range(2):
                    dve.wait_ge(S["u_D0"], k0 + m + 1)
                dve.wait_ge(S["u_E0"], k0 + 2)
                for s, join in enumerate(JOINS):
                    for m, u in enumerate(U):
                        dve.wait_ge(S["u_T1p"], (k0 + 0) * 5 + 2 * s + m + 1)
                        mark(TT(u["T1"][0:n, :, 0:n], bank4(mixer_bank[m] + 2, n),
                                    bc_mid(C(join)[0:n, 0:n], 4), ALU.mult), S["u_T1"])
                    for m, u in enumerate(U):
                        b = mixer_bank[m]
                        dve.wait_ge(S["u_EDp"], (k0 + 0) * 5 + 2 * s + m + 1)
                        both = s < len(JOINS) - 1
                        for x in ((0, 1) if both else (0,)):
                            dst = u["ED"][0:n, x, :, 0:n]
                            last = TT(dst, dst, bank4(b + x, n), ALU.add)
                        mark(last, S["u_ED"])
                    dve.wait_ge(S["u_ED"], (k0 + 0) * 5 + 2 * s + 2)
                for m, u in enumerate(U):
                    b = mixer_bank[m]
                    dve.wait_ge(S["u_OUTs"], k0 + m + 1)
                    dec_ = (decG, decR)[m]
                    for h in range(HEADS):
                        for c in range(nch):
                            cc = slice((h % 2) * 256 + c * CHUNK, (h % 2) * 256 + (c + 1) * CHUNK)
                            last = STT(u["OUT"][TOP, h, c * CHUNK:(c + 1) * CHUNK], ident[TOP, TOP],
                                       dec_[TOP, h, 2 * i + c:2 * i + c + 1], ps[TOP, b + h // 2, cc], ALU.mult, ALU.add)
                    mark(last, S["u_OUTv"])
                for c in range(nch):
                    for m, u in enumerate(U):
                        ch = 2 * i + c
                        dve.wait_ge(S["u_Sp"], 2 * ch + m + 1)
                        dst = 4 if ch == 8 else (ch + 1) % 3
                        mark(v.tensor_copy(u["IS"][TOP, dst],
                                        ps[TOP, mixer_bank[m] + 2, c * GW:(c + 1) * GW].rearrange("p (h t) -> p h t", h=4)), S["u_S"])
            dve.wait_ge(S["p_grs"], 1)
            o(TT(mixT[:, 2:4], mixT[:, 2:4], ta, ALU.mult))
            o(STT(mixT[:, 2:4], mixT[:, 2:4], pp("gnorm"), gzs, ALU.mult, ALU.mult))
            dve.wait_ge(S["p_rsum"], 1)
            mr = mixT[:, 4:6].rearrange("p c (u t) -> p (c u) t", u=2)
            o(STT(mr, ps[:, 4:8, 0:HALF], -1.0 / HD, mr, ALU.mult, ALU.add), S["p_rcen"])
            dve.wait_ge(S["p_rrs"], 1)
            o(TT(mixT[:, 4:6], mixT[:, 4:6], tb, ALU.mult))
            for c in range(2):
                o(TSC(mixT[:, 4 + c], mixT[:, 4 + c], pp("lnx_g", c), pp("lnx_b", c), ALU.mult, ALU.add))
            o(TT(mixT[:, 4:6], mixT[:, 4:6], bonus, ALU.add))
            o(TT(mixT[:, 4:6], mixT[:, 4:6], gate, ALU.mult), S["p_done"])
            dve.wait_ge(S["ld_xtok"], 16 * NT)
            dve.wait_ge(S["ld_lnp"], 64)

            def layer_norm(x, n, i, var, rstd, g, b, out, done):
                for k in range(2):
                    o(v.bn_stats(bst[0:n, 6 * k:6 * k + 6], x[:, k * 512:(k + 1) * 512]))
                o(v.bn_aggr(stat[0:n, 20:22], bst[0:n, 0:12]), S[var])
                dve.wait_ge(S[rstd], i + 1)
                o(TSC(x, x, stat[0:n, 20:21], stat[0:n, 24:25], ALU.subtract, ALU.mult))
                o(TT(x, x, lnp[0:n, g], ALU.mult))
                o(TT(out, x, lnp[0:n, b], ALU.add), S[done])

            for i, (t0, n) in enumerate(TILES):
                dve.wait_ge(S["o_y"], i + 1)
                x = xtok[0:n, i]
                b = 2 * (i % 2)
                o(STT(x, x, ALPHA, ps[0:n, b:b + 2, :].rearrange("p b t -> p (b t)"), ALU.mult, ALU.add), S["o_x"])
                layer_norm(x, n, i, "o_var", "o_rstd", 0, 1, x1[0:n, i], "o_x1")
            dve.wait_ge(S["ld_router"], 32)
            o(v.memset(logit, 0.0))
            dve.wait_ge(S["o_log"], 1)
            lp = ps[:, 6, 0:NT * 20].rearrange("p (i r) -> p i r", r=20)
            bias = bc_mid(rt[:, 0:20], 4)
            TT(logit[:, 0:4], lp[:, 0:4], bias, ALU.add)
            o(TT(logit[LOW, 4], lp[LOW, 4], rt[LOW, 0:20], ALU.add))
            lg = logit[:, :, 0:4]
            at = 65

            def tmp(*shape):
                nonlocal at
                n = int(np.prod(shape))
                t = rt[:, at:at + n]
                at += n
                if len(shape) > 1:
                    names_ = "abc"[:len(shape)]
                    t = t.rearrange(f"p ({' '.join(names_)}) -> p {' '.join(names_)}", **dict(zip(names_[1:], shape[1:])))
                return t

            def bc4(x):
                return x.rearrange("p (i o) -> p i o", o=1).to_broadcast([P, NT, 4])

            def first_max(values, best, hit):
                o(TT(hit, values, bc4(best), ALU.is_equal))
                free = tmp(NT)
                o(TSC(free, hit[:, :, 0], -1.0, 1.0, ALU.mult, ALU.add))
                for k in range(1, 4):
                    o(TT(hit[:, :, k], hit[:, :, k], free, ALU.mult))
                    o(TT(free, free, hit[:, :, k], ALU.subtract))

            mg, hitg = tmp(NT), tmp(NT, 4)
            o(v.reduce_max(mg, lg, AX))
            eg = rt[:, 40:60].rearrange("p (i k) -> p i k", k=4)
            o(TT(eg, lg, bc4(mg), ALU.subtract), S["o_lg"])
            first_max(lg, mg, hitg)
            le4 = tmp(NT, 4, 4)
            for g_ in range(4):
                o(TT(le4[:, :, g_], logit[:, :, 4 + 4 * g_:8 + 4 * g_], bc4(hitg[:, :, g_]), ALU.mult))
            le = tmp(NT, 4)
            o(TT(le, le4[:, :, 0], le4[:, :, 1], ALU.add))
            o(TT(le, le, le4[:, :, 2], ALU.add))
            o(TT(le, le, le4[:, :, 3], ALU.add))
            m1, hit1, m2, hit2, le2 = tmp(NT), tmp(NT, 4), tmp(NT), tmp(NT, 4), tmp(NT, 4)
            o(v.reduce_max(m1, le, AX))
            first_max(le, m1, hit1)
            o(STT(le2, hit1, NEG, le, ALU.mult, ALU.add))
            o(v.reduce_max(m2, le2, AX))
            first_max(le2, m2, hit2)
            d21 = rt[:, 60:65]
            o(TT(d21, m2, m1, ALU.subtract), S["o_w2"])
            dve.wait_ge(S["o_eg"], 2)
            gs, w1, w2 = tmp(NT), tmp(NT), tmp(NT)
            o(v.reduce_sum(gs, eg, AX))
            o(STT(gs, d21, 1.0, gs, ALU.add, ALU.mult))
            o(v.reciprocal(w1, gs))
            o(TT(w2, w1, d21, ALU.mult))
            o(TT(hit1, hit1, bc4(w1), ALU.mult))
            o(TT(hit2, hit2, bc4(w2), ALU.mult))
            o(TT(hit1, hit1, hit2, ALU.add))
            comb = tmp(NT, 4, 4)
            for g_ in range(4):
                o(TT(comb[:, :, g_], hit1, bc4(hitg[:, :, g_]), ALU.mult))
            comb = comb.rearrange("p i g e -> p i (g e)")
            for i, (t0, n) in enumerate(TILES):
                o(TSC(yacc[0:n, i], x1[0:n, i], ALPHA, None, ALU.mult))
            for e in range(EXPERTS):
                for f in range(2):
                    dve.wait_ge(S["m_silu"], 2 * e + f + 1)
                    if e >= 1:
                        dve.wait_ge(S["m_dn"], NT * e)
                    mark(TT(halves(hT[:, f]), halves(hg[:, f]), two_banks(4 * f + 2, HALF), ALU.mult), S["m_h"])
                for i, (t0, n) in enumerate(TILES):
                    dve.wait_ge(S["m_dn"], NT * e + i + 1)
                    b = 2 * (i % 2)
                    mark(STT(yacc[0:n, i], ps[0:n, b:b + 2, :].rearrange("p b t -> p (b t)"), comb[0:n, i, e:e + 1],
                          yacc[0:n, i], ALU.mult, ALU.add), S["m_acc"])
            dve.wait_ge(S["m_acc"], NT * EXPERTS)
            for i, (t0, n) in enumerate(TILES):
                layer_norm(yacc[0:n, i], n, i, "f_var", "f_rstd", 2, 3, x1[0:n, i], "f_y")

        @block.tensor
        def _(pe):
            mm, tr = nc.tensor.matmul, nc.tensor.transpose
            pe.wait_ge(S["ld_x"], 16)
            for j in range(NCH):
                pe.wait_ge(ld_w[j % RING], 16 * (j // RING + 1))
                if j >= RING:
                    pe.wait_ge(S["evac_act"], j - RING + 1)
                    pe.wait_ge(S["evac_vec"], j - RING + 1)
                for h in range(2):
                    for k in range(KD):
                        last = mm(ps[:, 2 * (j % RING) + h, 0:HALF], wring[j % RING][:, k], xT[:, k, h * HALF:(h + 1) * HALF],
                                  start=(k == 0), stop=(k == KD - 1))
                last.then_inc(S["proj_done"], 1)
            pe.wait_ge(S["evac_act"], NCH)
            pe.wait_ge(S["evac_vec"], NCH)
            pe.wait_ge(S["ld_const"], 32)
            for i, (t0, n) in enumerate(TILES):
                if i >= 2:
                    pe.wait_ge(S["vt_act"], i - 1)
                c0 = tile_cols(i)
                for pair in range(2):
                    last = tr(ps[0:n, 6 + i % 2, pair * P:(pair + 1) * P], hb[:, DV + pair, c0:c0 + n], ident)
                last.then_inc(S["vt_pe"], 1)
            units = [(i, h) for i in range(NT) for h in range(HEADS)]

            def scores(u):
                i, h = units[u]
                n, c0, b = TILES[i][1], tile_cols(i), 3 * (u % 2)
                pair, pb = HEADP[h]
                r = slice(pb, pb + HD)
                if u >= 2:
                    pe.wait_ge(S["o_act"], u - 1)
                if i < 4:
                    segs = [(hb[r, DK + pair, PAD:PAD + P * (i + 1)], Fp[:, 0:P * (i + 1)])]
                else:
                    segs = [(kcT[r, pair, 0:512], Fs[:, 0:512]), (kcT[r, pair, 512:PAST], Fs[:, 512:PAST]),
                            (hb[r, DK + pair, SCOL:SCOL + TS], Fs[:, PAST:])]
                for k, (keys, f) in enumerate(segs):
                    nk = keys.shape[1]
                    mm(ps[0:n, b + k, 0:nk], hb[r, DQ + pair, c0:c0 + n], keys, start=True, stop=False)
                    last = mm(ps[0:n, b + k, 0:nk], sel[:, SEL_F + h, 0:n], f, start=False, stop=True)
                last.then_inc(S["s_done"], 1)

            pe.wait_ge(S["rows_done"], 1)
            pe.wait_ge(S["ld_cache"], 48)
            pe.wait_ge(S["vt_act"], NT)
            scores(0)
            for u, (i, h) in enumerate(units):
                n, b = TILES[i][1], 3 * (u % 2)
                pair, pb = HEADP[h]
                if u + 1 < len(units):
                    scores(u + 1)
                pe.wait_ge(S["p_ready"], u + 1)
                if u >= 2:
                    pe.wait_ge(S["pt_copied"], u - 1)
                s = sc[u % 2]
                if i < 4:
                    for k in range(i + 1):
                        last = tr(ps[:, 6 + u % 2, k * P:(k + 1) * P], s[:, k * P:(k + 1) * P], ident)
                else:
                    for k in range(8):
                        tr(ps[:, 6 + u % 2, k * n:(k + 1) * n], s[0:n, k * P:(k + 1) * P], ident[0:n, 0:n])
                    last = tr(ps[LOW, b + 2, 64:128], s[0:n, PAST:], ident[0:n, 0:n])
                last.then_inc(S["t_done"], 1)
                pe.wait_ge(S["pt_copied"], u + 1)
                hs = slice(h * HD, (h + 1) * HD)
                out = ps[pb:pb + HD, b, 0:n]
                if i < 4:
                    for k in range(i + 1):
                        last = mm(out, vtok[:, k, hs], pT[:, u % 2, k * P:(k + 1) * P], start=(k == 0), stop=(k == i))
                else:
                    for k in range(8):
                        mm(out, vc[:, k, hs], pT[:, u % 2, k * n:(k + 1) * n], start=(k == 0), stop=False)
                    last = mm(out, vtok[LOW, 4, hs], pT[LOW, u % 2, 512:T], start=False, stop=True)
                last.then_inc(S["pv_done"], 1)
            pe.wait_ge(S["o_act"], len(units))
            pe.wait_ge(S["c_taps"], 2)
            for n, (dst, src) in enumerate([(ps[:, 0, :], (0, TP)), (ps[:, 1, 0:TS], (CPAD + TP, TS))]):
                for c in range(2):
                    last = mm(dst, C("mean_ones"), cacc[:, c, src[0]:src[0] + src[1]], start=(c == 0), stop=(c == 1))
            last.then_inc(S["c_mean"], 1)
            pe.wait_ge(S["c_sq"], 1)
            for h in range(2):
                for c in range(2):
                    last = mm(ps[:, 2 + h, 0:HALF], C("mean_ones"), csq[:, c, h * HALF:(h + 1) * HALF],
                              start=(c == 0), stop=(c == 1))
            last.then_inc(S["c_var"], 1)

            def head_sums(b, src, nc_):
                for c in range(nc_):
                    for h in range(2):
                        last = mm(ps[:, b + 2 * c + h, 0:HALF], C("head_ones"), src[:, c, h * HALF:(h + 1) * HALF],
                                  start=True, stop=True)
                return last

            pe.wait_ge(S["c_rstd"], 1)
            pe.wait_ge(S["c_cen"], 1)
            pe.wait_ge(S["g_sq"], 1)
            head_sums(0, gsq, 4).then_inc(S["g_sum"], 1)
            pe.wait_ge(S["g_rs"], 1)
            for p_ in range(2):
                for h in range(2):
                    mm(ps[:, 2 * p_ + h, 0:HALF], sel[ROWS, SEL_PAIR + p_, :], rowG[ROWS, h * HALF:(h + 1) * HALF],
                       start=True, stop=True)
            for h in range(HEADS):
                last = mm(ps[TOP, 4, h * 9:(h + 1) * 9], sel[ROWS, SEL_G + h, 0:64], rowG[ROWS, CHUNK - 1::CHUNK],
                          start=True, stop=True)
            last.then_inc(S["g_pairs"], 1)
            for i, (t0, n) in enumerate(TILES):
                for k, rows in enumerate((rowy, rowG, rowGL)):
                    at = (3 * i + k) * 12
                    last = mm(ps[0:n, 5, at:at + 12], rows[ROWS, t0:t0 + n], ident[ROWS, ROWS], start=True, stop=True)
            last.then_inc(S["g_tokp"], 1)
            pe.wait_ge(S["w_lora"], 1)
            pe.wait_ge(S["g_eg"], 1)
            pe.wait_ge(S["g_tok"], 1)

            def lora_product(b, rows):
                for c in range(2):
                    for h in range(2):
                        last = mm(ps[:, b + 2 * c + h, 0:HALF], lora[rows, c * P:(c + 1) * P],
                                  xm[rows, 6, h * HALF:(h + 1) * HALF], start=True, stop=True)
                return last

            lora_product(0, slice(0, 16))
            lora_product(4, slice(32, 48)).then_inc(S["w_wa"], 1)
            pe.wait_ge(S["w_sg"], 1)
            lora_product(0, slice(64, 96)).then_inc(S["w_gatep"], 1)
            pe.wait_ge(S["w_sq"], 1)
            head_sums(4, tb, 2).then_inc(S["w_ksum"], 1)
            pe.wait_ge(S["w_krs"], 1)
            pe.wait_ge(S["w_bon"], 1)
            head_sums(4, tb, 2).then_inc(S["w_bonp"], 1)
            pe.wait_ge(S["w_prep"], 1)
            pe.wait_ge(S["w_gate"], 1)
            pe.wait_ge(S["g_prep"], 1)
            g, w = U
            for i, (t0, n) in enumerate(TILES):
                k0 = 2 * i
                nch = n // CHUNK
                ts = slice(t0, t0 + n)
                if i >= 1:
                    pe.wait_ge(S["u_S"], 4 * i)
                    pe.wait_ge(S["u_O"], 2 * i)
                for p_ in range(2):
                    tr(ps[0:n, 0, p_ * P:(p_ + 1) * P], gk[:, p_, ts], ident)
                    tr(ps[0:n, 0, GW + p_ * P:GW + (p_ + 1) * P], gv[:, p_, ts], ident)
                for h in range(HEADS):
                    last = mm(ps[0:n, 1, h * n:(h + 1) * n], sel[ROWS, SEL_G + h, 0:n], rowG[ROWS, ts], start=True, stop=True)
                last.then_inc(S["u_tr"], 1)
                for h, (pair, pb) in enumerate(HEADP):
                    r = slice(pb, pb + HD)
                    kch = gk[r, pair, ts]
                    b = 2 + h % 2
                    mm(ps[0:n, b, pair * n:(pair + 1) * n], kch, kch, start=True, stop=True)
                    last = mm(ps[0:n, b, (2 + pair) * n:(3 + pair) * n], kch, gq[r, pair, ts], start=True, stop=True)
                last.then_inc(S["u_A"], 1)
                for p_ in range(2):
                    for b, q, src in ((4, 0, Au), (4, 1, xmv), (5, 0, Bb), (5, 1, Kb)):
                        last = tr(ps[0:n, b, q * GW + p_ * P:q * GW + (p_ + 1) * P], src[:, p_, ts], ident)
                last.then_inc(S["u_tr"], 1)
                pe.wait_ge(S["u_tok"], i + 1)
                for h in (1, 3, 0, 2):
                    pair, pb = HEADP[h]
                    r = slice(pb, pb + HD)
                    b = 4 + 2 * (h % 2)
                    for b_, q, lhs, rhs in ((b, 0, ac, bc), (b, 2, kc, ac), (b + 1, 0, bc, rc), (b + 1, 2, kc, rc)):
                        last = mm(ps[0:n, b_, (q + pair) * n:(q + pair + 1) * n], lhs[r, pair, ts], rhs[r, pair, ts],
                                  start=True, stop=True)
                last.then_inc(S["u_A"], 1)
                for m, u in enumerate(U):
                    pe.wait_ge(S["u_diag"], k0 + m + 1)
                    for h in range(HEADS):
                        last = tr(ps[0:n, mixer_bank[m] + 1, h * n:(h + 1) * n], u["N"][0:n, h, 0:n], ident[0:n, 0:n])
                    last.then_inc(S["u_NTp"], 1)
                for h in range(HEADS):
                    last = mm(ps[0:n, 4, h * HD:(h + 1) * HD], Aak[0:n, h, 0:n], V[0:n, h], start=True, stop=True)
                last.then_inc(S["u_P"], 1)
                for m in range(2):
                    pe.wait_ge(S["u_NTs"], k0 + m + 1)
                    pe.wait_ge(S["u_D0"], k0 + m + 1)
                    pe.wait_ge(S["u_E0"], k0 + m + 1)
                pe.wait_ge(S["u_Pq"], i + 1)
                for s in range(len(JOINS)):
                    for m, u in enumerate(U):
                        if s:
                            pe.wait_ge(S["u_ED"], k0 * 5 + 2 * (s - 1) + m + 1)
                        for h in range(HEADS):
                            last = mm(ps[0:n, mixer_bank[m] + 2, h * n:(h + 1) * n], u["NT"][0:n, h, 0:n],
                                      u["ED"][0:n, 1, h, 0:n], start=True, stop=True)
                        last.then_inc(S["u_T1p"], 1)
                    for m, u in enumerate(U):
                        b = mixer_bank[m]
                        pe.wait_ge(S["u_T1"], k0 * 5 + 2 * s + m + 1)
                        E_, D_ = u["ED"][0:n, 0], u["ED"][0:n, 1]
                        for h in range(HEADS):
                            t1 = u["T1"][0:n, h, 0:n]
                            last = mm(ps[0:n, b, h * n:(h + 1) * n], t1, E_[:, h, 0:n], start=True, stop=True)
                            if s < len(JOINS) - 1:
                                last = mm(ps[0:n, b + 1, h * n:(h + 1) * n], E_[:, h, 0:n], t1, start=True, stop=True)
                        last.then_inc(S["u_EDp"], 1)
                for m, u in enumerate(U):
                    pe.wait_ge(S["u_ED"], k0 * 5 + 2 * 4 + m + 1)
                    for h in range(HEADS):
                        last = mm(ps[0:n, mixer_bank[m] + 3, h * P:(h + 1) * P], u["ED"][0:n, 0, h, 0:n], u["QP"][0:n, h],
                                  start=True, stop=True)
                    last.then_inc(S["u_TPQp"], 1)
                for m, u in enumerate(U):
                    b = mixer_bank[m]
                    pe.wait_ge(S["u_TPQ"], k0 + m + 1)
                    R_ = (gR, Ru)[m]
                    for h, (pair, pb) in enumerate(HEADP):
                        at = (h % 2) * 256
                        mm(ps[:, b + h // 2, at:at + P + n], u["TPQ"][0:n, h], u["BA"][0:n, h, 0:P + n], start=True, stop=False,
                           skip_group_check=True)
                        if m == 1:
                            mm(ps[LOW, b + h // 2, at:at + P + n], V[0:n, h], KA[0:n, h, 0:P + n], start=False, stop=False,
                               skip_group_check=True)
                        last = mm(ps[:, b + h // 2, at + P:at + P + n], C(f"shift{h % 2}"), R_[:, pair, ts],
                                  start=False, stop=True, skip_group_check=True)
                    last.then_inc(S["u_OUTp"], 1)
                for c in range(nch):
                    ch = 2 * i + c
                    slot = 3 if ch == 8 else ch % 3
                    for m, u in enumerate(U):
                        b = mixer_bank[m]
                        if c == 0:
                            pe.wait_ge(S["u_OUTs"], k0 + m + 1)
                            pe.wait_ge(S["u_OUTv"], k0 + m + 1)
                        if ch:
                            pe.wait_ge(S["u_S"], 2 * (ch - 1) + m + 1)
                        for h in range(HEADS):
                            last = mm(ps[TOP, b + 2, c * GW + h * HD:c * GW + (h + 1) * HD], u["OUT"][:, h, c * CHUNK:(c + 1) * CHUNK],
                                      u["IS"][:, slot, h], start=True, stop=True)
                        last.then_inc(S["u_Sp"], 1)
                        for h, (pair, pb) in enumerate(HEADP):
                            last = mm(ps[pb:pb + HD, b + 3, pair * n + c * CHUNK:pair * n + (c + 1) * CHUNK], u["IS"][:, slot, h],
                                      u["OUT"][:, h, P + c * CHUNK:P + (c + 1) * CHUNK], start=True, stop=True)
                        if c == nch - 1:
                            last.then_inc(S["u_Op"], 1)
            pe.wait_ge(S["u_S"], 18)
            pe.wait_ge(S["u_O"], 2 * NT)
            head_sums(4, mixT[:, 4:6], 2).then_inc(S["p_rsum"], 1)
            pe.wait_ge(S["p_gsq"], 1)
            head_sums(0, ta, 2).then_inc(S["p_gsum"], 1)
            pe.wait_ge(S["p_grs"], 1)
            pe.wait_ge(S["p_rsq"], 1)
            head_sums(0, tb, 2).then_inc(S["p_rvar"], 1)
            pe.wait_ge(S["p_done"], 1)
            pe.wait_ge(S["ld_wout"], 16)

            def x1_transposes(i):
                t0, n = TILES[i]
                pe.wait_ge(S["o_x1"], i + 1)
                if i:
                    pe.wait_ge(S["o_x1T"], i)
                for k in range(KD):
                    last = tr(ps[:, 4 + k // 4, (k % 4) * n:(k % 4 + 1) * n], x1[0:n, i, k * P:(k + 1) * P], ident[0:n, 0:n])
                last.then_inc(S["o_x1t"], 1)

            for i, (t0, n) in enumerate(TILES):
                if i >= 2:
                    pe.wait_ge(S["o_x"], i - 1)
                for q in range(2):
                    for k in range(KD):
                        last = mm(ps[0:n, 2 * (i % 2) + q, :], mixT[:, k, t0:t0 + n], wout[:, k, q * 512:(q + 1) * 512],
                                  start=(k == 0), stop=(k == KD - 1))
                last.then_inc(S["o_y"], 1)
                if i:
                    x1_transposes(i - 1)
            x1_transposes(NT - 1)
            pe.wait_ge(S["o_x1T"], NT)
            pe.wait_ge(S["ld_router"], 32)
            for i, (t0, n) in enumerate(TILES):
                for k in range(KD):
                    last = mm(ps[0:n, 6, i * 20:(i + 1) * 20], x1T[:, k, t0:t0 + n], wr[:, k], start=(k == 0), stop=(k == KD - 1))
            last.then_inc(S["o_log"], 1)
            pe.wait_ge(S["o_x"], NT)
            for e in range(EXPERTS):
                pe.wait_ge(ld_e[e % 2], 32 * (e // 2 + 1))
                if e == 0:
                    pe.wait_ge(S["o_w2"], 1)
                if e:
                    pe.wait_ge(S["m_acc"], NT * e)
                for f in range(2):
                    for w_ in range(2):
                        for h in range(2):
                            for k in range(KD):
                                last = mm(ps[:, 4 * f + 2 * w_ + h, 0:HALF], wgu[e % 2][:, k, w_ * FF + f * P:w_ * FF + (f + 1) * P],
                                          x1T[:, k, h * HALF:(h + 1) * HALF], start=(k == 0), stop=(k == KD - 1))
                    last.then_inc(S["m_gu"], 1)
                pe.wait_ge(S["m_h"], 2 * e + 2)
                for i, (t0, n) in enumerate(TILES):
                    if i >= 2:
                        pe.wait_ge(S["m_acc"], NT * e + i - 1)
                    for q in range(2):
                        for f in range(2):
                            last = mm(ps[0:n, 2 * (i % 2) + q, :], hT[:, f, t0:t0 + n], wdn[e % 2][:, f, q * 512:(q + 1) * 512],
                                      start=(f == 0), stop=(f == 1))
                    last.then_inc(S["m_dn"], 1)


OUTS = {"o_y": (T, D), "o_gconv": (P, 2, 6, PAD), "o_shift": (P, 2, 7), "o_kv": (P, 4, T), "o_logf": (HEADS, T),
        "o_conv": (P, 2, 2, CPAD), "o_state": (2, 2, HD, HEADS, HD)}


def square_constants():
    i, j = np.arange(P)[:, None], np.arange(P)[None, :]
    same = i // CHUNK == j // CHUNK
    lower = same & (i > j)
    c = {"ident": i == j, "strict_l": lower, "strict_u": lower.T, "incl_u": same & (i <= j),
         "neg_strict_l": np.where(lower, 0, NEG), "neg_incl_u": np.where(same & (i <= j), 0, NEG)}
    for b in (1, 2, 4, 8, 16, 32):
        join = (i // (2 * b) == j // (2 * b)) & (i // b % 2 == 1) & (j // b % 2 == 0)
        if b == 1:
            c["first_l"], c["first_u"] = join | (i == j), join.T | (i == j)
        else:
            c[f"join{b}"] = join
    c["neg_causal"] = np.where(j <= i, 0, NEG)
    c["head_ones"] = same
    c["mean_ones"] = np.full((P, P), 1.0 / GW)
    for q in range(2):
        c[f"shift{q}"] = (j >= HD) & (i == j - HD + q * HD)
    return np.stack([np.asarray(c[n], np.float32) for n in CONST], 1)


def row_selectors():
    s = np.zeros((P, NSEL, P), np.float32)
    for h in range(HEADS):
        s[96 + h, SEL_G + h, :] = 1.0
        s[104 + h, SEL_F + h, :] = -float(HD) ** 0.5
        s[96 + h, SEL_PAIR + h // 2, (h % 2) * HD:(h % 2 + 1) * HD] = 1.0
    return s


def layout(x):
    g = {k: np.asarray(v) for k, v in x.items()}
    z = np.zeros
    f32 = np.float32
    o = {}
    xx = np.concatenate([g["x_prompt"][0], g["x_sample"][0]], 0)
    o["x_tok"] = xx
    o["xT"] = xx.T.reshape(KD, P, T).transpose(1, 0, 2)
    w = g["w_in"][0]
    nA, nB = 2 * GW, 4 * GW + 2 * HEADS
    nC = 3 * GW + 64
    A, B, Cc, Dd = w[:, :nA], w[:, nA:nA + nB], w[:, nA + nB:nA + nB + nC], w[:, nA + nB + nC:]
    sm = z((D, P), f32)
    sm[:, 0:16], sm[:, 32:48], sm[:, 64:96] = Cc[:, 768:784], Cc[:, 784:800], Cc[:, 800:832]
    sm[:, 96:104], sm[:, 104:108] = B[:, 1024:1032], Dd[:, 768:772]
    cols = np.concatenate([sm, B[:, :1024], Cc[:, :768], Dd[:, :768], A], 1)
    o["w_in"] = cols.reshape(KD, P, NCH, P).transpose(2, 1, 0, 3)
    pads = z((P, NCH, PAD), f32)
    pads[:, BQ:BQ + 6] = g["state_gdn_conv"][0, 0].T.reshape(6, P, PAD).transpose(1, 0, 2)
    sh = g["state_rwkv_shift"][0, 0]
    pads[:, CR:CR + 6, 2] = sh[:768].reshape(6, P).T
    pads[0:16, 0, 2], pads[32:48, 0, 2], pads[64:96, 0, 2] = sh[768:784], sh[784:800], sh[800:832]
    o["pads"] = pads
    o["conv_state"] = g["state_conv"][0, 0].T.reshape(2, P, CPAD).transpose(1, 0, 2)
    o["s_gdn"] = g["state_gdn"][0, 0].transpose(1, 0, 2)
    o["s_rwkv"] = g["state_rwkv"][0, 0].transpose(2, 0, 1)
    o["k_cache"] = g["cache_fox_k"][0, 0].transpose(1, 2, 0).reshape(2, P, PAST).transpose(1, 0, 2)
    o["v_cache"] = g["cache_fox_v"][0, 0].reshape(8, P, GW).transpose(1, 0, 2)
    fc = z((12, PAST), f32)
    fc[8:12] = g["cache_fox_logf"][0, 0].T
    o["f_cache"] = fc
    par = z((P, NPC), f32)

    def put(name, arr):
        arr = np.asarray(arr, f32)
        if arr.ndim == 1:
            arr = arr[:, None]
        k = arr.shape[1]
        a3 = arr.reshape(-1, P, k).transpose(1, 0, 2).reshape(P, -1)
        par[:, PCOL[name]:PCOL[name] + a3.shape[1]] = a3

    put("conv_w", g["conv_w"][0].T)
    put("conv_b", g["conv_b"][0]), put("conv_g", g["conv_ln_g"][0]), put("conv_lb", g["conv_ln_b"][0])
    put("gconv_w", g["gdn_conv_w"][0].T)
    put("gnorm", np.concatenate([g["gdn_norm_w"][0]] * 2))
    mu = g["rwkv_mu"][0]
    put("mu", mu[:768])
    c = PCOL["mu_s"]
    par[0:16, c], par[32:48, c], par[64:96, c] = mu[768:784], mu[784:800], mu[800:832]
    for n, k in (("w0", "rwkv_w0"), ("a0", "rwkv_a0"), ("k_k", "rwkv_k_k"), ("k_a", "rwkv_k_a"),
                 ("lnx_g", "rwkv_lnx_g"), ("lnx_b", "rwkv_lnx_b")):
        put(n, g[k][0])
    put("r_k", g["rwkv_r_k"][0].reshape(-1))
    par[96:100, PCOL["row_bias"]], par[104:108, PCOL["row_bias"]] = g["gdn_dt_bias"][0], g["fox_b_f"][0]
    par[96:100, PCOL["row_alog"]] = g["gdn_a_log"][0]
    par[96:100, PCOL["row_sign"]], par[100:108, PCOL["row_sign"]] = 1.0, -1.0
    o["params"] = par
    lo = z((P, GW), f32)
    lo[0:16], lo[32:48], lo[64:96] = g["rwkv_w_up"][0], g["rwkv_a_up"][0], g["rwkv_g_up"][0]
    o["lora"] = lo
    cm = np.ones((P, T), f32)
    cm[:, ::CHUNK] = 0
    o["ch_mask"] = cm
    o["consts"], o["sel"] = square_constants(), row_selectors()
    o["w_out"] = g["w_out"][0].reshape(8, P, D).transpose(1, 0, 2)
    o["ln"] = np.stack([g[k][0] for k in ("ln1_g", "ln1_b", "ln2_g", "ln2_b")])
    o["w_router"] = np.concatenate([g["router_g_w"][0], g["router_e_w"][0]], 1).reshape(KD, P, 20).transpose(1, 0, 2)
    o["b_router"] = np.concatenate([g["router_g_b"][0], g["router_e_b"][0]])[None]
    gu = np.concatenate([g["exp_w_gate"][0], g["exp_w_up"][0]], 2)
    o["w_gu"] = gu.reshape(EXPERTS, KD, P, 2 * FF).transpose(0, 2, 1, 3)
    o["w_dn"] = g["exp_w_down"][0].reshape(EXPERTS, 2, P, D).transpose(0, 2, 1, 3)
    return {k: np.ascontiguousarray(v) for k, v in o.items()}


def restore(r):
    y = r["o_y"]
    out = [y[None, :TP], y[None, TP:]]
    for k in range(2):
        t = slice(0, TP) if k == 0 else slice(TP, T)
        n = TP if k == 0 else TS
        sh = r["o_shift"][:, k]
        shift = np.concatenate([sh[:, :6].T.reshape(-1), sh[0:16, 6], sh[32:48, 6], sh[64:96, 6]])
        kv = [r["o_kv"][:, c:c + 2, t].transpose(2, 1, 0).reshape(1, 1, n, HEADS, HD) for c in (0, 2)]
        out += [r["o_conv"][:, k].transpose(2, 1, 0).reshape(1, 1, CPAD, GW),
                r["o_gconv"][:, k].transpose(2, 1, 0).reshape(1, 1, PAD, 3 * GW),
                r["o_state"][0, k].transpose(1, 0, 2)[None, None],
                shift[None, None],
                r["o_state"][1, k].transpose(1, 2, 0)[None, None],
                kv[0], kv[1], r["o_logf"][:, t].T[None, None]]
    return tuple(np.ascontiguousarray(v) for v in out)


def kernel(**inputs):
    import concourse.bacc as _bacc
    from concourse.bass_utils import run_bass_kernel_spmd as _run

    nc = _bacc.Bacc("TRN2", target_bir_lowering=False, num_devices=1)
    arrays = {f"in_{k}": v for k, v in layout(inputs).items()}
    a = {k[3:]: nc.dram_tensor(k, v.shape, F32, kind="ExternalInput").ap() for k, v in arrays.items()}
    a.update({k: nc.dram_tensor(k, s, F32, kind="ExternalOutput").ap() for k, s in OUTS.items()})
    step_kernel(nc, a)
    r = _run(nc, [arrays], core_ids=[0])
    return restore(r.results[0])
```

```python
from contextlib import ExitStack

import numpy as np

import concourse.bass as bass
from concourse import mybir

F32 = mybir.dt.float32
ALU = mybir.AluOpType
ACT = mybir.ActivationFunctionType
AX = mybir.AxisListType.X

P = 128
D = 1024
KD = D // P
TP, TS = 512, 64
T = TP + TS
HALF = T // 2
HEADS, HD = 4, 64
GW = HEADS * HD
CHUNK = 64
PAST = 1024
CW = 31
CPAD = CW - 1
GTAPS = 4
PAD = GTAPS - 1
HW = 2 * PAD + T
SCOL = 2 * PAD + TP
TILES = [(0, 128), (128, 128), (256, 128), (384, 128), (512, 64)]
PIECES = [(0, TP, PAD), (TP, TS, SCOL)]
NT = len(TILES)
EXPERTS, FF = 16, 256
CAP = 128
FAR = 1e6
GROUPS = 4
DECAY = float(np.exp(-0.5))
ALPHA = 2.0 ** 0.25
LN_EPS, GN_EPS, RMS_EPS, L2_EPS = 1e-5, 64e-5, 1e-6, 1e-6
NEG = -1e30

SMALL, BQ, BK, BV, BZ, CR, CK, CV, DQ, DK, DV, VAL, GATE = 0, 1, 3, 5, 7, 9, 11, 13, 15, 17, 19, 21, 23
NCH = 25
RING = 4
ROWS = slice(96, 108)
TOP, LOW = slice(64, 128), slice(0, 64)

CONST = ["ident", "strict_l", "strict_u", "incl_u", "neg_strict_l", "neg_incl_u", "first_l", "first_u",
         "join2", "join4", "join8", "join16", "join32", "neg_causal", "head_ones", "mean_ones", "shift0", "shift1"]
SEL_G, SEL_F, SEL_PAIR, NSEL = 0, 4, 8, 10
PARAMS = [("conv_w", 2 * CW), ("conv_b", 2), ("conv_g", 2), ("conv_lb", 2), ("gconv_w", 6 * GTAPS),
          ("gnorm", 1), ("mu", 6), ("mu_s", 1), ("w0", 2), ("a0", 2), ("k_k", 2), ("k_a", 2), ("r_k", 2),
          ("lnx_g", 2), ("lnx_b", 2), ("row_bias", 1), ("row_alog", 1), ("row_sign", 1)]
PCOL, NPC = {}, 0
for _n, _k in PARAMS:
    PCOL[_n] = NPC
    NPC += _k


STAGES = {
    "pe": """c_mean c_var g_sum g_pairs g_tokp w_wa w_gatep w_ksum w_bonp p_rsum p_gsum p_rvar
             o_log r_rank""",
    "act": """rows_log c_gate c_sq c_rstd c_sig g_sig g_sq g_zsig g_rs g_eg g_texp w_lora w_sg
             w_gate w_e w_e5 w_sq w_krs p_gsq p_grs p_rsq p_rrs""",
    "vec": """rows_neg rows_done c_glu c_taps c_cen c_lin c_done g_taps g_silu g_tok g_prep w_mix
             w_cum w_cprev w_k1 w_bon w_prep p_rcen p_done o_lg o_w2 r_mask r_slots""",
}
AFTER = {n: i + 1 for v in STAGES.values() for i, n in enumerate(v.split())}


def own_order(engine, own):
    count = {}

    def mark(instruction, sem=None):
        sem = own if sem is None else sem
        count[sem.name] = count.get(sem.name, 0) + 1
        instruction.then_inc(sem, 1)

    def o(instruction, sem=None):
        mark(instruction, sem)
        sem = own if sem is None else sem
        engine.wait_ge(sem, count[sem.name])

    return o, mark


def step_kernel(nc, a):
    ctx = ExitStack()
    with ctx:
        def sb(name, words):
            return ctx.enter_context(nc.sbuf_tensor(name, [P, words], F32))

        def sem(name):
            return ctx.enter_context(nc.semaphore(name))

        def carve(region, at, *shape):
            n = int(np.prod(shape))
            v = region[:, at:at + n]
            if len(shape) > 1:
                names = "abcd"[:len(shape)]
                v = v.rearrange(f"p ({' '.join(names)}) -> p {' '.join(names)}",
                                **dict(zip(names[1:], shape[1:])))
            assert at + n <= region.shape[1], (region.name, at + n)
            return v, at + n

        def carve_all(region, at, *shapes):
            out = []
            for shape in shapes:
                v, at = carve(region, at, *shape)
                out.append(v)
            return out + [at]

        rH = sb("r_proj", NCH * HW)
        rX = sb("r_x", KD * T + RING * KD * P)
        rU = sb("r_unit", 14600)
        rG = sb("r_gdn", 10 * T)
        rM = sb("mix", 8 * T)
        mixT, _ = carve(rM, 0, 8, T)
        consts, _ = carve(sb("consts", len(CONST) * P), 0, len(CONST), P)
        sel, _ = carve(sb("sel", NSEL * P), 0, NSEL, P)
        par = sb("par", NPC)
        lora = sb("lora", GW)
        ch_mask = sb("chunk_mask", T)
        small = sb("small", 160)
        ps = ctx.enter_context(nc.psum_tensor("ps", [P, 8, 512], F32))

        def C(name):
            return consts[:, CONST.index(name), :]

        def pp(name, i=0, rows=slice(0, P)):
            at = PCOL[name] + i
            return par[rows, at:at + 1]

        ident = C("ident")

        hb, _ = carve(rH, 0, NCH, HW)
        xT, wat = carve(rX, 0, KD, T)
        wring = [carve(rX, wat + i * KD * P, KD, P)[0] for i in range(RING)]
        (rowy, rowG, rowGL, toks, uat) = carve_all(rU, 0, [T], [T], [T], [NT, 3, 12])
        beta, tG, nG, nbeg, eGL, decG, decR, eL = [small[:, i * 20:(i + 1) * 20] for i in range(8)]
        beta, tG, nG, nbeg, eGL = [v.rearrange("p (i h) -> p i h", h=4) for v in (beta, tG, nG, nbeg, eGL)]
        dec = sb("dec", 90)
        decG, decR = [dec[:, i * 36:(i + 1) * 36].rearrange("p (h c) -> p h c", c=9) for i in range(2)]
        eL = dec[:, 72:90].rearrange("p (h c) -> p h c", c=9)
        (rowz, rowt, Fp, Fs, kcT, vc, sc0, sc1, pT, vtok, _) = carve_all(
            rU, uat, [T], [T], [TP], [PAST + TS], [2, PAST], [8, GW], [PAST + TS], [PAST + TS], [2, T], [NT, GW])
        sc = [sc0, sc1]
        stat = sb("stat", 64)
        mx, rs = stat[:, 0:2], stat[:, 2:4]
        ealog = stat[:, 4:5]
        (cu, cacc, csig, ccen, csq, crs, _) = carve_all(
            rX, 0, [2, 2 * CPAD + T], [2, CPAD + T], [2, HW], [2, T], [2, T], [T])
        (gacc, gsig, _) = carve_all(rX, 0, [6, PAD + T], [6, PAD + T])
        (gsq, grs, geG, gz, _) = carve_all(rX, 0, [4, T], [4, T], [2, T], [2, HW])
        (gq, gk, gv, gR, gzs, _) = carve_all(rG, 0, [2, T], [2, T], [2, T], [2, T], [2, T])
        (xm, wsig, wcum, ta, tb, _) = carve_all(rX, 0, [7, T], [2, T], [2, T], [2, T], [2, T])
        (ac, bc, kc, rc, Au, Ru, Bb, Kb, gate, hat) = carve_all(rH, 0, *[[2, T]] * 9)
        bonus = xm[:, 2:4, :]
        xmv = xm[:, 4:6, :]
        U = []
        at = uat
        (N, NTm, ED, T1, QP, TPQ, BA, OUT, IS, NB, DmT, at) = carve_all(
            rU, at, [4, P], [4, P], [2, 4, P], [4, P], [4, P], [4, P], [4, 256], [4, 256], [5, 4, HD], [4, P], [4, P])
        U.append(dict(N=N, NT=NTm, ED=ED, T1=T1, QP=QP, TPQ=TPQ, BA=BA, OUT=OUT, IS=IS))
        (N, NTm, ED, T1, QP, TPQ, Aak, V, at) = carve_all(
            rU, at, [4, P], [4, P], [2, 4, P], [4, P], [4, P], [4, P], [4, P], [4, HD])
        (BA, KA, OUT, hat) = carve_all(rH, hat, [4, 256], [4, 256], [4, 256])
        IS, _ = carve(rX, 7 * T, 5, 4, HD)
        U.append(dict(N=N, NT=NTm, ED=ED, T1=T1, QP=QP, TPQ=TPQ, BA=BA, OUT=OUT, IS=IS))
        dg = [small[:, 0:1]] * 2
        (wout, xtok, _) = carve_all(rU, 0, [8, D], [NT, D])
        (x1, yacc, hT, hg, wr, logit, _) = carve_all(rH, 0, [NT, D], [NT, D], [2, T], [2, T], [KD, 20], [NT, 20])
        (lnp, _) = carve_all(rG, 0, [4, D])
        (x1T, rt, _) = carve_all(rX, 0, [KD, T], [1200])
        wgu = [carve(rU, i * 6144, KD, 2 * FF)[0] for i in range(2)]
        wdn = [carve(rU, i * 6144 + 4096, 2, D)[0] for i in range(2)]
        slots_x = nc.dram_tensor("slots_x", (EXPERTS * CAP, D), F32, kind="Internal").ap()
        slots_y = nc.dram_tensor("slots_y", (EXPERTS * CAP, D), F32, kind="Internal").ap()
        zero_rows = mixT[:, 2:4, :].rearrange("p c t -> p (c t)")[:, 0:D]
        xb = [carve(rU, 12288 + i * D, D)[0] for i in range(2)]
        (xbT0, xbT1, yb0, yb1, hrow, hTs, _) = carve_all(rM, 0, [KD, P], [KD, P], [D], [D], [FF], [2, P])
        xbT, yb = [xbT0, xbT1], [yb0, yb1]
        hs = hg[:, 0, 0:FF]
        got = carve(rU, 0, NT, 2, D)[0]
        (slot_c, rank, pos, M1, M2, Mx, sl, _) = carve_all(
            rX, KD * T + 1200, [2 * P + EXPERTS], [NT, EXPERTS], [NT, EXPERTS], [NT, EXPERTS], [NT, EXPERTS],
            [NT, EXPERTS], [2, NT])
        idx = ctx.enter_context(nc.sbuf_tensor("slot_index", [P, 2 * NT + 1], mybir.dt.int32))
        lasts = sb("lasts", 14)[:, :].rearrange("p (k c) -> p k c", k=2)
        bst = stat[:, 8:24]

        names = """dense_step ld_x ld_const ld_param ld_pad ld_cache ld_state ld_wout ld_xtok ld_lnp ld_router
            shift_rows proj_done evac_act evac_vec pads_zero zeros_set vt_pe vt_act s_done s_max s_exp
            p_ready t_done pt_copied pv_done o_act u_tr u_tok u_A u_dexp u_N u_diag u_P u_Pq u_NTp
            u_NTs u_E0 u_D0 u_T1p u_T1 u_EDp u_ED u_TPQp u_TPQ u_OUTp u_OUTs u_OUTv u_Sp u_S u_Op u_O
            u_mask o_y o_x o_var o_rstd o_x1 o_x1t o_x1T o_eg m_gu m_silu m_h m_dn m_acc f_var f_rstd
            f_y rows_zero slots_zero r_scat x_t x_ta x_tv x_gu x_silu x_h x_ht x_hT x_dn x_ya
            x_yv y_sum st_hb st_rows st_conv st_state st_y vec_step act_step pool_step pe_stage
            act_stage vec_stage""".split()
        S = {n: sem(n) for n in names}
        ld_w = [sem(f"ld_w{i}") for i in range(RING)]
        ld_e = [sem(f"ld_e{i}") for i in range(2)]
        ld_f = [sem(f"ld_f{i}") for i in range(2)]
        ld_got = [sem(f"ld_got{i}") for i in range(NT)]
        ld_d = [sem(f"ld_d{i}") for i in range(2)]
        ld_xb = [sem(f"ld_xb{i}") for i in range(2)]
        st_yb = [sem(f"st_yb{i}") for i in range(2)]

        HEADP = [(h // 2, (h % 2) * HD) for h in range(HEADS)]
        mixer_bank = [0, 4]
        JOINS = ["join2", "join4", "join8", "join16", "join32"]

        def tile_cols(i):
            return PAD + TILES[i][0] if i < 4 else SCOL

        def bank4(b, n, rows=None):
            return ps[0:(rows or n), b, 0:4 * n].rearrange("p (h t) -> p h t", h=4)

        def par_pair(v):
            return v.rearrange("p (pair par) t -> p par pair t", par=2)

        def two_banks(b, n):
            return ps[:, b:b + 2, 0:n]

        def halves(v):
            return v.rearrange("p (u t) -> p u t", u=2)

        def chunks(v):
            return v.rearrange("p c (k t) -> p c k t", t=CHUNK)

        def bcast(v, shape):
            return v.to_broadcast(shape) if not isinstance(v, (int, float)) else v

        def bc_mid(v, k):
            return v.rearrange("p (o t) -> p o t", o=1).to_broadcast([v.shape[0], k, v.shape[1]])

        block = ctx.enter_context(nc.Block())

        @block.sync
        def _(sp):
            sp.dma_start(xT, a["xT"]).then_inc(S["ld_x"], 16)
            for j in range(NCH):
                if j >= RING:
                    sp.wait_ge(S["proj_done"], j - RING + 1)
                sp.dma_start(wring[j % RING], a["w_in"][j]).then_inc(ld_w[j % RING], 16)
            sp.wait_ge(S["evac_act"], NCH)
            sp.wait_ge(S["evac_vec"], NCH)
            sp.wait_ge(S["ld_pad"], 16)
            for k, end in enumerate((PAD + TP, HW)):
                sp.dma_start(a["o_gconv"][:, k], hb[:, BQ:BQ + 6, end - PAD:end]).then_inc(S["st_hb"], 16)
            sp.wait_ge(S["shift_rows"], 1)
            sp.dma_start(a["o_shift"], lasts).then_inc(S["st_hb"], 16)
            for t0, n, c0 in PIECES:
                sp.dma_start(a["o_kv"][:, :, t0:t0 + n], hb[:, DK:DK + 4, c0:c0 + n]).then_inc(S["st_hb"], 16)
            sp.wait_ge(S["vec_stage"], AFTER["rows_done"])
            sp.dma_start(a["o_logf"], rowy[104:108, :]).then_inc(S["st_rows"], 16)
            sp.wait_ge(S["vec_stage"], AFTER["c_glu"])
            for k, end in enumerate((CPAD + TP, 2 * CPAD + T)):
                sp.dma_start(a["o_conv"][:, k], cu[:, :, end - CPAD:end]).then_inc(S["st_conv"], 16)
            for m in range(2):
                sp.wait_ge(S["u_S"], 2 * 7 + 2 + m + 1 if m == 0 else 18)
            sp.wait_ge(S["u_S"], 18)
            for m in range(2):
                for k, slot in enumerate((2, 4)):
                    sp.dma_start(a["o_state"][m, k], U[m]["IS"][TOP, slot]).then_inc(S["st_state"], 16)
            sp.wait_ge(S["st_state"], 64)
            sp.wait_ge(S["u_O"], 2 * NT)
            sp.dma_start(wout, a["w_out"]).then_inc(S["ld_wout"], 16)
            for i, (t0, n) in enumerate(TILES):
                sp.dma_start(xtok[0:n, i], a["x_tok"][t0:t0 + n]).then_inc(S["ld_xtok"], 16)
            sp.wait_ge(S["vec_stage"], AFTER["p_done"])
            for i in range(4):
                sp.dma_start(lnp[:, i], a["ln"][i:i + 1, :].to_broadcast([P, D])).then_inc(S["ld_lnp"], 16)
            sp.dma_start(wr, a["w_router"]).then_inc(S["ld_router"], 16)
            sp.dma_start(rt[:, 0:20], a["b_router"].to_broadcast([P, 20])).then_inc(S["ld_router"], 16)
            sp.dma_start(slot_c, a["slot_c"]).then_inc(S["ld_router"], 16)
            sp.wait_ge(S["o_x"], NT)

            def gate_up(e, loaded):
                sp.dma_start(wgu[e % 2], a["w_gu"][e]).then_inc(loaded[e % 2], 16)

            def down(e, loaded):
                sp.dma_start(wdn[e % 2], a["w_dn"][e]).then_inc(loaded[e % 2], 16)

            def block_rows(e):
                sp.dma_start(xb[e % 2], slots_x[e * CAP:(e + 1) * CAP]).then_inc(ld_xb[e % 2], 16)

            gate_up(0, ld_e)
            down(0, ld_f)
            gate_up(1, ld_e)
            down(1, ld_f)
            sp.wait_ge(S["r_scat"], 32 * NT)
            sp.wait_ge(S["slots_zero"], 16)
            block_rows(0)
            block_rows(1)
            for e in range(1, EXPERTS):
                if e + 1 < EXPERTS:
                    sp.wait_ge(S["x_t"], e)
                    block_rows(e + 1)
                    sp.wait_ge(S["x_gu"], e)
                    gate_up(e + 1, ld_e)
                if e >= 2:
                    sp.wait_ge(S["x_dn"], e - 1)
                    down(e, ld_f)
            most = sp.value_load(idx[0:1, 2 * NT:], min_val=0, max_val=T)
            with sp.If(most > CAP):
                sp.wait_ge(S["y_sum"], NT)
                for e in range(EXPERTS):
                    if e >= 2:
                        sp.wait_ge(S["m_dn"], (e - 1) * NT)
                    gate_up(e, ld_d)
                    down(e, ld_d)
            for i, (t0, n) in enumerate(TILES):
                sp.wait_ge(S["f_y"], i + 1)
                sp.dma_start(a["o_y"][t0:t0 + n], x1[0:n, i]).then_inc(S["st_y"], 16)
            sp.wait_ge(S["st_y"], 16 * NT)
            sp.wait_ge(S["st_hb"], 80)
            sp.wait_ge(S["st_rows"], 16)
            sp.wait_ge(S["st_conv"], 32)

        @block.gpsimd
        def _(pool):
            o, mark = own_order(pool, S["pool_step"])
            o(nc.gpsimd.memset(zero_rows, 0.0), S["rows_zero"])
            pool.dma_start(slots_x.rearrange("(e p) d -> p e d", p=P),
                           zero_rows.rearrange("p (o d) -> p o d", o=1).to_broadcast([P, EXPERTS, D])).then_inc(S["slots_zero"], 16)
            nc.gpsimd.memset(hb[:, :, 0:PAD], 0.0).then_inc(S["pads_zero"], 1)
            nc.gpsimd.memset(Fp, 0.0)
            nc.gpsimd.memset(Fs, 0.0)
            nc.gpsimd.memset(toks, 0.0).then_inc(S["zeros_set"], 1)
            pool.wait_ge(S["o_act"], 20)
            pool.wait_ge(S["vec_stage"], AFTER["w_mix"])
            pool.wait_ge(S["st_hb"], 80)
            pool.wait_ge(S["vec_stage"], AFTER["w_prep"])
            for u in U:
                nc.gpsimd.memset(u["BA"], 0.0)
                o(nc.gpsimd.memset(u["IS"], 0.0))
                for c in range(5):
                    for h in range(HEADS):
                        nc.gpsimd.affine_select(out=u["IS"][LOW, c, h], in_=u["IS"][LOW, c, h],
                                                compare_op=ALU.not_equal, fill=1.0, base=0,
                                                pattern=[[-1, HD]], channel_multiplier=1)
            nc.gpsimd.memset(KA, 0.0).then_inc(S["u_mask"], 1)
            for i, (t0, n) in enumerate(TILES):
                for m, u in enumerate(U):
                    k = 2 * i + m + 1
                    pool.wait_ge(S["u_N"], k)
                    d = u["N"][0:n, :, 0:n]
                    nc.gpsimd.affine_select(out=d, in_=d, compare_op=ALU.not_equal, fill=1.0, base=0,
                                            pattern=[[0, 4], [-1, n]], channel_multiplier=1).then_inc(S["u_diag"], 1)
                for m, u in enumerate(U):
                    k = 2 * i + m + 1
                    pool.wait_ge(S["u_diag"], k)
                    nc.gpsimd.tensor_tensor(u["ED"][0:n, 1, :, 0:n], u["N"][0:n, :, 0:n],
                                            bc_mid(C("first_l")[0:n, 0:n], 4), ALU.mult).then_inc(S["u_D0"], 1)

            pool.wait_ge(S["vec_stage"], AFTER["r_slots"])
            pool.wait_ge(S["slots_zero"], 16)
            for i, (t0, n) in enumerate(TILES):
                for k in range(2):
                    c = k * NT + i
                    pool.indirect_dma_start(slots_x[:, :], bass.IndirectOffsetOnAxis(idx[0:n, c:c + 1], 0), x1[0:n, i], None,
                                            bounds_check=EXPERTS * CAP - 1, oob_is_err=False).then_inc(S["r_scat"], 16)
            pool.wait_ge(S["x_dn"], EXPERTS)
            for k in range(2):
                pool.wait_ge(st_yb[k], 8 * EXPERTS)
            for i, (t0, n) in enumerate(TILES):
                for k in range(2):
                    c = k * NT + i
                    pool.indirect_dma_start(got[0:n, i, k], None, slots_y[:, :], bass.IndirectOffsetOnAxis(idx[0:n, c:c + 1], 0),
                                            bounds_check=EXPERTS * CAP - 1, oob_is_err=False).then_inc(ld_got[i], 16)

        @block.scalar
        def _(act):
            o, mark = own_order(act, S["act_step"])
            A = nc.scalar.activation
            act.dma_start(consts, a["consts"]).then_inc(S["ld_const"], 16)
            act.dma_start(sel, a["sel"]).then_inc(S["ld_const"], 16)
            act.dma_start(par[:, :], a["params"]).then_inc(S["ld_param"], 16)
            act.dma_start(lora[:, :], a["lora"]).then_inc(S["ld_param"], 16)
            act.dma_start(ch_mask[:, :], a["ch_mask"]).then_inc(S["ld_param"], 16)
            act.dma_start(hb[:, :, SCOL - PAD:SCOL], a["pads"]).then_inc(S["ld_pad"], 16)
            act.dma_start(kcT, a["k_cache"]).then_inc(S["ld_cache"], 16)
            act.dma_start(vc, a["v_cache"]).then_inc(S["ld_cache"], 16)
            act.dma_start(sc1[ROWS, 0:PAST], a["f_cache"]).then_inc(S["ld_cache"], 16)
            for j in range(NCH):
                act.wait_ge(S["proj_done"], j + 1)
                nc.scalar.copy(hb[:, j, PAD:PAD + HALF], ps[:, 2 * (j % RING), 0:HALF]).then_inc(S["evac_act"], 1)
            act.wait_ge(S["vec_stage"], AFTER["rows_neg"])
            act.wait_ge(S["ld_param"], 48)
            o(A(rowt[ROWS, :], rowt[ROWS, :], ACT.Exp))
            A(ealog[ROWS, :], pp("row_alog", 0, ROWS), ACT.Exp)
            A(rowt[ROWS, :], rowt[ROWS, :], ACT.Ln, bias=1.0).then_inc(S["act_stage"], 1)
            for i, (t0, n) in enumerate(TILES):
                act.wait_ge(S["vt_pe"], i + 1)
                nc.scalar.copy(vtok[0:n, i], ps[0:n, 6 + i % 2, 0:GW]).then_inc(S["vt_act"], 1)
            units = [(i, h) for i in range(NT) for h in range(HEADS)]

            def exps(u):
                i, h = units[u]
                n = TILES[i][1]
                nk = P * (i + 1) if i < 4 else PAST + TS
                act.wait_ge(S["s_max"], u + 1)
                A(sc[u % 2][0:n, 0:nk], sc[u % 2][0:n, 0:nk], ACT.Exp, bias=mx[0:n, u % 2:u % 2 + 1],
                  accum_out=rs[0:n, u % 2:u % 2 + 1]).then_inc(S["s_exp"], 1)

            exps(0)
            for u, (i, h) in enumerate(units):
                n = TILES[i][1]
                pair, pb = HEADP[h]
                if u + 1 < len(units):
                    exps(u + 1)
                act.wait_ge(S["t_done"], u + 1)
                if i < 4:
                    nc.scalar.copy(pT[:, u % 2, 0:P * (i + 1)], ps[:, 6 + u % 2, 0:P * (i + 1)]).then_inc(S["pt_copied"], 1)
                else:
                    nc.scalar.copy(pT[:, u % 2, 0:512], ps[:, 6 + u % 2, :])
                    nc.scalar.copy(pT[LOW, u % 2, 512:T], ps[LOW, 3 * (u % 2) + 2, 64:128]).then_inc(S["pt_copied"], 1)
                act.wait_ge(S["pv_done"], u + 1)
                t0 = TILES[i][0]
                nc.scalar.copy(mixT[pb:pb + HD, 6 + pair, t0:t0 + n], ps[pb:pb + HD, 3 * (u % 2), 0:n]).then_inc(S["o_act"], 1)
            act.wait_ge(S["evac_vec"], NCH)
            act.dma_start(cu[:, :, CPAD + TP:2 * CPAD + TP], a["conv_state"]).then_inc(S["ld_state"], 16)
            A(csig, hb[:, GATE:GATE + 2, :], ACT.Sigmoid).then_inc(S["act_stage"], 1)
            act.wait_ge(S["vec_stage"], AFTER["c_cen"])
            A(csq, ccen, ACT.Square).then_inc(S["act_stage"], 1)
            act.wait_ge(S["pe_stage"], AFTER["c_var"])
            o(A(halves(crs), two_banks(2, HALF), ACT.Ln, bias=LN_EPS))
            A(crs, crs, ACT.Exp, scale=-0.5).then_inc(S["act_stage"], 1)
            act.wait_ge(S["vec_stage"], AFTER["c_lin"])
            A(csq, ccen, ACT.Sigmoid).then_inc(S["act_stage"], 1)
            act.wait_ge(S["vec_stage"], AFTER["g_taps"])
            A(gsig, gacc, ACT.Sigmoid).then_inc(S["act_stage"], 1)
            act.wait_ge(S["vec_stage"], AFTER["g_silu"])
            A(gsq, rG[:, 0:4 * T].rearrange("p (c t) -> p c t", c=4), ACT.Square).then_inc(S["act_stage"], 1)
            A(gz, hb[:, BZ:BZ + 2, :], ACT.Sigmoid).then_inc(S["act_stage"], 1)
            act.wait_ge(S["pe_stage"], AFTER["g_sum"])
            o(A(grs.rearrange("p c (u t) -> p (c u) t", u=2), ps[:, :, 0:HALF], ACT.Ln, bias=L2_EPS))
            A(grs, grs, ACT.Exp, scale=-0.5).then_inc(S["act_stage"], 1)
            act.wait_ge(S["pe_stage"], AFTER["g_pairs"])
            A(geG.rearrange("p c (u t) -> p (c u) t", u=2), ps[:, 0:4, 0:HALF], ACT.Exp)
            A(decG[TOP], ps[TOP, 4, 0:36].rearrange("p (h c) -> p h c", c=9), ACT.Exp).then_inc(S["act_stage"], 1)
            act.wait_ge(S["vec_stage"], AFTER["g_tok"])
            A(beta, toks[:, :, 0, 4:8], ACT.Exp)
            A(nbeg, tG, ACT.Exp)
            A(eGL, toks[:, :, 2, 0:4], ACT.Exp).then_inc(S["act_stage"], 1)
            act.wait_ge(S["vec_stage"], AFTER["w_mix"])
            A(xm[0:16, 6], xm[0:16, 6], ACT.Tanh)
            A(xm[64:96, 6], xm[64:96, 6], ACT.Sigmoid).then_inc(S["act_stage"], 1)
            act.wait_ge(S["pe_stage"], AFTER["w_wa"])
            for c in range(2):
                A(halves(wsig[:, c]), two_banks(2 * c, HALF), ACT.Sigmoid, bias=pp("w0", c))
                last = A(halves(ta[:, c]), two_banks(4 + 2 * c, HALF), ACT.Sigmoid, bias=pp("a0", c))
            last.then_inc(S["act_stage"], 1)
            act.wait_ge(S["pe_stage"], AFTER["w_gatep"])
            act.wait_ge(S["st_hb"], 80)
            nc.scalar.copy(gate.rearrange("p c (u t) -> p (c u) t", u=2), ps[:, 0:4, 0:HALF]).then_inc(S["act_stage"], 1)
            act.wait_ge(S["vec_stage"], AFTER["w_cum"])
            A(rc, tb, ACT.Exp, scale=-DECAY)
            A(kc, tb, ACT.Exp, scale=DECAY)
            A(Ru, wcum, ACT.Exp, scale=-DECAY)
            A(eL, eL, ACT.Exp, scale=-DECAY)
            for q in range(2):
                last = A(decR[TOP, q::2, :], wcum[q * HD:(q + 1) * HD, :, CHUNK - 1::CHUNK], ACT.Exp, scale=-DECAY)
            last.then_inc(S["act_stage"], 1)
            act.wait_ge(S["vec_stage"], AFTER["w_cprev"])
            A(ac, tb, ACT.Exp, scale=-DECAY)
            A(Au, wsig, ACT.Exp, scale=-DECAY).then_inc(S["act_stage"], 1)
            act.wait_ge(S["vec_stage"], AFTER["w_k1"])
            A(tb, wsig, ACT.Square).then_inc(S["act_stage"], 1)
            act.wait_ge(S["pe_stage"], AFTER["w_ksum"])
            o(A(tb.rearrange("p c (u t) -> p (c u) t", u=2), ps[:, 4:8, 0:HALF], ACT.Ln, bias=L2_EPS))
            A(tb, tb, ACT.Exp, scale=-0.5).then_inc(S["act_stage"], 1)
            act.wait_ge(S["u_mask"], 1)
            act.dma_start(U[0]["IS"][TOP, 3], a["s_gdn"]).then_inc(S["ld_state"], 16)
            act.dma_start(U[1]["IS"][TOP, 3], a["s_rwkv"]).then_inc(S["ld_state"], 16)
            act.wait_ge(S["vec_stage"], AFTER["w_prep"])
            act.wait_ge(S["slots_zero"], 16)
            for i, (t0, n) in enumerate(TILES):
                nch = n // CHUNK
                k0 = 2 * i
                act.wait_ge(S["u_mask"], 2 + i)
                for h in range(HEADS):
                    A(NB[0:n, h, 0:n], NB[0:n, h, 0:n], ACT.Exp, bias=tG[0:n, i, h:h + 1])
                    last = A(DmT[0:n, h, 0:n], DmT[0:n, h, 0:n], ACT.Exp, bias=nG[0:n, i, h:h + 1])
                last.then_inc(S["u_dexp"], 1)
                act.wait_ge(S["u_tr"], k0 + 2)
                u = U[1]
                t4 = bank4(4, P, n)
                nc.scalar.copy(u["QP"][0:n, :, HD:P], ps[0:n, 4, 0:GW].rearrange("p (h t) -> p h t", h=4))
                nc.scalar.copy(V[0:n], ps[0:n, 4, GW:512].rearrange("p (h t) -> p h t", h=4))
                for c in range(nch):
                    r = slice(c * CHUNK, (c + 1) * CHUNK)
                    nc.scalar.copy(u["BA"][r, :, r], ps[r, 5, 0:GW].rearrange("p (h t) -> p h t", h=4))
                    last = nc.scalar.copy(KA[r, :, r], ps[r, 5, GW:512].rearrange("p (h t) -> p h t", h=4))
                last.then_inc(S["u_tok"], 1)
                for m, u in enumerate(U):
                    act.wait_ge(S["u_NTp"], k0 + m + 1)
                    nc.scalar.copy(u["NT"][0:n, :, 0:n], bank4(mixer_bank[m] + 1, n)).then_inc(S["u_NTs"], 1)
                for m, u in enumerate(U):
                    act.wait_ge(S["u_TPQp"], k0 + m + 1)
                    nc.scalar.copy(u["TPQ"][0:n], ps[0:n, mixer_bank[m] + 3, :].rearrange("p (h t) -> p h t", h=4)).then_inc(S["u_TPQ"], 1)
                for m, u in enumerate(U):
                    b = mixer_bank[m]
                    act.wait_ge(S["u_OUTp"], k0 + m + 1)
                    src = ps[:, b:b + 2, :].rearrange("p b (h t) -> p (b h) t", h=2)
                    nc.scalar.copy(u["OUT"][LOW, :, 0:P], src[LOW, :, 0:P])
                    nc.scalar.copy(u["OUT"][:, :, P:P + n], src[:, :, P:P + n]).then_inc(S["u_OUTs"], 1)
                for m, u in enumerate(U):
                    act.wait_ge(S["u_Op"], k0 + m + 1)
                    nc.scalar.copy(mixT[:, 2 + 2 * m:4 + 2 * m, t0:t0 + n],
                                   ps[:, mixer_bank[m] + 3, 0:2 * n].rearrange("p (c t) -> p c t", c=2)).then_inc(S["u_O"], 1)
            act.wait_ge(S["u_O"], 2 * NT)
            A(ta, mixT[:, 2:4], ACT.Square).then_inc(S["act_stage"], 1)
            act.wait_ge(S["pe_stage"], AFTER["p_gsum"])
            o(A(ta.rearrange("p c (u t) -> p (c u) t", u=2), ps[:, 0:4, 0:HALF], ACT.Ln, bias=RMS_EPS, scale=1.0 / HD))
            A(ta, ta, ACT.Exp, scale=-0.5).then_inc(S["act_stage"], 1)
            act.wait_ge(S["vec_stage"], AFTER["p_rcen"])
            A(tb, mixT[:, 4:6], ACT.Square).then_inc(S["act_stage"], 1)
            act.wait_ge(S["pe_stage"], AFTER["p_rvar"])
            o(A(tb.rearrange("p c (u t) -> p (c u) t", u=2), ps[:, 0:4, 0:HALF], ACT.Ln, bias=GN_EPS, scale=1.0 / HD))
            A(tb, tb, ACT.Exp, scale=-0.5).then_inc(S["act_stage"], 1)
            for i, (t0, n) in enumerate(TILES):
                act.wait_ge(S["o_var"], i + 1)
                o(A(stat[0:n, 24:25], stat[0:n, 21:22], ACT.Ln, bias=LN_EPS))
                A(stat[0:n, 24:25], stat[0:n, 24:25], ACT.Exp, scale=-0.5).then_inc(S["o_rstd"], 1)
                act.wait_ge(S["o_x1t"], i + 1)
                nc.scalar.copy(x1T[:, :, t0:t0 + n], ps[:, 4:6, 0:4 * n].rearrange("p b (k t) -> p b k t", t=n)).then_inc(S["o_x1T"], 1)
            act.wait_ge(S["vec_stage"], AFTER["o_lg"])
            A(rt[:, 40:60], rt[:, 40:60], ACT.Exp).then_inc(S["o_eg"], 1)
            act.wait_ge(S["vec_stage"], AFTER["o_w2"])
            A(rt[:, 60:65], rt[:, 60:65], ACT.Exp).then_inc(S["o_eg"], 1)
            for e in range(EXPERTS + 2):
                if e < EXPERTS:
                    act.wait_ge(S["x_t"], e + 1)
                    nc.scalar.copy(xbT[e % 2][:, 0:4], ps[:, 0].rearrange("p (k t) -> p k t", k=4)).then_inc(S["x_ta"], 1)
                if 1 <= e <= EXPERTS:
                    act.wait_ge(S["x_gu"], e)
                    if e >= 2:
                        act.wait_ge(S["x_h"], e - 1)
                    A(hs, ps[:, 2 + (e - 1) % 2, 0:FF], ACT.Silu).then_inc(S["x_silu"], 1)
                if e >= 2:
                    d = e - 2
                    act.wait_ge(S["x_dn"], d + 1)
                    if d >= 2:
                        act.wait_ge(st_yb[d % 2], 16 * (d // 2))
                    nc.scalar.copy(yb[d % 2][:, 0:512], ps[:, 5]).then_inc(S["x_ya"], 1)
                    act.wait_ge(S["x_ya"], d + 1)
                    act.wait_ge(S["x_yv"], d + 1)
                    act.dma_start(slots_y[d * CAP:(d + 1) * CAP], yb[d % 2]).then_inc(st_yb[d % 2], 16)
            most = act.value_load(idx[0:1, 2 * NT:], min_val=0, max_val=T)
            with act.If(most > CAP):
                for e in range(EXPERTS):
                    for f in range(2):
                        act.wait_ge(S["m_gu"], 2 * e + f + 1)
                        if e >= 1:
                            act.wait_ge(S["m_h"], 2 * (e - 1) + f + 1)
                        A(halves(hg[:, f]), two_banks(4 * f, HALF), ACT.Silu).then_inc(S["m_silu"], 1)
            for i, (t0, n) in enumerate(TILES):
                act.wait_ge(S["f_var"], i + 1)
                o(A(stat[0:n, 24:25], stat[0:n, 21:22], ACT.Ln, bias=LN_EPS))
                A(stat[0:n, 24:25], stat[0:n, 24:25], ACT.Exp, scale=-0.5).then_inc(S["f_rstd"], 1)

        @block.vector
        def _(dve):
            o, mark = own_order(dve, S["vec_step"])
            v = nc.vector
            STT, TT, TSC = v.scalar_tensor_tensor, v.tensor_tensor, v.tensor_scalar
            for j in range(NCH):
                dve.wait_ge(S["proj_done"], j + 1)
                b = 2 * (j % RING) + 1
                k = TP - HALF
                v.tensor_copy(hb[:, j, PAD + HALF:PAD + TP], ps[:, b, 0:k])
                o(v.tensor_copy(hb[:, j, SCOL:SCOL + TS], ps[:, b, k:HALF]), S["evac_vec"])
            dve.wait_ge(S["evac_act"], NCH)
            for k, end in enumerate((PAD + TP, HW)):
                v.tensor_copy(lasts[:, k, 0:6], hb[:, CR:CR + 6, end - 1])
                last = v.tensor_copy(lasts[:, k, 6:7], hb[:, SMALL, end - 1:end])
            mark(last, S["shift_rows"])
            dve.wait_ge(S["evac_act"], NCH)
            dve.wait_ge(S["ld_param"], 48)
            dve.wait_ge(S["ld_cache"], 48)
            dve.wait_ge(S["zeros_set"], 1)
            for t0, n, c0 in PIECES:
                o(TSC(rowz[ROWS, t0:t0 + n], hb[ROWS, SMALL, c0:c0 + n], pp("row_bias", 0, ROWS),
                      pp("row_sign", 0, ROWS), ALU.add, ALU.mult))
            o(STT(rowt[ROWS, :], rowz[ROWS, :], -1.0, rowz[ROWS, :], ALU.mult, ALU.min), S["vec_stage"])
            dve.wait_ge(S["act_stage"], AFTER["rows_log"])
            o(STT(rowy[ROWS, :], rowz[ROWS, :], 0.0, rowt[ROWS, :], ALU.max, ALU.add))
            o(TSC(rowy[ROWS, :], rowy[ROWS, :], ealog[ROWS, :], -1.0, ALU.mult, ALU.mult))
            o(v.tensor_tensor_scan(rowG[ROWS, :], ch_mask[ROWS, :], rowy[ROWS, :], 0.0, ALU.mult, ALU.add))
            G3 = rowG[ROWS, :].rearrange("p (k t) -> p k t", t=CHUNK)
            o(TT(rowGL[ROWS, :].rearrange("p (k t) -> p k t", t=CHUNK),
                 G3[:, :, CHUNK - 1:CHUNK].to_broadcast([12, 9, CHUNK]), G3, ALU.subtract))
            SCAN = v.tensor_tensor_scan
            o(SCAN(Fp[ROWS, :], rowy[ROWS, 0:TP], rowy[ROWS, 0:TP], 0.0, ALU.add, ALU.min))
            o(SCAN(Fs[ROWS, 0:PAST], sc1[ROWS, 0:PAST], sc1[ROWS, 0:PAST], 0.0, ALU.add, ALU.min))
            o(SCAN(Fs[ROWS, PAST:], rowy[ROWS, TP:], rowy[ROWS, TP:], Fs[ROWS, PAST - 1:PAST], ALU.add, ALU.min),
              S["vec_stage"])
            units = [(i, h) for i in range(NT) for h in range(HEADS)]

            def scores(u):
                i, h = units[u]
                n = TILES[i][1]
                nk = P * i if i < 4 else PAST
                b, s = 3 * (u % 2), sc[u % 2]
                dve.wait_ge(S["s_done"], u + 1)
                if u >= 2:
                    dve.wait_ge(S["t_done"], u - 1)
                if nk:
                    src = ps[0:n, b, 0:nk] if i < 4 else ps[0:n, b:b + 2, :].rearrange("p b t -> p (b t)")
                    o(TSC(s[0:n, 0:nk], src, HD ** -0.5, None, ALU.mult))
                diag = ps[0:n, b, nk:nk + n] if i < 4 else ps[0:n, b + 2, 0:n]
                o(STT(s[0:n, nk:nk + n], diag, HD ** -0.5, C("neg_causal")[0:n, 0:n], ALU.mult, ALU.add))
                o(v.reduce_max(mx[0:n, u % 2:u % 2 + 1], s[0:n, 0:nk + n], AX))
                o(TSC(mx[0:n, u % 2:u % 2 + 1], mx[0:n, u % 2:u % 2 + 1], -1.0, None, ALU.mult), S["s_max"])

            dve.wait_ge(S["ld_const"], 32)
            scores(0)
            for u, (i, h) in enumerate(units):
                if u + 1 < len(units):
                    scores(u + 1)
                n = TILES[i][1]
                nk = P * (i + 1) if i < 4 else PAST + TS
                dve.wait_ge(S["s_exp"], u + 1)
                o(v.reciprocal(rs[0:n, u % 2:u % 2 + 1], rs[0:n, u % 2:u % 2 + 1]))
                o(TSC(sc[u % 2][0:n, 0:nk], sc[u % 2][0:n, 0:nk], rs[0:n, u % 2:u % 2 + 1], None, ALU.mult), S["p_ready"])
            dve.wait_ge(S["proj_done"], NCH)
            o(v.memset(cu[:, :, 0:CPAD], 0.0))
            dve.wait_ge(S["ld_state"], 16)
            dve.wait_ge(S["act_stage"], AFTER["c_gate"])
            TT(cu[:, :, CPAD:CPAD + TP], csig[:, :, PAD:PAD + TP], hb[:, VAL:VAL + 2, PAD:PAD + TP], ALU.mult)
            o(TT(cu[:, :, 2 * CPAD + TP:], csig[:, :, SCOL:], hb[:, VAL:VAL + 2, SCOL:], ALU.mult), S["vec_stage"])
            NC_ = CPAD + T
            for j in range(CW):
                for c in range(2):
                    w = pp("conv_w", c * CW + j)
                    if j == 0:
                        o(TSC(cacc[:, c], cu[:, c, 0:NC_], w, pp("conv_b", c), ALU.mult, ALU.add))
                    else:
                        o(STT(cacc[:, c], cu[:, c, j:j + NC_], w, cacc[:, c], ALU.mult, ALU.add),
                          S["vec_stage"] if (j, c) == (CW - 1, 1) else None)
            dve.wait_ge(S["pe_stage"], AFTER["c_mean"])
            TT(ccen[:, :, 0:TP], cacc[:, :, 0:TP], bc_mid(ps[:, 0, :], 2), ALU.subtract)
            o(TT(ccen[:, :, TP:], cacc[:, :, CPAD + TP:], bc_mid(ps[:, 1, 0:TS], 2), ALU.subtract), S["vec_stage"])
            dve.wait_ge(S["act_stage"], AFTER["c_rstd"])
            o(TT(ccen, ccen, bc_mid(crs, 2), ALU.mult))
            for c in range(2):
                o(TSC(ccen[:, c], ccen[:, c], pp("conv_g", c), pp("conv_lb", c), ALU.mult, ALU.add),
                  S["vec_stage"] if c == 1 else None)
            dve.wait_ge(S["act_stage"], AFTER["c_sig"])
            o(TT(mixT[:, 0:2], ccen, csq, ALU.mult), S["vec_stage"])
            dve.wait_ge(S["st_conv"], 32)
            dve.wait_ge(S["pads_zero"], 1)
            dve.wait_ge(S["ld_pad"], 16)
            for j in range(GTAPS):
                for c in range(6):
                    w = pp("gconv_w", c * GTAPS + j)
                    src = hb[:, BQ + c, j:j + PAD + T]
                    if j == 0:
                        o(TSC(gacc[:, c], src, w, None, ALU.mult))
                    else:
                        o(STT(gacc[:, c], src, w, gacc[:, c], ALU.mult, ALU.add),
                          S["vec_stage"] if (j, c) == (GTAPS - 1, 5) else None)
            dve.wait_ge(S["act_stage"], AFTER["g_sig"])
            qkv = rG[:, 0:6 * T].rearrange("p (c t) -> p c t", c=6)
            TT(qkv[:, :, 0:TP], gacc[:, :, 0:TP], gsig[:, :, 0:TP], ALU.mult)
            o(TT(qkv[:, :, TP:], gacc[:, :, PAD + TP:], gsig[:, :, PAD + TP:], ALU.mult), S["vec_stage"])
            dve.wait_ge(S["act_stage"], AFTER["g_zsig"])
            for t0, n, c0 in PIECES:
                o(TT(gzs[:, :, t0:t0 + n], hb[:, BZ:BZ + 2, c0:c0 + n], gz[:, :, c0:c0 + n], ALU.mult))
            dve.wait_ge(S["act_stage"], AFTER["g_rs"])
            o(STT(gq, gq, HD ** -0.5, grs[:, 0:2], ALU.mult, ALU.mult))
            o(TT(gk, gk, grs[:, 2:4], ALU.mult))
            dve.wait_ge(S["act_stage"], AFTER["g_eg"])
            o(TT(gR, gq, geG, ALU.mult))
            dve.wait_ge(S["pe_stage"], AFTER["g_tokp"])
            tk = ps[:, 5, 0:NT * 36].rearrange("p (i k r) -> p i k r", k=3, r=12)
            v.tensor_copy(toks[:, 0:4], tk[:, 0:4])
            o(v.tensor_copy(toks[LOW, 4], tk[LOW, 4]))
            o(TT(tG, toks[:, :, 1, 0:4], toks[:, :, 0, 4:8], ALU.add))
            o(TSC(nG, toks[:, :, 1, 0:4], -1.0, None, ALU.mult), S["vec_stage"])
            dve.wait_ge(S["act_stage"], AFTER["g_texp"])
            o(TSC(nbeg, nbeg, -1.0, None, ALU.mult), S["vec_stage"])
            for c in range(7):
                src = hb[:, CR + c if c < 6 else SMALL]
                m = pp("mu", c) if c < 6 else pp("mu_s")
                d = wcum[:, :, :].rearrange("p c t -> p (c t)")[:, 0:PAD + T]
                o(TT(d, src[:, PAD - 1:HW - 1], src[:, PAD:HW], ALU.subtract))
                for t0, n, c0 in PIECES:
                    o(STT(xm[:, c, t0:t0 + n], d[:, c0 - PAD:c0 - PAD + n], m, src[:, c0:c0 + n], ALU.mult, ALU.add),
                      S["vec_stage"] if (c, t0) == (6, TP) else None)
            dve.wait_ge(S["act_stage"], AFTER["w_sg"])
            for c in range(2):
                o(SCAN(wcum[:, c], ch_mask[:, :], wsig[:, c], 0.0, ALU.mult, ALU.add))
            W4 = chunks(wcum)
            for c in range(2):
                o(TT(chunks(tb)[:, c], W4[:, c], W4[:, c, :, 31:32].to_broadcast([P, 9, CHUNK]), ALU.subtract))
            o(TT(eL, W4[:, :, :, 63:64].rearrange("p c k o -> p c (k o)"),
                 W4[:, :, :, 31:32].rearrange("p c k o -> p c (k o)"), ALU.subtract), S["vec_stage"])
            dve.wait_ge(S["act_stage"], AFTER["w_e"])
            o(TT(tb, tb, wsig, ALU.subtract))
            o(TT(wsig, wcum, wsig, ALU.subtract), S["vec_stage"])
            dve.wait_ge(S["act_stage"], AFTER["w_e5"])
            r, k = xm[:, 0:2], xm[:, 2:4]
            for c in range(2):
                o(TSC(wsig[:, c], k[:, c], pp("k_k", c), None, ALU.mult), S["vec_stage"] if c == 1 else None)
            dve.wait_ge(S["act_stage"], AFTER["w_krs"])
            o(TT(wsig, wsig, tb, ALU.mult))
            o(STT(ac, wsig, -1.0, ac, ALU.mult, ALU.mult))
            o(STT(Au, wsig, -1.0, Au, ALU.mult, ALU.mult))
            o(TT(tb, wsig, ta, ALU.mult))
            o(TT(bc, tb, kc, ALU.mult))
            for c in range(2):
                o(TSC(ta[:, c], ta[:, c], 1.0, pp("k_a", c), ALU.subtract, ALU.mult))
            o(STT(k, ta, 1.0, k, ALU.add, ALU.mult))
            for c in range(2):
                o(STT(tb[:, c], r[:, c], pp("r_k", c), k[:, c], ALU.mult, ALU.mult),
                  S["vec_stage"] if c == 1 else None)
            o(TT(kc, k, kc, ALU.mult))
            o(TT(rc, r, rc, ALU.mult))
            o(TT(Ru, r, Ru, ALU.mult))
            for c in range(2):
                e = eL[:, c].rearrange("p (k o) -> p k o", o=1).to_broadcast([P, 9, CHUNK])
                o(TT(chunks(Bb)[:, c], chunks(bc)[:, c], e, ALU.mult))
                o(TT(chunks(Kb)[:, c], chunks(kc)[:, c], e, ALU.mult))
            dve.wait_ge(S["pe_stage"], AFTER["w_bonp"])
            o(TT(bonus.rearrange("p c (u t) -> p (c u) t", u=2), xmv.rearrange("p c (u t) -> p (c u) t", u=2),
                 ps[:, 4:8, 0:HALF], ALU.mult), S["vec_stage"])
            dve.wait_ge(S["u_mask"], 1)
            dve.wait_ge(S["ld_state"], 48)
            for i, (t0, n) in enumerate(TILES):
                k0 = 2 * i
                nch = n // CHUNK
                g, w = U
                dve.wait_ge(S["u_tr"], k0 + 1)
                Gb = bank4(1, n)
                STT(NB[0:n, :, 0:n], Gb, -1.0, bc_mid(C("neg_strict_l")[0:n, 0:n], 4), ALU.mult, ALU.add)
                mark(TT(DmT[0:n, :, 0:n], Gb, bc_mid(C("neg_incl_u")[0:n, 0:n], 4), ALU.add), S["u_mask"])
                kt = ps[0:n, 0, 0:GW].rearrange("p (h t) -> p h t", h=4)
                vt = ps[0:n, 0, GW:512].rearrange("p (h t) -> p h t", h=4)

                def per_token(x, rows, m=64):
                    return x[rows, i].rearrange("p (h o) -> p h o", o=1).to_broadcast([rows.stop - rows.start, 4, m])

                rn = slice(0, n)
                TT(g["QP"][0:n, :, 0:HD], vt, per_token(beta, rn), ALU.mult)
                TT(g["QP"][0:n, :, HD:P], kt, per_token(nbeg, rn), ALU.mult)
                for c in range(nch):
                    rr = slice(c * CHUNK, (c + 1) * CHUNK)
                    TT(g["BA"][rr, :, rr], kt[rr], per_token(eGL, rr), ALU.mult)
                dve.wait_ge(S["u_dexp"], i + 1)
                dve.wait_ge(S["u_A"], k0 + 1)
                for q in range(2):
                    blk = ps[0:n, 2 + q, 0:4 * n].rearrange("p (k c t) -> p k c t", k=2, c=2)
                    STT(g["N"][0:n, q::2, 0:n], blk[:, 0], -1.0, NB[0:n, q::2, 0:n], ALU.mult, ALU.mult)
                    last = TT(g["BA"][0:n, q::2, P:P + n], blk[:, 1], DmT[0:n, q::2, 0:n], ALU.mult)
                o(last, S["u_N"])
                dve.wait_ge(S["u_A"], k0 + 2)
                for q in range(2):
                    blk = ps[0:n, 4 + 2 * q, 0:4 * n].rearrange("p (k c t) -> p k c t", k=2, c=2)
                    blk2 = ps[0:n, 5 + 2 * q, 0:4 * n].rearrange("p (k c t) -> p k c t", k=2, c=2)
                    TT(w["N"][0:n, q::2, 0:n], blk[:, 0], bc_mid(C("strict_l")[0:n, 0:n], 2), ALU.mult)
                    TT(Aak[0:n, q::2, 0:n], blk[:, 1], bc_mid(C("strict_u")[0:n, 0:n], 2), ALU.mult)
                    TT(w["BA"][0:n, q::2, P:P + n], blk2[:, 0], bc_mid(C("incl_u")[0:n, 0:n], 2), ALU.mult)
                    last = TT(KA[0:n, q::2, P:P + n], blk2[:, 1], bc_mid(C("incl_u")[0:n, 0:n], 2), ALU.mult)
                o(last, S["u_N"])
                for m, u in enumerate(U):
                    dve.wait_ge(S["u_NTs"], k0 + m + 1)
                    mark(TT(u["ED"][0:n, 0, :, 0:n], u["NT"][0:n, :, 0:n],
                                bc_mid(C("first_u")[0:n, 0:n], 4), ALU.mult), S["u_E0"])
                dve.wait_ge(S["u_P"], i + 1)
                mark(v.tensor_copy(w["QP"][0:n, :, 0:HD], ps[0:n, 4, 0:GW].rearrange("p (h t) -> p h t", h=4)), S["u_Pq"])
                for m in range(2):
                    dve.wait_ge(S["u_D0"], k0 + m + 1)
                dve.wait_ge(S["u_E0"], k0 + 2)
                for s, join in enumerate(JOINS):
                    for m, u in enumerate(U):
                        dve.wait_ge(S["u_T1p"], (k0 + 0) * 5 + 2 * s + m + 1)
                        mark(TT(u["T1"][0:n, :, 0:n], bank4(mixer_bank[m] + 2, n),
                                    bc_mid(C(join)[0:n, 0:n], 4), ALU.mult), S["u_T1"])
                    for m, u in enumerate(U):
                        b = mixer_bank[m]
                        dve.wait_ge(S["u_EDp"], (k0 + 0) * 5 + 2 * s + m + 1)
                        both = s < len(JOINS) - 1
                        for x in ((0, 1) if both else (0,)):
                            dst = u["ED"][0:n, x, :, 0:n]
                            last = TT(dst, dst, bank4(b + x, n), ALU.add)
                        mark(last, S["u_ED"])
                    dve.wait_ge(S["u_ED"], (k0 + 0) * 5 + 2 * s + 2)
                for m, u in enumerate(U):
                    b = mixer_bank[m]
                    dve.wait_ge(S["u_OUTs"], k0 + m + 1)
                    dec_ = (decG, decR)[m]
                    for h in range(HEADS):
                        for c in range(nch):
                            cc = slice((h % 2) * 256 + c * CHUNK, (h % 2) * 256 + (c + 1) * CHUNK)
                            last = STT(u["OUT"][TOP, h, c * CHUNK:(c + 1) * CHUNK], ident[TOP, TOP],
                                       dec_[TOP, h, 2 * i + c:2 * i + c + 1], ps[TOP, b + h // 2, cc], ALU.mult, ALU.add)
                    mark(last, S["u_OUTv"])
                for c in range(nch):
                    for m, u in enumerate(U):
                        ch = 2 * i + c
                        dve.wait_ge(S["u_Sp"], 2 * ch + m + 1)
                        dst = 4 if ch == 8 else (ch + 1) % 3
                        mark(v.tensor_copy(u["IS"][TOP, dst],
                                        ps[TOP, mixer_bank[m] + 2, c * GW:(c + 1) * GW].rearrange("p (h t) -> p h t", h=4)), S["u_S"])
            dve.wait_ge(S["act_stage"], AFTER["p_grs"])
            o(TT(mixT[:, 2:4], mixT[:, 2:4], ta, ALU.mult))
            o(STT(mixT[:, 2:4], mixT[:, 2:4], pp("gnorm"), gzs, ALU.mult, ALU.mult))
            dve.wait_ge(S["pe_stage"], AFTER["p_rsum"])
            mr = mixT[:, 4:6].rearrange("p c (u t) -> p (c u) t", u=2)
            o(STT(mr, ps[:, 4:8, 0:HALF], -1.0 / HD, mr, ALU.mult, ALU.add), S["vec_stage"])
            dve.wait_ge(S["act_stage"], AFTER["p_rrs"])
            o(TT(mixT[:, 4:6], mixT[:, 4:6], tb, ALU.mult))
            for c in range(2):
                o(TSC(mixT[:, 4 + c], mixT[:, 4 + c], pp("lnx_g", c), pp("lnx_b", c), ALU.mult, ALU.add))
            o(TT(mixT[:, 4:6], mixT[:, 4:6], bonus, ALU.add))
            o(TT(mixT[:, 4:6], mixT[:, 4:6], gate, ALU.mult), S["vec_stage"])
            dve.wait_ge(S["ld_xtok"], 16 * NT)
            dve.wait_ge(S["ld_lnp"], 64)

            def layer_norm(x, n, i, var, rstd, g, b, out, done):
                for k in range(2):
                    o(v.bn_stats(bst[0:n, 6 * k:6 * k + 6], x[:, k * 512:(k + 1) * 512]))
                o(v.bn_aggr(stat[0:n, 20:22], bst[0:n, 0:12]), S[var])
                dve.wait_ge(S[rstd], i + 1)
                o(TSC(x, x, stat[0:n, 20:21], stat[0:n, 24:25], ALU.subtract, ALU.mult))
                o(TT(x, x, lnp[0:n, g], ALU.mult))
                o(TT(out, x, lnp[0:n, b], ALU.add), S[done])

            for i, (t0, n) in enumerate(TILES):
                dve.wait_ge(S["o_y"], i + 1)
                x = xtok[0:n, i]
                b = 2 * (i % 2)
                o(STT(x, x, ALPHA, ps[0:n, b:b + 2, :].rearrange("p b t -> p (b t)"), ALU.mult, ALU.add), S["o_x"])
                layer_norm(x, n, i, "o_var", "o_rstd", 0, 1, x1[0:n, i], "o_x1")
            dve.wait_ge(S["ld_router"], 48)
            o(v.memset(logit, 0.0))
            dve.wait_ge(S["pe_stage"], AFTER["o_log"])
            lp = ps[:, 6, 0:NT * 20].rearrange("p (i r) -> p i r", r=20)
            bias = bc_mid(rt[:, 0:20], 4)
            TT(logit[:, 0:4], lp[:, 0:4], bias, ALU.add)
            o(TT(logit[LOW, 4], lp[LOW, 4], rt[LOW, 0:20], ALU.add))
            lg = logit[:, :, 0:4]
            at = 65

            def tmp(*shape):
                nonlocal at
                n = int(np.prod(shape))
                t = rt[:, at:at + n]
                at += n
                if len(shape) > 1:
                    names_ = "abc"[:len(shape)]
                    t = t.rearrange(f"p ({' '.join(names_)}) -> p {' '.join(names_)}", **dict(zip(names_[1:], shape[1:])))
                return t

            def bc4(x):
                return x.rearrange("p (i o) -> p i o", o=1).to_broadcast([P, NT, 4])

            def first_max(values, best, hit):
                o(TT(hit, values, bc4(best), ALU.is_equal))
                free = tmp(NT)
                o(TSC(free, hit[:, :, 0], -1.0, 1.0, ALU.mult, ALU.add))
                for k in range(1, 4):
                    o(TT(hit[:, :, k], hit[:, :, k], free, ALU.mult))
                    o(TT(free, free, hit[:, :, k], ALU.subtract))

            mg, hitg = tmp(NT), tmp(NT, 4)
            o(v.reduce_max(mg, lg, AX))
            eg = rt[:, 40:60].rearrange("p (i k) -> p i k", k=4)
            o(TT(eg, lg, bc4(mg), ALU.subtract), S["vec_stage"])
            first_max(lg, mg, hitg)
            le4 = tmp(NT, 4, 4)
            for g_ in range(4):
                o(TT(le4[:, :, g_], logit[:, :, 4 + 4 * g_:8 + 4 * g_], bc4(hitg[:, :, g_]), ALU.mult))
            le = tmp(NT, 4)
            o(TT(le, le4[:, :, 0], le4[:, :, 1], ALU.add))
            o(TT(le, le, le4[:, :, 2], ALU.add))
            o(TT(le, le, le4[:, :, 3], ALU.add))
            m1, hit1, m2, hit2, le2 = tmp(NT), tmp(NT, 4), tmp(NT), tmp(NT, 4), tmp(NT, 4)
            o(v.reduce_max(m1, le, AX))
            first_max(le, m1, hit1)
            o(STT(le2, hit1, NEG, le, ALU.mult, ALU.add))
            o(v.reduce_max(m2, le2, AX))
            first_max(le2, m2, hit2)
            d21 = rt[:, 60:65]
            o(TT(d21, m2, m1, ALU.subtract), S["vec_stage"])
            dve.wait_ge(S["o_eg"], 2)
            gs, w1, w2 = tmp(NT), tmp(NT), tmp(NT)
            o(v.reduce_sum(gs, eg, AX))
            o(STT(gs, d21, 1.0, gs, ALU.add, ALU.mult))
            o(v.reciprocal(w1, gs))
            o(TT(w2, w1, d21, ALU.mult))
            for k, (M, hit) in enumerate(((M1, hit1), (M2, hit2))):
                for g_ in range(4):
                    o(TT(M[:, :, 4 * g_:4 * g_ + 4], hit, bc4(hitg[:, :, g_]), ALU.mult))
                o(v.memset(M[TOP, 4], 0.0))
            o(TT(Mx, M1, M2, ALU.add), S["vec_stage"])
            o(TT(hit1, hit1, bc4(w1), ALU.mult))
            o(TT(hit2, hit2, bc4(w2), ALU.mult))
            o(TT(hit1, hit1, hit2, ALU.add))
            comb = tmp(NT, 4, 4)
            for g_ in range(4):
                o(TT(comb[:, :, g_], hit1, bc4(hitg[:, :, g_]), ALU.mult))
            comb = comb.rearrange("p i g e -> p i (g e)")
            dve.wait_ge(S["pe_stage"], AFTER["r_rank"])
            o(v.tensor_copy(rank, ps[:, 7, 0:NT * EXPERTS].rearrange("p (i e) -> p i e", e=EXPERTS)))
            o(v.reduce_max(stat[:, 31:32], ps[:, 7, NT * EXPERTS:(NT + 1) * EXPERTS], AX))
            o(TSC(pos, rank, float(CAP), FAR, ALU.is_ge, ALU.mult))
            o(TT(pos, pos, rank, ALU.add))
            o(TT(pos, pos, bc_mid(slot_c[:, 2 * P:], NT), ALU.add))
            for k, M in enumerate((M1, M2)):
                o(TT(M, M, pos, ALU.mult))
                o(v.reduce_sum(sl[:, k], M, AX))
            o(v.tensor_copy(idx[:, 2 * NT:], stat[:, 31:32]))
            o(v.tensor_copy(idx[:, 0:2 * NT], sl.rearrange("p k i -> p (k i)")), S["vec_stage"])
            for i, (t0, n) in enumerate(TILES):
                o(TSC(yacc[0:n, i], x1[0:n, i], ALPHA, None, ALU.mult))
            for e in range(EXPERTS + 2):
                if e < EXPERTS:
                    dve.wait_ge(S["x_t"], e + 1)
                    v.tensor_copy(xbT[e % 2][:, 4:8], ps[:, 1].rearrange("p (k t) -> p k t", k=4)).then_inc(S["x_tv"], 1)
                if e >= 2:
                    d = e - 2
                    dve.wait_ge(S["x_ht"], d + 1)
                    v.tensor_copy(hTs, ps[:, 4, 0:FF].rearrange("p (f t) -> p f t", f=2)).then_inc(S["x_hT"], 1)
                if 1 <= e <= EXPERTS:
                    dve.wait_ge(S["x_silu"], e)
                    if e >= 2:
                        dve.wait_ge(S["x_ht"], e - 1)
                    TT(hrow, hs, ps[:, 2 + (e - 1) % 2, FF:], ALU.mult).then_inc(S["x_h"], 1)
                if e >= 2:
                    dve.wait_ge(S["x_dn"], d + 1)
                    if d >= 2:
                        dve.wait_ge(st_yb[d % 2], 16 * (d // 2))
                    v.tensor_copy(yb[d % 2][:, 512:], ps[:, 6]).then_inc(S["x_yv"], 1)
            for i, (t0, n) in enumerate(TILES):
                dve.wait_ge(ld_got[i], 32)
                o(STT(yacc[0:n, i], got[0:n, i, 0], w1[0:n, i:i + 1], yacc[0:n, i], ALU.mult, ALU.add))
                o(STT(yacc[0:n, i], got[0:n, i, 1], w2[0:n, i:i + 1], yacc[0:n, i], ALU.mult, ALU.add), S["y_sum"])
            most = dve.value_load(idx[0:1, 2 * NT:], min_val=0, max_val=T)
            with dve.If(most > CAP):
                od, _ = own_order(dve, S["dense_step"])
                for i, (t0, n) in enumerate(TILES):
                    od(TSC(yacc[0:n, i], x1[0:n, i], ALPHA, None, ALU.mult))
                for e in range(EXPERTS):
                    for f in range(2):
                        dve.wait_ge(S["m_silu"], 2 * e + f + 1)
                        if e >= 1:
                            dve.wait_ge(S["m_dn"], NT * e)
                        mark(TT(halves(hT[:, f]), halves(hg[:, f]), two_banks(4 * f + 2, HALF), ALU.mult), S["m_h"])
                    for i, (t0, n) in enumerate(TILES):
                        dve.wait_ge(S["m_dn"], NT * e + i + 1)
                        b = 2 * (i % 2)
                        mark(STT(yacc[0:n, i], ps[0:n, b:b + 2, :].rearrange("p b t -> p (b t)"), comb[0:n, i, e:e + 1],
                                 yacc[0:n, i], ALU.mult, ALU.add), S["m_acc"])
                dve.wait_ge(S["m_acc"], NT * EXPERTS)
            for i, (t0, n) in enumerate(TILES):
                layer_norm(yacc[0:n, i], n, i, "f_var", "f_rstd", 2, 3, x1[0:n, i], "f_y")

        @block.tensor
        def _(pe):
            mm, tr = nc.tensor.matmul, nc.tensor.transpose
            pe.wait_ge(S["ld_x"], 16)
            for j in range(NCH):
                pe.wait_ge(ld_w[j % RING], 16 * (j // RING + 1))
                if j >= RING:
                    pe.wait_ge(S["evac_act"], j - RING + 1)
                    pe.wait_ge(S["evac_vec"], j - RING + 1)
                for h in range(2):
                    for k in range(KD):
                        last = mm(ps[:, 2 * (j % RING) + h, 0:HALF], wring[j % RING][:, k], xT[:, k, h * HALF:(h + 1) * HALF],
                                  start=(k == 0), stop=(k == KD - 1))
                last.then_inc(S["proj_done"], 1)
            pe.wait_ge(S["evac_act"], NCH)
            pe.wait_ge(S["evac_vec"], NCH)
            pe.wait_ge(S["ld_const"], 32)
            for i, (t0, n) in enumerate(TILES):
                if i >= 2:
                    pe.wait_ge(S["vt_act"], i - 1)
                c0 = tile_cols(i)
                for pair in range(2):
                    last = tr(ps[0:n, 6 + i % 2, pair * P:(pair + 1) * P], hb[:, DV + pair, c0:c0 + n], ident)
                last.then_inc(S["vt_pe"], 1)
            units = [(i, h) for i in range(NT) for h in range(HEADS)]

            def scores(u):
                i, h = units[u]
                n, c0, b = TILES[i][1], tile_cols(i), 3 * (u % 2)
                pair, pb = HEADP[h]
                r = slice(pb, pb + HD)
                if u >= 2:
                    pe.wait_ge(S["o_act"], u - 1)
                if i < 4:
                    segs = [(hb[r, DK + pair, PAD:PAD + P * (i + 1)], Fp[:, 0:P * (i + 1)])]
                else:
                    segs = [(kcT[r, pair, 0:512], Fs[:, 0:512]), (kcT[r, pair, 512:PAST], Fs[:, 512:PAST]),
                            (hb[r, DK + pair, SCOL:SCOL + TS], Fs[:, PAST:])]
                for k, (keys, f) in enumerate(segs):
                    nk = keys.shape[1]
                    mm(ps[0:n, b + k, 0:nk], hb[r, DQ + pair, c0:c0 + n], keys, start=True, stop=False)
                    last = mm(ps[0:n, b + k, 0:nk], sel[:, SEL_F + h, 0:n], f, start=False, stop=True)
                last.then_inc(S["s_done"], 1)

            pe.wait_ge(S["vec_stage"], AFTER["rows_done"])
            pe.wait_ge(S["ld_cache"], 48)
            pe.wait_ge(S["vt_act"], NT)
            scores(0)
            for u, (i, h) in enumerate(units):
                n, b = TILES[i][1], 3 * (u % 2)
                pair, pb = HEADP[h]
                if u + 1 < len(units):
                    scores(u + 1)
                pe.wait_ge(S["p_ready"], u + 1)
                if u >= 2:
                    pe.wait_ge(S["pt_copied"], u - 1)
                s = sc[u % 2]
                if i < 4:
                    for k in range(i + 1):
                        last = tr(ps[:, 6 + u % 2, k * P:(k + 1) * P], s[:, k * P:(k + 1) * P], ident)
                else:
                    for k in range(8):
                        tr(ps[:, 6 + u % 2, k * n:(k + 1) * n], s[0:n, k * P:(k + 1) * P], ident[0:n, 0:n])
                    last = tr(ps[LOW, b + 2, 64:128], s[0:n, PAST:], ident[0:n, 0:n])
                last.then_inc(S["t_done"], 1)
                pe.wait_ge(S["pt_copied"], u + 1)
                hs = slice(h * HD, (h + 1) * HD)
                out = ps[pb:pb + HD, b, 0:n]
                if i < 4:
                    for k in range(i + 1):
                        last = mm(out, vtok[:, k, hs], pT[:, u % 2, k * P:(k + 1) * P], start=(k == 0), stop=(k == i))
                else:
                    for k in range(8):
                        mm(out, vc[:, k, hs], pT[:, u % 2, k * n:(k + 1) * n], start=(k == 0), stop=False)
                    last = mm(out, vtok[LOW, 4, hs], pT[LOW, u % 2, 512:T], start=False, stop=True)
                last.then_inc(S["pv_done"], 1)
            pe.wait_ge(S["o_act"], len(units))
            pe.wait_ge(S["vec_stage"], AFTER["c_taps"])
            for n, (dst, src) in enumerate([(ps[:, 0, :], (0, TP)), (ps[:, 1, 0:TS], (CPAD + TP, TS))]):
                for c in range(2):
                    last = mm(dst, C("mean_ones"), cacc[:, c, src[0]:src[0] + src[1]], start=(c == 0), stop=(c == 1))
            last.then_inc(S["pe_stage"], 1)
            pe.wait_ge(S["act_stage"], AFTER["c_sq"])
            for h in range(2):
                for c in range(2):
                    last = mm(ps[:, 2 + h, 0:HALF], C("mean_ones"), csq[:, c, h * HALF:(h + 1) * HALF],
                              start=(c == 0), stop=(c == 1))
            last.then_inc(S["pe_stage"], 1)

            def head_sums(b, src, nc_):
                for c in range(nc_):
                    for h in range(2):
                        last = mm(ps[:, b + 2 * c + h, 0:HALF], C("head_ones"), src[:, c, h * HALF:(h + 1) * HALF],
                                  start=True, stop=True)
                return last

            pe.wait_ge(S["act_stage"], AFTER["c_rstd"])
            pe.wait_ge(S["vec_stage"], AFTER["c_cen"])
            pe.wait_ge(S["act_stage"], AFTER["g_sq"])
            head_sums(0, gsq, 4).then_inc(S["pe_stage"], 1)
            pe.wait_ge(S["act_stage"], AFTER["g_rs"])
            for p_ in range(2):
                for h in range(2):
                    mm(ps[:, 2 * p_ + h, 0:HALF], sel[ROWS, SEL_PAIR + p_, :], rowG[ROWS, h * HALF:(h + 1) * HALF],
                       start=True, stop=True)
            for h in range(HEADS):
                last = mm(ps[TOP, 4, h * 9:(h + 1) * 9], sel[ROWS, SEL_G + h, 0:64], rowG[ROWS, CHUNK - 1::CHUNK],
                          start=True, stop=True)
            last.then_inc(S["pe_stage"], 1)
            for i, (t0, n) in enumerate(TILES):
                for k, rows in enumerate((rowy, rowG, rowGL)):
                    at = (3 * i + k) * 12
                    last = mm(ps[0:n, 5, at:at + 12], rows[ROWS, t0:t0 + n], ident[ROWS, ROWS], start=True, stop=True)
            last.then_inc(S["pe_stage"], 1)
            pe.wait_ge(S["act_stage"], AFTER["w_lora"])
            pe.wait_ge(S["act_stage"], AFTER["g_eg"])
            pe.wait_ge(S["vec_stage"], AFTER["g_tok"])

            def lora_product(b, rows):
                for c in range(2):
                    for h in range(2):
                        last = mm(ps[:, b + 2 * c + h, 0:HALF], lora[rows, c * P:(c + 1) * P],
                                  xm[rows, 6, h * HALF:(h + 1) * HALF], start=True, stop=True)
                return last

            lora_product(0, slice(0, 16))
            lora_product(4, slice(32, 48)).then_inc(S["pe_stage"], 1)
            pe.wait_ge(S["act_stage"], AFTER["w_sg"])
            lora_product(0, slice(64, 96)).then_inc(S["pe_stage"], 1)
            pe.wait_ge(S["act_stage"], AFTER["w_sq"])
            head_sums(4, tb, 2).then_inc(S["pe_stage"], 1)
            pe.wait_ge(S["act_stage"], AFTER["w_krs"])
            pe.wait_ge(S["vec_stage"], AFTER["w_bon"])
            head_sums(4, tb, 2).then_inc(S["pe_stage"], 1)
            pe.wait_ge(S["vec_stage"], AFTER["w_prep"])
            pe.wait_ge(S["act_stage"], AFTER["w_gate"])
            pe.wait_ge(S["vec_stage"], AFTER["g_prep"])
            g, w = U
            for i, (t0, n) in enumerate(TILES):
                k0 = 2 * i
                nch = n // CHUNK
                ts = slice(t0, t0 + n)
                if i >= 1:
                    pe.wait_ge(S["u_S"], 4 * i)
                    pe.wait_ge(S["u_O"], 2 * i)
                for p_ in range(2):
                    tr(ps[0:n, 0, p_ * P:(p_ + 1) * P], gk[:, p_, ts], ident)
                    tr(ps[0:n, 0, GW + p_ * P:GW + (p_ + 1) * P], gv[:, p_, ts], ident)
                for h in range(HEADS):
                    last = mm(ps[0:n, 1, h * n:(h + 1) * n], sel[ROWS, SEL_G + h, 0:n], rowG[ROWS, ts], start=True, stop=True)
                last.then_inc(S["u_tr"], 1)
                for h, (pair, pb) in enumerate(HEADP):
                    r = slice(pb, pb + HD)
                    kch = gk[r, pair, ts]
                    b = 2 + h % 2
                    mm(ps[0:n, b, pair * n:(pair + 1) * n], kch, kch, start=True, stop=True)
                    last = mm(ps[0:n, b, (2 + pair) * n:(3 + pair) * n], kch, gq[r, pair, ts], start=True, stop=True)
                last.then_inc(S["u_A"], 1)
                for p_ in range(2):
                    for b, q, src in ((4, 0, Au), (4, 1, xmv), (5, 0, Bb), (5, 1, Kb)):
                        last = tr(ps[0:n, b, q * GW + p_ * P:q * GW + (p_ + 1) * P], src[:, p_, ts], ident)
                last.then_inc(S["u_tr"], 1)
                pe.wait_ge(S["u_tok"], i + 1)
                for h in (1, 3, 0, 2):
                    pair, pb = HEADP[h]
                    r = slice(pb, pb + HD)
                    b = 4 + 2 * (h % 2)
                    for b_, q, lhs, rhs in ((b, 0, ac, bc), (b, 2, kc, ac), (b + 1, 0, bc, rc), (b + 1, 2, kc, rc)):
                        last = mm(ps[0:n, b_, (q + pair) * n:(q + pair + 1) * n], lhs[r, pair, ts], rhs[r, pair, ts],
                                  start=True, stop=True)
                last.then_inc(S["u_A"], 1)
                for m, u in enumerate(U):
                    pe.wait_ge(S["u_diag"], k0 + m + 1)
                    for h in range(HEADS):
                        last = tr(ps[0:n, mixer_bank[m] + 1, h * n:(h + 1) * n], u["N"][0:n, h, 0:n], ident[0:n, 0:n])
                    last.then_inc(S["u_NTp"], 1)
                for h in range(HEADS):
                    last = mm(ps[0:n, 4, h * HD:(h + 1) * HD], Aak[0:n, h, 0:n], V[0:n, h], start=True, stop=True)
                last.then_inc(S["u_P"], 1)
                for m in range(2):
                    pe.wait_ge(S["u_NTs"], k0 + m + 1)
                    pe.wait_ge(S["u_D0"], k0 + m + 1)
                    pe.wait_ge(S["u_E0"], k0 + m + 1)
                pe.wait_ge(S["u_Pq"], i + 1)
                for s in range(len(JOINS)):
                    for m, u in enumerate(U):
                        if s:
                            pe.wait_ge(S["u_ED"], k0 * 5 + 2 * (s - 1) + m + 1)
                        for h in range(HEADS):
                            last = mm(ps[0:n, mixer_bank[m] + 2, h * n:(h + 1) * n], u["NT"][0:n, h, 0:n],
                                      u["ED"][0:n, 1, h, 0:n], start=True, stop=True)
                        last.then_inc(S["u_T1p"], 1)
                    for m, u in enumerate(U):
                        b = mixer_bank[m]
                        pe.wait_ge(S["u_T1"], k0 * 5 + 2 * s + m + 1)
                        E_, D_ = u["ED"][0:n, 0], u["ED"][0:n, 1]
                        for h in range(HEADS):
                            t1 = u["T1"][0:n, h, 0:n]
                            last = mm(ps[0:n, b, h * n:(h + 1) * n], t1, E_[:, h, 0:n], start=True, stop=True)
                            if s < len(JOINS) - 1:
                                last = mm(ps[0:n, b + 1, h * n:(h + 1) * n], E_[:, h, 0:n], t1, start=True, stop=True)
                        last.then_inc(S["u_EDp"], 1)
                for m, u in enumerate(U):
                    pe.wait_ge(S["u_ED"], k0 * 5 + 2 * 4 + m + 1)
                    for h in range(HEADS):
                        last = mm(ps[0:n, mixer_bank[m] + 3, h * P:(h + 1) * P], u["ED"][0:n, 0, h, 0:n], u["QP"][0:n, h],
                                  start=True, stop=True)
                    last.then_inc(S["u_TPQp"], 1)
                for m, u in enumerate(U):
                    b = mixer_bank[m]
                    pe.wait_ge(S["u_TPQ"], k0 + m + 1)
                    R_ = (gR, Ru)[m]
                    for h, (pair, pb) in enumerate(HEADP):
                        at = (h % 2) * 256
                        mm(ps[:, b + h // 2, at:at + P + n], u["TPQ"][0:n, h], u["BA"][0:n, h, 0:P + n], start=True, stop=False,
                           skip_group_check=True)
                        if m == 1:
                            mm(ps[LOW, b + h // 2, at:at + P + n], V[0:n, h], KA[0:n, h, 0:P + n], start=False, stop=False,
                               skip_group_check=True)
                        last = mm(ps[:, b + h // 2, at + P:at + P + n], C(f"shift{h % 2}"), R_[:, pair, ts],
                                  start=False, stop=True, skip_group_check=True)
                    last.then_inc(S["u_OUTp"], 1)
                for c in range(nch):
                    ch = 2 * i + c
                    slot = 3 if ch == 8 else ch % 3
                    for m, u in enumerate(U):
                        b = mixer_bank[m]
                        if c == 0:
                            pe.wait_ge(S["u_OUTs"], k0 + m + 1)
                            pe.wait_ge(S["u_OUTv"], k0 + m + 1)
                        if ch:
                            pe.wait_ge(S["u_S"], 2 * (ch - 1) + m + 1)
                        for h in range(HEADS):
                            last = mm(ps[TOP, b + 2, c * GW + h * HD:c * GW + (h + 1) * HD], u["OUT"][:, h, c * CHUNK:(c + 1) * CHUNK],
                                      u["IS"][:, slot, h], start=True, stop=True)
                        last.then_inc(S["u_Sp"], 1)
                        for h, (pair, pb) in enumerate(HEADP):
                            last = mm(ps[pb:pb + HD, b + 3, pair * n + c * CHUNK:pair * n + (c + 1) * CHUNK], u["IS"][:, slot, h],
                                      u["OUT"][:, h, P + c * CHUNK:P + (c + 1) * CHUNK], start=True, stop=True)
                        if c == nch - 1:
                            last.then_inc(S["u_Op"], 1)
            pe.wait_ge(S["u_S"], 18)
            pe.wait_ge(S["u_O"], 2 * NT)
            head_sums(4, mixT[:, 4:6], 2).then_inc(S["pe_stage"], 1)
            pe.wait_ge(S["act_stage"], AFTER["p_gsq"])
            head_sums(0, ta, 2).then_inc(S["pe_stage"], 1)
            pe.wait_ge(S["act_stage"], AFTER["p_grs"])
            pe.wait_ge(S["act_stage"], AFTER["p_rsq"])
            head_sums(0, tb, 2).then_inc(S["pe_stage"], 1)
            pe.wait_ge(S["vec_stage"], AFTER["p_done"])
            pe.wait_ge(S["ld_wout"], 16)

            def x1_transposes(i):
                t0, n = TILES[i]
                pe.wait_ge(S["o_x1"], i + 1)
                if i:
                    pe.wait_ge(S["o_x1T"], i)
                for k in range(KD):
                    last = tr(ps[:, 4 + k // 4, (k % 4) * n:(k % 4 + 1) * n], x1[0:n, i, k * P:(k + 1) * P], ident[0:n, 0:n])
                last.then_inc(S["o_x1t"], 1)

            for i, (t0, n) in enumerate(TILES):
                if i >= 2:
                    pe.wait_ge(S["o_x"], i - 1)
                for q in range(2):
                    for k in range(KD):
                        last = mm(ps[0:n, 2 * (i % 2) + q, :], mixT[:, k, t0:t0 + n], wout[:, k, q * 512:(q + 1) * 512],
                                  start=(k == 0), stop=(k == KD - 1))
                last.then_inc(S["o_y"], 1)
                if i:
                    x1_transposes(i - 1)
            x1_transposes(NT - 1)
            pe.wait_ge(S["o_x1T"], NT)
            pe.wait_ge(S["ld_router"], 48)
            for i, (t0, n) in enumerate(TILES):
                for k in range(KD):
                    last = mm(ps[0:n, 6, i * 20:(i + 1) * 20], x1T[:, k, t0:t0 + n], wr[:, k], start=(k == 0), stop=(k == KD - 1))
            last.then_inc(S["pe_stage"], 1)
            pe.wait_ge(S["vec_stage"], AFTER["r_mask"])
            pe.wait_ge(S["ld_router"], 48)
            before, ones = slot_c[:, 0:P], slot_c[:, P:2 * P]
            for i in range(NT + 1):
                at = ps[:, 7, i * EXPERTS:(i + 1) * EXPERTS]
                for j in range(min(i + 1, NT)):
                    last = mm(at, before if j == i else ones, Mx[:, j], start=(j == 0), stop=(j == min(i, NT - 1)))
            last.then_inc(S["pe_stage"], 1)
            pe.wait_ge(S["vec_stage"], AFTER["r_slots"])
            pe.wait_ge(S["o_x"], NT)

            def block_in(e):
                pe.wait_ge(ld_xb[e % 2], 16 * (e // 2 + 1))
                if e:
                    pe.wait_ge(S["x_ta"], e)
                    pe.wait_ge(S["x_tv"], e)
                for k in range(KD):
                    last = tr(ps[:, k // 4, (k % 4) * P:(k % 4 + 1) * P], xb[e % 2][:, k * P:(k + 1) * P], ident)
                last.then_inc(S["x_t"], 1)

            block_in(0)
            for e in range(EXPERTS + 1):
                if e + 1 < EXPERTS:
                    block_in(e + 1)
                if e:
                    pe.wait_ge(S["x_h"], e)
                    if e >= 2:
                        pe.wait_ge(S["x_hT"], e - 1)
                    for f in range(2):
                        last = tr(ps[:, 4, f * P:(f + 1) * P], hrow[:, f * P:(f + 1) * P], ident)
                    last.then_inc(S["x_ht"], 1)
                if e < EXPERTS:
                    pe.wait_ge(ld_e[e % 2], 16 * (e // 2 + 1))
                    pe.wait_ge(S["x_ta"], e + 1)
                    pe.wait_ge(S["x_tv"], e + 1)
                    if e >= 2:
                        pe.wait_ge(S["x_h"], e - 1)
                    for k in range(KD):
                        last = mm(ps[:, 2 + e % 2], xbT[e % 2][:, k], wgu[e % 2][:, k], start=(k == 0), stop=(k == KD - 1))
                    last.then_inc(S["x_gu"], 1)
                if e:
                    pe.wait_ge(S["x_hT"], e)
                    if e >= 2:
                        pe.wait_ge(S["x_ya"], e - 1)
                        pe.wait_ge(S["x_yv"], e - 1)
                    pe.wait_ge(ld_f[(e - 1) % 2], 16 * ((e - 1) // 2 + 1))
                    for q in range(2):
                        for f in range(2):
                            last = mm(ps[:, 5 + q], hTs[:, f], wdn[(e - 1) % 2][:, f, q * 512:(q + 1) * 512],
                                      start=(f == 0), stop=(f == 1))
                    last.then_inc(S["x_dn"], 1)
            pe.wait_ge(S["x_ya"], EXPERTS)
            pe.wait_ge(S["x_yv"], EXPERTS)
            most = pe.value_load(idx[0:1, 2 * NT:], min_val=0, max_val=T)
            with pe.If(most > CAP):
                for e in range(EXPERTS):
                    pe.wait_ge(ld_d[e % 2], 32 * (e // 2 + 1))
                    if e:
                        pe.wait_ge(S["m_acc"], NT * e)
                    for f in range(2):
                        for w_ in range(2):
                            for h in range(2):
                                for k in range(KD):
                                    last = mm(ps[:, 4 * f + 2 * w_ + h, 0:HALF], wgu[e % 2][:, k, w_ * FF + f * P:w_ * FF + (f + 1) * P],
                                              x1T[:, k, h * HALF:(h + 1) * HALF], start=(k == 0), stop=(k == KD - 1))
                        last.then_inc(S["m_gu"], 1)
                    pe.wait_ge(S["m_h"], 2 * e + 2)
                    for i, (t0, n) in enumerate(TILES):
                        if i >= 2:
                            pe.wait_ge(S["m_acc"], NT * e + i - 1)
                        for q in range(2):
                            for f in range(2):
                                last = mm(ps[0:n, 2 * (i % 2) + q, :], hT[:, f, t0:t0 + n], wdn[e % 2][:, f, q * 512:(q + 1) * 512],
                                          start=(f == 0), stop=(f == 1))
                        last.then_inc(S["m_dn"], 1)


OUTS = {"o_y": (T, D), "o_gconv": (P, 2, 6, PAD), "o_shift": (P, 2, 7), "o_kv": (P, 4, T), "o_logf": (HEADS, T),
        "o_conv": (P, 2, 2, CPAD), "o_state": (2, 2, HD, HEADS, HD)}


def square_constants():
    i, j = np.arange(P)[:, None], np.arange(P)[None, :]
    same = i // CHUNK == j // CHUNK
    lower = same & (i > j)
    c = {"ident": i == j, "strict_l": lower, "strict_u": lower.T, "incl_u": same & (i <= j),
         "neg_strict_l": np.where(lower, 0, NEG), "neg_incl_u": np.where(same & (i <= j), 0, NEG)}
    for b in (1, 2, 4, 8, 16, 32):
        join = (i // (2 * b) == j // (2 * b)) & (i // b % 2 == 1) & (j // b % 2 == 0)
        if b == 1:
            c["first_l"], c["first_u"] = join | (i == j), join.T | (i == j)
        else:
            c[f"join{b}"] = join
    c["neg_causal"] = np.where(j <= i, 0, NEG)
    c["head_ones"] = same
    c["mean_ones"] = np.full((P, P), 1.0 / GW)
    for q in range(2):
        c[f"shift{q}"] = (j >= HD) & (i == j - HD + q * HD)
    return np.stack([np.asarray(c[n], np.float32) for n in CONST], 1)


def row_selectors():
    s = np.zeros((P, NSEL, P), np.float32)
    for h in range(HEADS):
        s[96 + h, SEL_G + h, :] = 1.0
        s[104 + h, SEL_F + h, :] = -float(HD) ** 0.5
        s[96 + h, SEL_PAIR + h // 2, (h % 2) * HD:(h % 2 + 1) * HD] = 1.0
    return s


def layout(x):
    g = {k: np.asarray(v) for k, v in x.items()}
    z = np.zeros
    f32 = np.float32
    o = {}
    xx = np.concatenate([g["x_prompt"][0], g["x_sample"][0]], 0)
    o["x_tok"] = xx
    o["xT"] = xx.T.reshape(KD, P, T).transpose(1, 0, 2)
    w = g["w_in"][0]
    nA, nB = 2 * GW, 4 * GW + 2 * HEADS
    nC = 3 * GW + 64
    A, B, Cc, Dd = w[:, :nA], w[:, nA:nA + nB], w[:, nA + nB:nA + nB + nC], w[:, nA + nB + nC:]
    sm = z((D, P), f32)
    sm[:, 0:16], sm[:, 32:48], sm[:, 64:96] = Cc[:, 768:784], Cc[:, 784:800], Cc[:, 800:832]
    sm[:, 96:104], sm[:, 104:108] = B[:, 1024:1032], Dd[:, 768:772]
    cols = np.concatenate([sm, B[:, :1024], Cc[:, :768], Dd[:, :768], A], 1)
    o["w_in"] = cols.reshape(KD, P, NCH, P).transpose(2, 1, 0, 3)
    pads = z((P, NCH, PAD), f32)
    pads[:, BQ:BQ + 6] = g["state_gdn_conv"][0, 0].T.reshape(6, P, PAD).transpose(1, 0, 2)
    sh = g["state_rwkv_shift"][0, 0]
    pads[:, CR:CR + 6, 2] = sh[:768].reshape(6, P).T
    pads[0:16, 0, 2], pads[32:48, 0, 2], pads[64:96, 0, 2] = sh[768:784], sh[784:800], sh[800:832]
    o["pads"] = pads
    o["conv_state"] = g["state_conv"][0, 0].T.reshape(2, P, CPAD).transpose(1, 0, 2)
    o["s_gdn"] = g["state_gdn"][0, 0].transpose(1, 0, 2)
    o["s_rwkv"] = g["state_rwkv"][0, 0].transpose(2, 0, 1)
    o["k_cache"] = g["cache_fox_k"][0, 0].transpose(1, 2, 0).reshape(2, P, PAST).transpose(1, 0, 2)
    o["v_cache"] = g["cache_fox_v"][0, 0].reshape(8, P, GW).transpose(1, 0, 2)
    fc = z((12, PAST), f32)
    fc[8:12] = g["cache_fox_logf"][0, 0].T
    o["f_cache"] = fc
    par = z((P, NPC), f32)

    def put(name, arr):
        arr = np.asarray(arr, f32)
        if arr.ndim == 1:
            arr = arr[:, None]
        k = arr.shape[1]
        a3 = arr.reshape(-1, P, k).transpose(1, 0, 2).reshape(P, -1)
        par[:, PCOL[name]:PCOL[name] + a3.shape[1]] = a3

    put("conv_w", g["conv_w"][0].T)
    put("conv_b", g["conv_b"][0]), put("conv_g", g["conv_ln_g"][0]), put("conv_lb", g["conv_ln_b"][0])
    put("gconv_w", g["gdn_conv_w"][0].T)
    put("gnorm", np.concatenate([g["gdn_norm_w"][0]] * 2))
    mu = g["rwkv_mu"][0]
    put("mu", mu[:768])
    c = PCOL["mu_s"]
    par[0:16, c], par[32:48, c], par[64:96, c] = mu[768:784], mu[784:800], mu[800:832]
    for n, k in (("w0", "rwkv_w0"), ("a0", "rwkv_a0"), ("k_k", "rwkv_k_k"), ("k_a", "rwkv_k_a"),
                 ("lnx_g", "rwkv_lnx_g"), ("lnx_b", "rwkv_lnx_b")):
        put(n, g[k][0])
    put("r_k", g["rwkv_r_k"][0].reshape(-1))
    par[96:100, PCOL["row_bias"]], par[104:108, PCOL["row_bias"]] = g["gdn_dt_bias"][0], g["fox_b_f"][0]
    par[96:100, PCOL["row_alog"]] = g["gdn_a_log"][0]
    par[96:100, PCOL["row_sign"]], par[100:108, PCOL["row_sign"]] = 1.0, -1.0
    o["params"] = par
    lo = z((P, GW), f32)
    lo[0:16], lo[32:48], lo[64:96] = g["rwkv_w_up"][0], g["rwkv_a_up"][0], g["rwkv_g_up"][0]
    o["lora"] = lo
    cm = np.ones((P, T), f32)
    cm[:, ::CHUNK] = 0
    o["ch_mask"] = cm
    o["consts"], o["sel"] = square_constants(), row_selectors()
    o["w_out"] = g["w_out"][0].reshape(8, P, D).transpose(1, 0, 2)
    o["ln"] = np.stack([g[k][0] for k in ("ln1_g", "ln1_b", "ln2_g", "ln2_b")])
    ij = np.arange(P)
    o["slot_c"] = np.concatenate([(ij[:, None] < ij[None, :]).astype(f32), np.ones((P, P), f32),
                                  np.tile(np.arange(EXPERTS, dtype=f32) * CAP, (P, 1))], 1)
    o["w_router"] = np.concatenate([g["router_g_w"][0], g["router_e_w"][0]], 1).reshape(KD, P, 20).transpose(1, 0, 2)
    o["b_router"] = np.concatenate([g["router_g_b"][0], g["router_e_b"][0]])[None]
    gu = np.concatenate([g["exp_w_gate"][0], g["exp_w_up"][0]], 2)
    o["w_gu"] = gu.reshape(EXPERTS, KD, P, 2 * FF).transpose(0, 2, 1, 3)
    o["w_dn"] = g["exp_w_down"][0].reshape(EXPERTS, 2, P, D).transpose(0, 2, 1, 3)
    return {k: np.ascontiguousarray(v) for k, v in o.items()}


def restore(r):
    y = r["o_y"]
    out = [y[None, :TP], y[None, TP:]]
    for k in range(2):
        t = slice(0, TP) if k == 0 else slice(TP, T)
        n = TP if k == 0 else TS
        sh = r["o_shift"][:, k]
        shift = np.concatenate([sh[:, :6].T.reshape(-1), sh[0:16, 6], sh[32:48, 6], sh[64:96, 6]])
        kv = [r["o_kv"][:, c:c + 2, t].transpose(2, 1, 0).reshape(1, 1, n, HEADS, HD) for c in (0, 2)]
        out += [r["o_conv"][:, k].transpose(2, 1, 0).reshape(1, 1, CPAD, GW),
                r["o_gconv"][:, k].transpose(2, 1, 0).reshape(1, 1, PAD, 3 * GW),
                r["o_state"][0, k].transpose(1, 0, 2)[None, None],
                shift[None, None],
                r["o_state"][1, k].transpose(1, 2, 0)[None, None],
                kv[0], kv[1], r["o_logf"][:, t].T[None, None]]
    return tuple(np.ascontiguousarray(v) for v in out)


def kernel(**inputs):
    import concourse.bacc as _bacc
    from concourse.bass_utils import run_bass_kernel_spmd as _run

    nc = _bacc.Bacc("TRN2", target_bir_lowering=False, num_devices=1)
    arrays = {f"in_{k}": v for k, v in layout(inputs).items()}
    a = {k[3:]: nc.dram_tensor(k, v.shape, F32, kind="ExternalInput").ap() for k, v in arrays.items()}
    a.update({k: nc.dram_tensor(k, s, F32, kind="ExternalOutput").ap() for k, s in OUTS.items()})
    step_kernel(nc, a)
    r = _run(nc, [arrays], core_ids=[0])
    return restore(r.results[0])
```

```python
from contextlib import ExitStack

import numpy as np

import concourse.bass as bass
from concourse import mybir

F32 = mybir.dt.float32
ALU = mybir.AluOpType
ACT = mybir.ActivationFunctionType
AX = mybir.AxisListType.X

P = 128
D = 1024
KD = D // P
TP, TS = 512, 64
T = TP + TS
HALF = T // 2
HEADS, HD = 4, 64
GW = HEADS * HD
CHUNK = 64
PAST = 1024
CW = 31
CPAD = CW - 1
GTAPS = 4
PAD = GTAPS - 1
HW = 2 * PAD + T
SCOL = 2 * PAD + TP
TILES = [(0, 128), (128, 128), (256, 128), (384, 128), (512, 64)]
PIECES = [(0, TP, PAD), (TP, TS, SCOL)]
NT = len(TILES)
EXPERTS, FF = 16, 256
CAP = 128
FAR = 1e6
GROUPS = 4
RT = 1000
DECAY = float(np.exp(-0.5))
ALPHA = 2.0 ** 0.25
LN_EPS, GN_EPS, RMS_EPS, L2_EPS = 1e-5, 64e-5, 1e-6, 1e-6
NEG = -1e30

SMALL, VAL, GATE, BQ, BK, BV, BZ, CR, CK, CV, DQ, DK, DV = 0, 1, 3, 5, 7, 9, 11, 13, 15, 17, 19, 21, 23
NCH = 25
RING = 4
ROWS = slice(96, 108)
TOP, LOW = slice(64, 128), slice(0, 64)

CONST = ["ident", "strict_l", "strict_u", "incl_u", "neg_strict_l", "neg_incl_u", "first_l", "first_u",
         "join2", "join4", "join8", "join16", "join32", "neg_causal", "head_ones", "mean_ones", "shift0", "shift1"]
SEL_G, SEL_F, SEL_PAIR, NSEL = 0, 4, 8, 10
PARAMS = [("conv_w", 2 * CW), ("conv_b", 2), ("conv_g", 2), ("conv_lb", 2), ("gconv_w", 6 * GTAPS),
          ("gnorm", 1), ("mu", 6), ("mu_s", 1), ("w0", 2), ("a0", 2), ("k_k", 2), ("k_a", 2), ("r_k", 2),
          ("lnx_g", 2), ("lnx_b", 2), ("row_bias", 1), ("row_alog", 1), ("row_sign", 1)]
PCOL, NPC = {}, 0
for _n, _k in PARAMS:
    PCOL[_n] = NPC
    NPC += _k


STAGES = {
    "pe": """g_decp g_tokp g_pairs c_mean c_var g_sumq g_sumk w_w w_a w_gatep w_ksum w_bonp
             p_gsum0 p_rsum0 p_rvar0 p_gsum1 p_rsum1 p_rvar1 o_log r_rank""",
    "act": """rows_log c_gate g_dec g_texp g_eg c_sq c_rstd c_sig g_sig g_sq g_zsig g_rsq w_lora g_rs
             w_sg w_asig w_gate w_e w_e5 w_sq w_krs p_gsq0 p_grs0 p_rsq0 p_rrs0
             p_gsq1 p_grs1 p_rsq1 p_rrs1""",
    "vec": """rows_neg rows_done g_tok c_glu g_prep c_taps g_taps c_cen c_lin c_done g_silu
             w_small g_norm w_mix w_cum w_cprev w_k1 w_bon w_prep p_rcen0 p_done0 p_rcen1 p_done1 o_lg o_w2
             r_mask r_slots""",
}
AFTER = {n: i + 1 for v in STAGES.values() for i, n in enumerate(v.split())}


def own_order(engine, own):
    count = {}

    def mark(instruction, sem=None):
        sem = own if sem is None else sem
        count[sem.name] = count.get(sem.name, 0) + 1
        instruction.then_inc(sem, 1)

    def o(instruction, sem=None):
        mark(instruction, sem)
        sem = own if sem is None else sem
        engine.wait_ge(sem, count[sem.name])

    return o, mark


def step_kernel(nc, a):
    ctx = ExitStack()
    with ctx:
        def sb(name, words):
            return ctx.enter_context(nc.sbuf_tensor(name, [P, words], F32))

        def sem(name):
            return ctx.enter_context(nc.semaphore(name))

        def carve(region, at, *shape):
            n = int(np.prod(shape))
            v = region[:, at:at + n]
            if len(shape) > 1:
                names = "abcd"[:len(shape)]
                v = v.rearrange(f"p ({' '.join(names)}) -> p {' '.join(names)}",
                                **dict(zip(names[1:], shape[1:])))
            assert at + n <= region.shape[1], (region.name, at + n)
            return v, at + n

        def carve_all(region, at, *shapes):
            out = []
            for shape in shapes:
                v, at = carve(region, at, *shape)
                out.append(v)
            return out + [at]

        rH = sb("r_proj", NCH * HW)
        rX = sb("r_x", KD * T + RING * KD * P)
        rU = sb("r_unit", 14600)
        rG = sb("r_gdn", 10 * T)
        rM = sb("mix", 8 * T)
        mixT, _ = carve(rM, 0, 8, T)
        consts, _ = carve(sb("consts", len(CONST) * P), 0, len(CONST), P)
        sel, _ = carve(sb("sel", NSEL * P), 0, NSEL, P)
        par = sb("par", NPC)
        lora = sb("lora", GW)
        ch_mask = sb("chunk_mask", T)
        small = sb("small", 160)
        ps = ctx.enter_context(nc.psum_tensor("ps", [P, 8, 512], F32))

        def C(name):
            return consts[:, CONST.index(name), :]

        def pp(name, i=0, rows=slice(0, P)):
            at = PCOL[name] + i
            return par[rows, at:at + 1]

        ident = C("ident")

        hb, _ = carve(rH, 0, NCH, HW)
        xT, wat = carve(rX, 0, KD, T)
        wring = [carve(rX, wat + i * KD * P, KD, P)[0] for i in range(RING)]
        (rowy, rowG, rowGL, toks, uat) = carve_all(rU, 0, [T], [T], [T], [NT, 3, 12])
        beta, tG, nG, nbeg, eGL, decG, decR, eL = [small[:, i * 20:(i + 1) * 20] for i in range(8)]
        beta, tG, nG, nbeg, eGL = [v.rearrange("p (i h) -> p i h", h=4) for v in (beta, tG, nG, nbeg, eGL)]
        dec = sb("dec", 90)
        decG, decR = [dec[:, i * 36:(i + 1) * 36].rearrange("p (h c) -> p h c", c=9) for i in range(2)]
        eL = dec[:, 72:90].rearrange("p (h c) -> p h c", c=9)
        uat0 = uat
        (rowz, rowt, Fp, Fs, uat) = carve_all(rU, uat0, [T], [T], [TP], [PAST + TS])
        fcache, _ = carve(rM, 4 * T, PAST)
        (kcT, vc, sc0, sc1, pT, vtok, _) = carve_all(
            rX, 0, [2, PAST], [8, GW], [PAST + TS], [PAST + TS], [2, T], [NT, GW])
        sc = [sc0, sc1]
        stat = sb("stat", 64)
        mx, rs = stat[:, 40:44], stat[:, 44:48]
        ealog = stat[:, 4:5]
        f_mean, f_rstd = stat[:, 48:53], stat[:, 53:58]
        (cu, cacc, csig, csq, crs, gacc, _) = carve_all(
            rU, uat, [2, 2 * CPAD + T], [2, CPAD + T], [2, HW], [2, T], [T], [6, PAD + T])
        ccen = csig[:, :, 0:T]
        (gsig, _) = carve_all(rU, uat, [6, PAD + T])
        (gsq, _) = carve(rU, uat, 4, T)
        (grs, _) = carve(rU, uat + 7 * T, 4, T)
        (gq, gk, gv, gR, gzs, _) = carve_all(rG, 0, [2, T], [2, T], [2, T], [2, T], [2, T])
        (xm, wsig, wcum, ta, tb, gate, _) = carve_all(rU, uat, [7, T], [2, T], [2, T], [2, T], [2, T], [2, T])
        gz, _ = carve(rU, uat + 11 * T, 2, HW)
        (ac, bc, kc, rc, Au, Ru, Bb, Kb, hat) = carve_all(rH, 0, *[[2, T]] * 8)
        bonus = xm[:, 2:4, :]
        xmv = xm[:, 4:6, :]
        U = []
        (N, NTm, ED, T1, QP, TPQ, BA, OUT, IS, NB, DmT, DI, _) = carve_all(
            rX, 0, [4, P], [4, P], [2, 4, P], [4, P], [4, P], [4, P], [4, 256], [4, 256], [5, 4, HD], [4, P], [4, P], [4, P])
        U.append(dict(DI=DI, N=N, NT=NTm, ED=ED, T1=T1, QP=QP, TPQ=TPQ, BA=BA, OUT=OUT, IS=IS))
        (N, NTm, ED, T1, _) = carve_all(rU, uat0, [4, P], [4, P], [2, 4, P], [4, P])
        (QP, TPQ, _) = carve_all(rU, uat, [4, P], [4, P])
        IS, _ = carve(rU, uat + 7 * T, 5, 4, HD)
        (Aak, V, BA, KA, OUT, DI, _) = carve_all(rH, hat, [4, P], [4, HD], [4, 256], [4, 256], [4, 256], [4, P])
        U.append(dict(DI=DI, N=N, NT=NTm, ED=ED, T1=T1, QP=QP, TPQ=TPQ, BA=BA, OUT=OUT, IS=IS))
        slots_at = KD * T + RT
        slots_end = slots_at + 2 * P + EXPERTS + NT + 5 * NT * EXPERTS + 2 * NT
        wout = [carve(r, at, D)[0] for r, at in ((rU, 0), (rU, uat + 4 * T), (rU, uat + 7 * T + 5 * GW), (rX, slots_end))]
        wout += [carve(rG, i * D, D)[0] for i in range(4)]
        (x1, yacc, hT, hg, wr, logit, _) = carve_all(rH, 0, [NT, D], [NT, D], [2, T], [2, T], [KD, 20], [NT, 20])
        xtok = x1
        ln2, _ = carve(rG, 0, 2, D)
        (x1T, rt, _) = carve_all(rX, 0, [KD, T], [RT])
        wgu = [carve(rU, i * 6144, KD, 2 * FF)[0] for i in range(2)]
        wdn = [carve(rU, i * 6144 + 4096, 2, D)[0] for i in range(2)]
        slot_token = nc.dram_tensor("slot_token", (EXPERTS * CAP, 1), mybir.dt.int32, kind="Internal").ap()
        x1_rows = nc.dram_tensor("x1_rows", (T, D), F32, kind="Internal").ap()
        slots_y = nc.dram_tensor("slots_y", (EXPERTS * CAP, D), F32, kind="Internal").ap()
        xb = [carve(rU, 12288 + i * D, D)[0] for i in range(2)]
        (xbT0, xbT1, yb0, yb1, hrow, hTs, _) = carve_all(rM, 0, [KD, P], [KD, P], [D], [D], [FF], [2, P])
        xbT, yb = [xbT0, xbT1], [yb0, yb1]
        hs = hg[:, 0, 0:FF]
        got = carve(rU, 0, NT, 2, D)[0]
        (slot_c, rank, pos, M1, M2, Mx, sl, _) = carve_all(
            rX, slots_at, [2 * P + EXPERTS + NT], [NT, EXPERTS], [NT, EXPERTS], [NT, EXPERTS], [NT, EXPERTS],
            [NT, EXPERTS], [2, NT])
        ln1_g, _ = carve(rX, slots_end + D, D)
        ln1_b, _ = carve(rU, 2 * D, D)
        lnp = [ln1_g, ln1_b, ln2[:, 0], ln2[:, 1]]
        idx = ctx.enter_context(nc.sbuf_tensor("slot_index", [P, 2 * NT + 1], mybir.dt.int32))
        token_ids = ctx.enter_context(nc.sbuf_tensor("token_ids", [P, NT], mybir.dt.int32))
        block_tokens = ctx.enter_context(nc.sbuf_tensor("block_tokens", [P, EXPERTS], mybir.dt.int32))
        lasts = sb("lasts", 14)[:, :].rearrange("p (k c) -> p k c", k=2)
        bst = stat[:, 8:24]

        names = """dense_step ld_const ld_param ld_pad ld_cache ld_fcache ld_state ld_wout ld_xtok ld_ln1 ld_ln2 ld_router
            shift_rows proj_done evac pads_zero zeros_set vt_pe vt_act s_done s_max s_exp
            p_ready t_done pt_copied pv_done o_act u_tr u_tok u_A u_dexp u_N u_diag u_P u_Pq u_NTp
            u_NTs u_E0 u_D0 u_T1p u_T1 u_DI u_Dp u_Dd u_Ep u_Es u_TPQp u_TPQ u_OUTp u_OUTs u_OUTv u_Sp u_S u_Op u_O
            u_mask u_zero_B u_zero_C o_y o_x o_var o_rstd o_x1 o_x1t o_x1T o_eg m_gu m_silu m_h m_dn m_acc f_rstd
            f_y table_zero ld_zero st_x1 r_scat ld_table x_t x_ta x_tv x_gu x_silu x_h x_ht x_hT x_dn x_ya
            x_yv y_sum st_hb st_gconv st_rows st_conv st_y vec_step act_step pool_step pe_stage
            act_stage vec_stage""".split()
        S = {n: sem(n) for n in names}
        ld_x = [sem(f"ld_x{i}") for i in range(2)]
        ld_w = [sem(f"ld_w{i}") for i in range(RING)]
        ld_e = [sem(f"ld_e{i}") for i in range(2)]
        ld_f = [sem(f"ld_f{i}") for i in range(2)]
        ld_got = [sem(f"ld_got{i}") for i in range(NT)]
        ld_d = [sem(f"ld_d{i}") for i in range(2)]
        ld_xb = [sem(f"ld_xb{i}") for i in range(2)]
        st_state = [sem(f"st_state{i}") for i in range(2)]
        st_yb = [sem(f"st_yb{i}") for i in range(2)]

        HEADP = [(h // 2, (h % 2) * HD) for h in range(HEADS)]
        mixer_bank = [0, 4]
        NORM_PIECES = [(0, TP), (TP, TS)]
        JOINS = ["join2", "join4", "join8", "join16", "join32"]

        def tile_cols(i):
            return PAD + TILES[i][0] if i < 4 else SCOL

        def bank4(b, n, rows=None):
            return ps[0:(rows or n), b, 0:4 * n].rearrange("p (h t) -> p h t", h=4)

        def par_pair(v):
            return v.rearrange("p (pair par) t -> p par pair t", par=2)

        def two_banks(b, n):
            return ps[:, b:b + 2, 0:n]

        def halves(v):
            return v.rearrange("p (u t) -> p u t", u=2)

        def chunks(v):
            return v.rearrange("p c (k t) -> p c k t", t=CHUNK)

        def bcast(v, shape):
            return v.to_broadcast(shape) if not isinstance(v, (int, float)) else v

        def bc_mid(v, k):
            return v.rearrange("p (o t) -> p o t", o=1).to_broadcast([v.shape[0], k, v.shape[1]])

        UNITS, LONG = NT * HEADS, 4 * HEADS

        def heads_n(u):
            return TILES[u // HEADS][1]

        def heads_keys(u):
            return P * (u // HEADS + 1) if u < LONG else PAST + TS

        def score_bank(u):
            n, nk = heads_n(u), heads_keys(u)
            if u < LONG:
                return ps[0:n, u % 4, 0:nk]
            b = 3 * (u % 2)
            return ps[0:n, b:b + 3, :].rearrange("p b t -> p (b t)")[:, 0:nk]

        def out_bank(u):
            return 4 + u % 2 if u < LONG else 3 * (u % 2)

        JOBS, NJ = 2 * NT, len(JOINS)

        def norm_banks(x, m):
            if x == 0:
                return ps[:, 2 * m:2 * m + 2, :]
            return ps[:, 6 + m, 0:2 * TS].rearrange("p (c t) -> p c t", c=2)

        def chunks_of(k):
            return TILES[k // 2][1] // CHUNK

        def chunks_before(k):
            return sum(chunks_of(x) for x in range(k))

        block = ctx.enter_context(nc.Block())

        @block.sync
        def _(sp):
            sp.dma_start(wring[0], a["w_in"][0]).then_inc(ld_w[0], 16)
            for h in range(2):
                c = slice(h * HALF, (h + 1) * HALF)
                sp.dma_start(xT[:, :, c], a["xT"][:, :, c]).then_inc(ld_x[h], 16)
            for j in range(1, NCH):
                if j >= RING:
                    sp.wait_ge(S["proj_done"], j - RING + 1)
                sp.dma_start(wring[j % RING], a["w_in"][j]).then_inc(ld_w[j % RING], 16)
                if j == GATE + RING + 2:
                    sp.wait_ge(S["vec_stage"], AFTER["c_glu"])
                    for k, end in enumerate((CPAD + TP, 2 * CPAD + T)):
                        sp.dma_start(a["o_conv"][:, k], cu[:, :, end - CPAD:end]).then_inc(S["st_conv"], 16)
                if j == BZ + RING:
                    sp.wait_ge(S["evac"], BZ)
                    sp.wait_ge(S["ld_pad"], 16)
                    for k, end in enumerate((PAD + TP, HW)):
                        sp.dma_start(a["o_gconv"][:, k], hb[:, BQ:BQ + 6, end - PAD:end]).then_inc(S["st_gconv"], 16)
            sp.wait_ge(S["shift_rows"], 1)
            sp.dma_start(a["o_shift"], lasts).then_inc(S["st_hb"], 16)
            sp.wait_ge(S["evac"], NCH)
            for t0, n, c0 in PIECES:
                sp.dma_start(a["o_kv"][:, :, t0:t0 + n], hb[:, DK:DK + 4, c0:c0 + n]).then_inc(S["st_hb"], 16)
            sp.wait_ge(S["vec_stage"], AFTER["rows_done"])
            sp.dma_start(a["o_logf"], rowy[104:108, :]).then_inc(S["st_rows"], 16)
            def load_wout(k):
                sp.dma_start(wout[k], a["w_out"][:, k]).then_inc(S["ld_wout"], 16)

            def store_states(m):
                for k, slot in enumerate((2, 4)):
                    sp.dma_start(a["o_state"][m, k], U[m]["IS"][TOP, slot]).then_inc(st_state[m], 16)

            sp.wait_ge(S["u_tr"], JOBS)
            sp.wait_ge(S["st_rows"], 16)
            for k in range(3):
                load_wout(k)
            sp.wait_ge(S["u_A"], JOBS)
            for i, (t0, n) in enumerate(TILES):
                sp.dma_start(xtok[0:n, i], a["x_tok"][t0:t0 + n]).then_inc(S["ld_xtok"], 16)
            sp.wait_ge(S["u_S"], 17)
            store_states(0)
            sp.wait_ge(S["u_O"], JOBS - 1)
            for k in range(4, 8):
                load_wout(k)
            sp.wait_ge(st_state[0], 32)
            load_wout(3)
            sp.dma_start(ln1_g, a["ln"][0:1, :].to_broadcast([P, D])).then_inc(S["ld_ln1"], 16)
            sp.wait_ge(S["u_S"], 18)
            store_states(1)
            sp.wait_ge(S["u_O"], JOBS)
            sp.dma_start(ln1_b, a["ln"][1:2, :].to_broadcast([P, D])).then_inc(S["ld_ln1"], 16)
            sp.dma_start(wr, a["w_router"]).then_inc(S["ld_router"], 16)
            sp.dma_start(rt[:, 0:20], a["b_router"].to_broadcast([P, 20])).then_inc(S["ld_router"], 16)
            sp.dma_start(slot_c, a["slot_c"]).then_inc(S["ld_router"], 16)

            def gate_up(e, loaded):
                sp.dma_start(wgu[e % 2], a["w_gu"][e]).then_inc(loaded[e % 2], 16)

            def down(e, loaded):
                sp.dma_start(wdn[e % 2], a["w_dn"][e]).then_inc(loaded[e % 2], 16)

            sp.wait_ge(st_state[1], 32)
            sp.wait_ge(S["o_x"], NT)
            down(0, ld_f)
            gate_up(1, ld_e)
            down(1, ld_f)
            sp.wait_ge(S["o_x1"], NT)
            gate_up(0, ld_e)
            for i in range(2):
                sp.dma_start(lnp[2 + i], a["ln"][2 + i:3 + i, :].to_broadcast([P, D])).then_inc(S["ld_ln2"], 16)
            for e in range(1, EXPERTS):
                if e + 1 < EXPERTS:
                    sp.wait_ge(S["x_gu"], e)
                    gate_up(e + 1, ld_e)
                if e >= 2:
                    sp.wait_ge(S["x_dn"], e - 1)
                    down(e, ld_f)
            most = sp.value_load(idx[0:1, 2 * NT:], min_val=0, max_val=T)
            with sp.If(most > CAP):
                sp.wait_ge(S["y_sum"], NT)
                for e in range(EXPERTS):
                    if e >= 2:
                        sp.wait_ge(S["m_dn"], (e - 1) * NT)
                    gate_up(e, ld_d)
                    down(e, ld_d)
            for i, (t0, n) in enumerate(TILES):
                sp.wait_ge(S["f_y"], i + 1)
                sp.dma_start(a["o_y"][t0:t0 + n], x1[0:n, i]).then_inc(S["st_y"], 16)
            sp.wait_ge(S["st_y"], 16 * NT)
            sp.wait_ge(S["st_hb"], 48)
            sp.wait_ge(S["st_gconv"], 32)
            sp.wait_ge(S["st_rows"], 16)
            sp.wait_ge(S["st_conv"], 32)

        @block.gpsimd
        def _(pool):
            o, mark = own_order(pool, S["pool_step"])
            o(nc.gpsimd.memset(block_tokens[:, :], 0), S["table_zero"])
            pool.dma_start(slot_token.rearrange("(p e) o -> p (e o)", p=P), block_tokens[:, :]).then_inc(S["ld_zero"], 16)
            nc.gpsimd.memset(hb[:, :, 0:PAD], 0.0).then_inc(S["pads_zero"], 1)
            nc.gpsimd.memset(Fp, 0.0)
            nc.gpsimd.memset(Fs, 0.0)
            nc.gpsimd.memset(toks, 0.0).then_inc(S["zeros_set"], 1)
            pool.wait_ge(S["ld_const"], 32)
            pool.wait_ge(S["vec_stage"], AFTER["w_prep"])
            u = U[1]
            nc.gpsimd.tensor_copy(u["IS"][LOW].rearrange("p c h t -> p (c h) t"), bc_mid(ident[LOW, LOW], 20))
            o(nc.gpsimd.memset(u["BA"][:, :, 0:P], 0.0))
            o(nc.gpsimd.memset(u["IS"][TOP, 0], 0.0))
            pool.wait_ge(S["o_act"], UNITS)
            nc.gpsimd.memset(KA[:, :, 0:P], 0.0).then_inc(S["u_zero_C"], 1)
            for k in range(2 * NT):
                n, u, nch = TILES[k // 2][1], U[k % 2], chunks_of(k)
                pool.wait_ge(S["u_N"], k + 1)
                d = u["N"][0:n, :, 0:n]
                nc.gpsimd.affine_select(out=d, in_=d, compare_op=ALU.not_equal, fill=1.0, base=0,
                                        pattern=[[0, 4], [-1, n]], channel_multiplier=1).then_inc(S["u_diag"], 1)
                pool.wait_ge(S["u_diag"], k + 1)
                nc.gpsimd.tensor_tensor(u["ED"][0:n, 1, :, 0:n], u["N"][0:n, :, 0:n],
                                        bc_mid(C("first_l")[0:n, 0:n], 4), ALU.mult).then_inc(S["u_D0"], 1)
                pool.wait_ge(S["u_D0"], k + 1)
                dec_ = (decG, decR)[k % 2][TOP, :, k // 2 * 2:k // 2 * 2 + nch]
                nc.gpsimd.tensor_tensor(u["DI"][TOP, :, 0:n].rearrange("p h (c t) -> p h c t", c=nch),
                                        ident[TOP, TOP].rearrange("p (a b t) -> p a b t", a=1, b=1).to_broadcast([64, 4, nch, 64]),
                                        dec_.rearrange("p h (c o) -> p h c o", o=1).to_broadcast([64, 4, nch, 64]),
                                        ALU.mult).then_inc(S["u_DI"], 1)
                pool.wait_ge(S["u_DI"], k + 1)

            pool.wait_ge(S["ld_zero"], 16)
            pool.wait_ge(S["vec_stage"], AFTER["r_slots"])
            for i, (t0, n) in enumerate(TILES):
                for k in range(2):
                    c = k * NT + i
                    pool.indirect_dma_start(slot_token[:, :], bass.IndirectOffsetOnAxis(idx[0:n, c:c + 1], 0), token_ids[0:n, i:i + 1], None,
                                            bounds_check=EXPERTS * CAP - 1, oob_is_err=False).then_inc(S["r_scat"], 16)
            pool.wait_ge(S["r_scat"], 32 * NT)
            pool.dma_start(block_tokens[:, :], slot_token.rearrange("(p e) o -> p (e o)", p=P)).then_inc(S["ld_table"], 16)
            pool.wait_ge(S["ld_table"], 16)
            pool.wait_ge(S["st_x1"], 16 * NT)
            for e in range(EXPERTS):
                if e >= 2:
                    pool.wait_ge(S["x_t"], e - 1)
                pool.indirect_dma_start(xb[e % 2], None, x1_rows[:, :], bass.IndirectOffsetOnAxis(block_tokens[:, e:e + 1], 0),
                                        bounds_check=T - 1, oob_is_err=False).then_inc(ld_xb[e % 2], 16)
            pool.wait_ge(S["x_dn"], EXPERTS)
            for k in range(2):
                pool.wait_ge(st_yb[k], 8 * EXPERTS)
            for i, (t0, n) in enumerate(TILES):
                for k in range(2):
                    c = k * NT + i
                    pool.indirect_dma_start(got[0:n, i, k], None, slots_y[:, :], bass.IndirectOffsetOnAxis(idx[0:n, c:c + 1], 0),
                                            bounds_check=EXPERTS * CAP - 1, oob_is_err=False).then_inc(ld_got[i], 16)

        @block.scalar
        def _(act):
            o, mark = own_order(act, S["act_step"])
            A = nc.scalar.activation
            act.dma_start(par[:, :], a["params"]).then_inc(S["ld_param"], 16)
            act.dma_start(lora[:, :], a["lora"]).then_inc(S["ld_param"], 16)
            act.dma_start(ch_mask[:, :], a["ch_mask"]).then_inc(S["ld_param"], 16)
            act.dma_start(fcache[ROWS, :], a["f_cache"]).then_inc(S["ld_fcache"], 16)
            act.dma_start(consts, a["consts"]).then_inc(S["ld_const"], 16)
            act.dma_start(sel, a["sel"]).then_inc(S["ld_const"], 16)
            act.dma_start(hb[:, :, SCOL - PAD:SCOL], a["pads"]).then_inc(S["ld_pad"], 16)
            act.dma_start(cu[:, :, CPAD + TP:2 * CPAD + TP], a["conv_state"]).then_inc(S["ld_state"], 16)

            def rows_log():
                act.wait_ge(S["vec_stage"], AFTER["rows_neg"])
                act.wait_ge(S["ld_param"], 48)
                o(A(rowt[ROWS, :], rowt[ROWS, :], ACT.Exp))
                A(ealog[ROWS, :], pp("row_alog", 0, ROWS), ACT.Exp)
                A(rowt[ROWS, :], rowt[ROWS, :], ACT.Ln, bias=1.0).then_inc(S["act_stage"], 1)

            def conv_gate():
                act.wait_ge(S["evac"], GATE + 2)
                act.wait_ge(S["ld_pad"], 16)
                act.wait_ge(S["pads_zero"], 1)
                A(csig, hb[:, GATE:GATE + 2, :], ACT.Sigmoid).then_inc(S["act_stage"], 1)
                act.wait_ge(S["pe_stage"], AFTER["g_decp"])
                A(decG[TOP], ps[TOP, 4, 0:36].rearrange("p (h c) -> p h c", c=9), ACT.Exp).then_inc(S["act_stage"], 1)

            def gdn_per_token():
                act.wait_ge(S["vec_stage"], AFTER["g_tok"])
                A(beta, toks[:, :, 0, 4:8], ACT.Exp)
                A(nbeg, tG, ACT.Exp)
                A(eGL, toks[:, :, 2, 0:4], ACT.Exp).then_inc(S["act_stage"], 1)

            def four_banks(v):
                return v.rearrange("p c (u t) -> p (c u) t", u=2)

            def gdn_decay():
                act.wait_ge(S["pe_stage"], AFTER["g_pairs"])
                A(four_banks(gR), ps[:, 4:8, 0:HALF], ACT.Exp).then_inc(S["act_stage"], 1)

            def conv_square():
                act.wait_ge(S["vec_stage"], AFTER["c_cen"])
                A(csq, ccen, ACT.Square).then_inc(S["act_stage"], 1)

            def conv_norm():
                act.wait_ge(S["pe_stage"], AFTER["c_var"])
                o(A(halves(crs), two_banks(6, HALF), ACT.Ln, bias=LN_EPS))
                A(crs, crs, ACT.Exp, scale=-0.5).then_inc(S["act_stage"], 1)
                act.wait_ge(S["vec_stage"], AFTER["c_lin"])
                A(csq, ccen, ACT.Sigmoid).then_inc(S["act_stage"], 1)

            def gdn_sigmoid():
                act.wait_ge(S["st_conv"], 32)
                act.wait_ge(S["vec_stage"], AFTER["c_done"])
                A(gsig, gacc, ACT.Sigmoid).then_inc(S["act_stage"], 1)

            def gdn_square():
                act.wait_ge(S["vec_stage"], AFTER["g_silu"])
                A(gsq, rG[:, 0:4 * T].rearrange("p (c t) -> p c t", c=4), ACT.Square).then_inc(S["act_stage"], 1)
                A(gz, hb[:, BZ:BZ + 2, :], ACT.Sigmoid).then_inc(S["act_stage"], 1)

            def gdn_rsqrt(c, stage):
                act.wait_ge(S["pe_stage"], AFTER[stage])
                o(A(four_banks(grs[:, c:c + 2]), ps[:, 4:8, 0:HALF], ACT.Ln, bias=L2_EPS))
                A(grs[:, c:c + 2], grs[:, c:c + 2], ACT.Exp, scale=-0.5).then_inc(S["act_stage"], 1)

            def rwkv_lora():
                act.wait_ge(S["vec_stage"], AFTER["w_small"])
                A(xm[0:16, 6], xm[0:16, 6], ACT.Tanh)
                A(xm[64:96, 6], xm[64:96, 6], ACT.Sigmoid).then_inc(S["act_stage"], 1)

            def rwkv_w():
                act.wait_ge(S["pe_stage"], AFTER["w_w"])
                act.wait_ge(S["vec_stage"], AFTER["g_norm"])
                for c in range(2):
                    last = A(halves(wsig[:, c]), two_banks(4 + 2 * c, HALF), ACT.Sigmoid, bias=pp("w0", c))
                last.then_inc(S["act_stage"], 1)

            def rwkv_a():
                act.wait_ge(S["pe_stage"], AFTER["w_a"])
                for c in range(2):
                    last = A(halves(ta[:, c]), two_banks(4 + 2 * c, HALF), ACT.Sigmoid, bias=pp("a0", c))
                last.then_inc(S["act_stage"], 1)

            def rwkv_gate_and_decays():
                act.wait_ge(S["pe_stage"], AFTER["w_gatep"])
                act.wait_ge(S["vec_stage"], AFTER["w_mix"])
                nc.scalar.copy(four_banks(gate), ps[:, 4:8, 0:HALF]).then_inc(S["act_stage"], 1)
                act.wait_ge(S["st_gconv"], 32)
                act.wait_ge(S["vec_stage"], AFTER["w_cum"])
                A(rc, tb, ACT.Exp, scale=-DECAY)
                A(kc, tb, ACT.Exp, scale=DECAY)
                A(Ru, wcum, ACT.Exp, scale=-DECAY)
                A(eL, eL, ACT.Exp, scale=-DECAY)
                for q in range(2):
                    last = A(decR[TOP, q::2, :], wcum[q * HD:(q + 1) * HD, :, CHUNK - 1::CHUNK], ACT.Exp, scale=-DECAY)
                last.then_inc(S["act_stage"], 1)

            def rwkv_square():
                act.wait_ge(S["vec_stage"], AFTER["w_cprev"])
                A(ac, tb, ACT.Exp, scale=-DECAY)
                A(Au, wsig, ACT.Exp, scale=-DECAY).then_inc(S["act_stage"], 1)
                act.wait_ge(S["vec_stage"], AFTER["w_k1"])
                A(tb, wsig, ACT.Square).then_inc(S["act_stage"], 1)

            def rwkv_rsqrt():
                act.wait_ge(S["pe_stage"], AFTER["w_ksum"])
                o(A(four_banks(tb), ps[:, 4:8, 0:HALF], ACT.Ln, bias=L2_EPS))
                A(tb, tb, ACT.Exp, scale=-0.5).then_inc(S["act_stage"], 1)

            steps = {0: rows_log, GATE + 1: conv_gate, 5: gdn_per_token, 7: gdn_decay, 12: conv_square,
                     13: conv_norm, 14: gdn_sigmoid, 15: gdn_square, 19: rwkv_a, 20: rwkv_gate_and_decays,
                     21: rwkv_square, 22: rwkv_rsqrt, 18: rwkv_w}
            for j in range(NCH):
                act.wait_ge(S["proj_done"], j + 1)
                b = 2 * (j % 2)
                nc.scalar.copy(hb[:, j, PAD:PAD + HALF], ps[:, b, 0:HALF])
                nc.scalar.copy(hb[:, j, PAD + HALF:PAD + TP], ps[:, b + 1, 0:TP - HALF])
                nc.scalar.copy(hb[:, j, SCOL:SCOL + TS], ps[:, b + 1, TP - HALF:HALF]).then_inc(S["evac"], 1)
                if j == 16:
                    gdn_rsqrt(0, "g_sumq")
                    rwkv_lora()
                elif j == 17:
                    gdn_rsqrt(2, "g_sumk")
                elif j in steps:
                    steps[j]()
            act.dma_start(kcT, a["k_cache"]).then_inc(S["ld_cache"], 16)
            act.dma_start(vc, a["v_cache"]).then_inc(S["ld_cache"], 16)
            for i, (t0, n) in enumerate(TILES):
                act.wait_ge(S["vt_pe"], i + 1)
                nc.scalar.copy(vtok[0:n, i], ps[0:n, 6 + i % 2, 0:GW]).then_inc(S["vt_act"], 1)
            def exps(u):
                n, nk = heads_n(u), heads_keys(u)
                act.wait_ge(S["s_max"], u + 1)
                if u >= 2:
                    act.wait_ge(S["t_done"], u - 1)
                c = slice(u % 4, u % 4 + 1)
                A(sc[u % 2][0:n, 0:nk], score_bank(u), ACT.Exp, bias=mx[0:n, c], scale=HD ** -0.5,
                  accum_out=rs[0:n, c]).then_inc(S["s_exp"], 1)

            def output(u):
                i, h = divmod(u, HEADS)
                t0, n = TILES[i]
                pair, pb = HEADP[h]
                act.wait_ge(S["pv_done"], u + 1)
                nc.scalar.copy(mixT[pb:pb + HD, 6 + pair, t0:t0 + n], ps[pb:pb + HD, out_bank(u), 0:n]).then_inc(S["o_act"], 1)

            exps(0)
            for u in range(UNITS):
                if u + 1 <= LONG:
                    exps(u + 1)
                nk = heads_keys(u)
                act.wait_ge(S["t_done"], u + 1)
                if u >= 2:
                    act.wait_ge(S["pv_done"], u - 1)
                if u < LONG:
                    nc.scalar.copy(pT[:, u % 2, 0:nk], ps[:, 6 + u % 2, 0:nk]).then_inc(S["pt_copied"], 1)
                else:
                    nc.scalar.copy(pT[:, u % 2, 0:512], ps[:, 6 + u % 2, :])
                    nc.scalar.copy(pT[LOW, u % 2, 512:T], ps[LOW, out_bank(u) + 2, 64:128]).then_inc(S["pt_copied"], 1)
                if 1 <= u <= LONG:
                    output(u - 1)
                if u >= LONG:
                    output(u)
                if LONG <= u < UNITS - 1:
                    exps(u + 1)
            act.wait_ge(S["pv_done"], UNITS)
            act.dma_start(U[0]["IS"][TOP, 3], a["s_gdn"]).then_inc(S["ld_state"], 16)
            act.dma_start(U[1]["IS"][TOP, 3], a["s_rwkv"]).then_inc(S["ld_state"], 16)
            act.wait_ge(S["st_hb"], 48)

            def begin(k):
                i, m = divmod(k, 2)
                n, u = TILES[i][1], U[m]
                if m == 0:
                    act.wait_ge(S["u_mask"], 1 + i)
                    for h in range(HEADS):
                        A(NB[0:n, h, 0:n], NB[0:n, h, 0:n], ACT.Exp, bias=tG[0:n, i, h:h + 1])
                        last = A(DmT[0:n, h, 0:n], DmT[0:n, h, 0:n], ACT.Exp, bias=nG[0:n, i, h:h + 1])
                    last.then_inc(S["u_dexp"], 1)
                    act.wait_ge(S["u_tr"], k + 1)
                    if k == 0:
                        act.wait_ge(S["u_zero_B"], 1)
                    for h in range(HEADS):
                        hs_ = slice(h * HD, (h + 1) * HD)
                        A(u["QP"][0:n, h, 0:HD], ps[0:n, 0, GW + h * HD:GW + (h + 1) * HD], ACT.Copy, scale=beta[0:n, i, h:h + 1])
                        A(u["QP"][0:n, h, HD:P], ps[0:n, 0, hs_], ACT.Copy, scale=nbeg[0:n, i, h:h + 1])
                        for c in range(chunks_of(k)):
                            r = slice(c * CHUNK, (c + 1) * CHUNK)
                            A(u["BA"][r, h, r], ps[r, 0, hs_], ACT.Copy, scale=eGL[r, i, h:h + 1])
                else:
                    act.wait_ge(S["u_tr"], k + 1)
                    if k == 1:
                        act.wait_ge(S["u_zero_C"], 1)
                    nc.scalar.copy(u["QP"][0:n, :, HD:P], ps[0:n, 4, 0:GW].rearrange("p (h t) -> p h t", h=4))
                    nc.scalar.copy(V[0:n], ps[0:n, 4, GW:512].rearrange("p (h t) -> p h t", h=4))
                    for c in range(chunks_of(k)):
                        r = slice(c * CHUNK, (c + 1) * CHUNK)
                        nc.scalar.copy(u["BA"][r, :, r], ps[r, 5, 0:GW].rearrange("p (h t) -> p h t", h=4))
                        last = nc.scalar.copy(KA[r, :, r], ps[r, 5, GW:512].rearrange("p (h t) -> p h t", h=4))
                    last.then_inc(S["u_tok"], 1)
                act.wait_ge(S["u_NTp"], k + 1)
                nc.scalar.copy(u["NT"][0:n, :, 0:n], bank4(mixer_bank[m] + 1, n)).then_inc(S["u_NTs"], 1)

            def end(k):
                i, m = divmod(k, 2)
                (t0, n), u, b = TILES[i], U[m], mixer_bank[m]
                act.wait_ge(S["u_TPQp"], k + 1)
                nc.scalar.copy(u["TPQ"][0:n], ps[0:n, b + 3, :].rearrange("p (h t) -> p h t", h=4)).then_inc(S["u_TPQ"], 1)
                act.wait_ge(S["u_OUTp"], k + 1)
                src = ps[:, b:b + 2, :].rearrange("p b (h t) -> p (b h) t", h=2)
                nc.scalar.copy(u["OUT"][LOW, :, 0:P], src[LOW, :, 0:P])
                nc.scalar.copy(u["OUT"][:, :, P:P + n], src[:, :, P:P + n]).then_inc(S["u_OUTs"], 1)
                act.wait_ge(S["u_Op"], k + 1)
                nc.scalar.copy(mixT[:, 2 + 2 * m:4 + 2 * m, t0:t0 + n],
                               ps[:, b + 3, 0:2 * n].rearrange("p (c t) -> p c t", c=2)).then_inc(S["u_O"], 1)

            def norm_squares(x):
                t0, n = NORM_PIECES[x]
                A(ta[:, :, t0:t0 + n], mixT[:, 2:4, t0:t0 + n], ACT.Square).then_inc(S["act_stage"], 1)

            def norm_mixer_b(x):
                t0, n = NORM_PIECES[x]
                r = ta[:, :, t0:t0 + n]
                act.wait_ge(S["pe_stage"], AFTER[f"p_gsum{x}"])
                o(A(r, norm_banks(x, 0), ACT.Ln, bias=RMS_EPS, scale=1.0 / HD))
                A(r, r, ACT.Exp, scale=-0.5).then_inc(S["act_stage"], 1)

            def norm_mixer_c_squares(x):
                t0, n = NORM_PIECES[x]
                act.wait_ge(S["vec_stage"], AFTER[f"p_rcen{x}"])
                A(tb[:, :, t0:t0 + n], mixT[:, 4:6, t0:t0 + n], ACT.Square).then_inc(S["act_stage"], 1)

            def norm_mixer_c_end(x):
                t0, n = NORM_PIECES[x]
                r = tb[:, :, t0:t0 + n]
                act.wait_ge(S["pe_stage"], AFTER[f"p_rvar{x}"])
                o(A(r, norm_banks(x, 1), ACT.Ln, bias=GN_EPS, scale=1.0 / HD))
                A(r, r, ACT.Exp, scale=-0.5).then_inc(S["act_stage"], 1)

            def norm_mixer_c(x):
                norm_mixer_c_squares(x)
                norm_mixer_c_end(x)

            begin(0)
            for k in range(JOBS + 1):
                if k:
                    end(k - 1)
                if k + 1 < JOBS:
                    begin(k + 1)
                if k == JOBS - 1:
                    norm_squares(0)
                    norm_mixer_b(0)
                    norm_mixer_c(0)
            norm_squares(1)
            for i, (t0, n) in enumerate(TILES):
                act.wait_ge(S["o_var"], i + 1)
                o(A(stat[0:n, 24:25], stat[0:n, 21:22], ACT.Ln, bias=LN_EPS))
                A(stat[0:n, 24:25], stat[0:n, 24:25], ACT.Exp, scale=-0.5).then_inc(S["o_rstd"], 1)
                act.wait_ge(S["o_x1t"], i + 1)
                nc.scalar.copy(x1T[:, :, t0:t0 + n], ps[:, 4:6, 0:4 * n].rearrange("p b (k t) -> p b k t", t=n)).then_inc(S["o_x1T"], 1)
                act.dma_start(x1_rows[t0:t0 + n], x1[0:n, i]).then_inc(S["st_x1"], 16)
                if i == 0:
                    norm_mixer_b(1)
                    norm_mixer_c_squares(1)
                elif i == 1:
                    norm_mixer_c_end(1)
            act.wait_ge(S["vec_stage"], AFTER["o_lg"])
            A(rt[:, 40:60], rt[:, 40:60], ACT.Exp).then_inc(S["o_eg"], 1)
            act.wait_ge(S["vec_stage"], AFTER["o_w2"])
            A(rt[:, 60:65], rt[:, 60:65], ACT.Exp).then_inc(S["o_eg"], 1)
            act.wait_ge(S["vec_stage"], AFTER["r_slots"])
            most = act.value_load(idx[0:1, 2 * NT:], min_val=0, max_val=T)
            for e in range(EXPERTS + 2):
                if e < EXPERTS:
                    act.wait_ge(S["x_t"], e + 1)
                    nc.scalar.copy(xbT[e % 2][:, 0:4], ps[:, 0].rearrange("p (k t) -> p k t", k=4)).then_inc(S["x_ta"], 1)
                if 1 <= e <= EXPERTS:
                    act.wait_ge(S["x_gu"], e)
                    if e >= 2:
                        act.wait_ge(S["x_h"], e - 1)
                    A(hs, ps[:, 2 + (e - 1) % 2, 0:FF], ACT.Silu).then_inc(S["x_silu"], 1)
                if e >= 2:
                    d = e - 2
                    act.wait_ge(S["x_dn"], d + 1)
                    if d >= 2:
                        act.wait_ge(st_yb[d % 2], 16 * (d // 2))
                    nc.scalar.copy(yb[d % 2][:, 0:512], ps[:, 5]).then_inc(S["x_ya"], 1)
                    act.wait_ge(S["x_ya"], d + 1)
                    act.wait_ge(S["x_yv"], d + 1)
                    act.dma_start(slots_y.rearrange("(p e) d -> p e d", p=P)[:, d], yb[d % 2]).then_inc(st_yb[d % 2], 16)
            with act.If(most > CAP):
                for e in range(EXPERTS):
                    for f in range(2):
                        act.wait_ge(S["m_gu"], 2 * e + f + 1)
                        if e >= 1:
                            act.wait_ge(S["m_h"], 2 * (e - 1) + f + 1)
                        A(halves(hg[:, f]), two_banks(4 * f, HALF), ACT.Silu).then_inc(S["m_silu"], 1)
                act.wait_ge(S["m_acc"], NT * EXPERTS)
            squares = xbT0.rearrange("p k t -> p (k t)")
            for i, (t0, n) in enumerate(TILES):
                act.wait_ge(S["y_sum"], i + 1)
                mean, rstd = f_mean[0:n, i:i + 1], f_rstd[0:n, i:i + 1]
                o(A(mean, mean, ACT.Copy, scale=-1.0 / D))
                o(A(squares[0:n], yacc[0:n, i], ACT.Square, bias=mean, accum_out=rstd))
                o(A(rstd, rstd, ACT.Ln, bias=LN_EPS, scale=1.0 / D))
                A(rstd, rstd, ACT.Exp, scale=-0.5).then_inc(S["f_rstd"], 1)

        @block.vector
        def _(dve):
            o, mark = own_order(dve, S["vec_step"])
            v = nc.vector
            STT, TT, TSC = v.scalar_tensor_tensor, v.tensor_tensor, v.tensor_scalar
            o(v.memset(cu[:, :, 0:CPAD], 0.0))
            dve.wait_ge(S["evac"], 1)
            dve.wait_ge(S["ld_param"], 48)
            dve.wait_ge(S["zeros_set"], 1)
            for t0, n, c0 in PIECES:
                o(TSC(rowz[ROWS, t0:t0 + n], hb[ROWS, SMALL, c0:c0 + n], pp("row_bias", 0, ROWS),
                      pp("row_sign", 0, ROWS), ALU.add, ALU.mult))
            o(STT(rowt[ROWS, :], rowz[ROWS, :], -1.0, rowz[ROWS, :], ALU.mult, ALU.min), S["vec_stage"])
            dve.wait_ge(S["act_stage"], AFTER["rows_log"])
            o(STT(rowy[ROWS, :], rowz[ROWS, :], 0.0, rowt[ROWS, :], ALU.max, ALU.add))
            o(TSC(rowy[ROWS, :], rowy[ROWS, :], ealog[ROWS, :], -1.0, ALU.mult, ALU.mult))
            o(v.tensor_tensor_scan(rowG[ROWS, :], ch_mask[ROWS, :], rowy[ROWS, :], 0.0, ALU.mult, ALU.add))
            G3 = rowG[ROWS, :].rearrange("p (k t) -> p k t", t=CHUNK)
            o(TT(rowGL[ROWS, :].rearrange("p (k t) -> p k t", t=CHUNK),
                 G3[:, :, CHUNK - 1:CHUNK].to_broadcast([12, 9, CHUNK]), G3, ALU.subtract))
            SCAN = v.tensor_tensor_scan
            o(SCAN(Fp[ROWS, :], rowy[ROWS, 0:TP], rowy[ROWS, 0:TP], 0.0, ALU.add, ALU.min))
            dve.wait_ge(S["ld_fcache"], 16)
            o(SCAN(Fs[ROWS, 0:PAST], fcache[ROWS, :], fcache[ROWS, :], 0.0, ALU.add, ALU.min))
            o(SCAN(Fs[ROWS, PAST:], rowy[ROWS, TP:], rowy[ROWS, TP:], Fs[ROWS, PAST - 1:PAST], ALU.add, ALU.min),
              S["vec_stage"])
            dve.wait_ge(S["pe_stage"], AFTER["g_tokp"])
            tk = ps[:, 5, 0:NT * 36].rearrange("p (i k r) -> p i k r", k=3, r=12)
            v.tensor_copy(toks[:, 0:4], tk[:, 0:4])
            o(v.tensor_copy(toks[LOW, 4], tk[LOW, 4]))
            o(TT(tG, toks[:, :, 1, 0:4], toks[:, :, 0, 4:8], ALU.add))
            o(TSC(nG, toks[:, :, 1, 0:4], -1.0, None, ALU.mult), S["vec_stage"])
            dve.wait_ge(S["ld_state"], 16)
            dve.wait_ge(S["evac"], GATE + 2)
            dve.wait_ge(S["act_stage"], AFTER["c_gate"])
            TT(cu[:, :, CPAD:CPAD + TP], csig[:, :, PAD:PAD + TP], hb[:, VAL:VAL + 2, PAD:PAD + TP], ALU.mult)
            o(TT(cu[:, :, 2 * CPAD + TP:], csig[:, :, SCOL:], hb[:, VAL:VAL + 2, SCOL:], ALU.mult), S["vec_stage"])
            NC_ = CPAD + T
            for j in range(CW):
                for c in range(2):
                    w = pp("conv_w", c * CW + j)
                    if j == 0:
                        o(TSC(cacc[:, c], cu[:, c, 0:NC_], w, pp("conv_b", c), ALU.mult, ALU.add))
                    else:
                        o(STT(cacc[:, c], cu[:, c, j:j + NC_], w, cacc[:, c], ALU.mult, ALU.add),
                          S["vec_stage"] if (j, c) == (CW - 1, 1) else None)
                if j == 16:
                    dve.wait_ge(S["act_stage"], AFTER["g_texp"])
                    o(TSC(nbeg, nbeg, -1.0, None, ALU.mult), S["vec_stage"])
            dve.wait_ge(S["pads_zero"], 1)
            dve.wait_ge(S["ld_pad"], 16)
            dve.wait_ge(S["evac"], BZ)
            for j in range(GTAPS):
                for c in range(6):
                    w = pp("gconv_w", c * GTAPS + j)
                    src = hb[:, BQ + c, j:j + PAD + T]
                    if j == 0:
                        o(TSC(gacc[:, c], src, w, None, ALU.mult))
                    else:
                        o(STT(gacc[:, c], src, w, gacc[:, c], ALU.mult, ALU.add),
                          S["vec_stage"] if (j, c) == (GTAPS - 1, 5) else None)
            dve.wait_ge(S["pe_stage"], AFTER["c_mean"])
            TT(ccen[:, :, 0:TP], cacc[:, :, 0:TP], bc_mid(ps[:, 4, :], 2), ALU.subtract)
            o(TT(ccen[:, :, TP:], cacc[:, :, CPAD + TP:], bc_mid(ps[:, 5, 0:TS], 2), ALU.subtract), S["vec_stage"])
            dve.wait_ge(S["act_stage"], AFTER["c_rstd"])
            o(TT(ccen, ccen, bc_mid(crs, 2), ALU.mult))
            for c in range(2):
                o(TSC(ccen[:, c], ccen[:, c], pp("conv_g", c), pp("conv_lb", c), ALU.mult, ALU.add),
                  S["vec_stage"] if c == 1 else None)
            dve.wait_ge(S["act_stage"], AFTER["c_sig"])
            o(TT(mixT[:, 0:2], ccen, csq, ALU.mult), S["vec_stage"])
            dve.wait_ge(S["act_stage"], AFTER["g_sig"])
            qkv = rG[:, 0:6 * T].rearrange("p (c t) -> p c t", c=6)
            TT(qkv[:, :, 0:TP], gacc[:, :, 0:TP], gsig[:, :, 0:TP], ALU.mult)
            o(TT(qkv[:, :, TP:], gacc[:, :, PAD + TP:], gsig[:, :, PAD + TP:], ALU.mult), S["vec_stage"])

            def token_shift(c, stage):
                src = hb[:, CR + c if c < 6 else SMALL]
                m = pp("mu", c) if c < 6 else pp("mu_s")
                d = gate.rearrange("p c t -> p (c t)")[:, 0:PAD + T]
                if c < 6:
                    dve.wait_ge(S["evac"], CR + c + 1)
                o(TT(d, src[:, PAD - 1:HW - 1], src[:, PAD:HW], ALU.subtract))
                for t0, n, c0 in PIECES:
                    o(STT(xm[:, c, t0:t0 + n], d[:, c0 - PAD:c0 - PAD + n], m, src[:, c0:c0 + n], ALU.mult, ALU.add),
                      S["vec_stage"] if stage and t0 == TP else None)

            token_shift(6, True)
            dve.wait_ge(S["act_stage"], AFTER["g_zsig"])
            for t0, n, c0 in PIECES:
                o(TT(gzs[:, :, t0:t0 + n], hb[:, BZ:BZ + 2, c0:c0 + n], gz[:, :, c0:c0 + n], ALU.mult))
            dve.wait_ge(S["act_stage"], AFTER["g_rsq"])
            o(STT(gq, gq, HD ** -0.5, grs[:, 0:2], ALU.mult, ALU.mult))
            o(TT(gR, gq, gR, ALU.mult))
            dve.wait_ge(S["act_stage"], AFTER["g_rs"])
            o(TT(gk, gk, grs[:, 2:4], ALU.mult), S["vec_stage"])
            for c in range(6):
                token_shift(c, c == 5)
            for k, end in enumerate((PAD + TP, HW)):
                v.tensor_copy(lasts[:, k, 0:6], hb[:, CR:CR + 6, end - 1])
                last = v.tensor_copy(lasts[:, k, 6:7], hb[:, SMALL, end - 1:end])
            o(last, S["shift_rows"])
            dve.wait_ge(S["act_stage"], AFTER["w_sg"])
            for c in range(2):
                o(SCAN(wcum[:, c], ch_mask[:, :], wsig[:, c], 0.0, ALU.mult, ALU.add))
            W4 = chunks(wcum)
            for c in range(2):
                o(TT(chunks(tb)[:, c], W4[:, c], W4[:, c, :, 31:32].to_broadcast([P, 9, CHUNK]), ALU.subtract))
            o(TT(eL, W4[:, :, :, 63:64].rearrange("p c k o -> p c (k o)"),
                 W4[:, :, :, 31:32].rearrange("p c k o -> p c (k o)"), ALU.subtract), S["vec_stage"])
            dve.wait_ge(S["act_stage"], AFTER["w_e"])
            o(TT(tb, tb, wsig, ALU.subtract))
            o(TT(wsig, wcum, wsig, ALU.subtract), S["vec_stage"])
            dve.wait_ge(S["act_stage"], AFTER["w_e5"])
            r, k = xm[:, 0:2], xm[:, 2:4]
            for c in range(2):
                o(TSC(wsig[:, c], k[:, c], pp("k_k", c), None, ALU.mult), S["vec_stage"] if c == 1 else None)
            for c in range(2):
                o(TSC(wcum[:, c], ta[:, c], 1.0, pp("k_a", c), ALU.subtract, ALU.mult))
            o(STT(k, wcum, 1.0, k, ALU.add, ALU.mult))
            o(TT(rc, r, rc, ALU.mult))
            o(TT(Ru, r, Ru, ALU.mult))
            for c in range(2):
                o(STT(wcum[:, c], r[:, c], pp("r_k", c), k[:, c], ALU.mult, ALU.mult),
                  S["vec_stage"] if c == 1 else None)
            dve.wait_ge(S["act_stage"], AFTER["w_krs"])
            o(TT(wsig, wsig, tb, ALU.mult))
            o(STT(ac, wsig, -1.0, ac, ALU.mult, ALU.mult))
            o(STT(Au, wsig, -1.0, Au, ALU.mult, ALU.mult))
            o(TT(tb, wsig, ta, ALU.mult))
            o(TT(bc, tb, kc, ALU.mult))
            o(TT(kc, k, kc, ALU.mult))
            for c in range(2):
                e = eL[:, c].rearrange("p (k o) -> p k o", o=1).to_broadcast([P, 9, CHUNK])
                o(TT(chunks(Bb)[:, c], chunks(bc)[:, c], e, ALU.mult))
                o(TT(chunks(Kb)[:, c], chunks(kc)[:, c], e, ALU.mult))
            dve.wait_ge(S["pe_stage"], AFTER["w_bonp"])
            o(TT(bonus.rearrange("p c (u t) -> p (c u) t", u=2), xmv.rearrange("p c (u t) -> p (c u) t", u=2),
                 ps[:, 4:8, 0:HALF], ALU.mult), S["vec_stage"])
            def negative_max(u):
                dve.wait_ge(S["s_done"], u + 1)
                m = mx[0:heads_n(u), u % 4:u % 4 + 1]
                o(v.reduce_max(m, score_bank(u), AX))
                o(TSC(m, m, -HD ** -0.5, None, ALU.mult), S["s_max"])

            negative_max(0)
            negative_max(1)
            for u in range(UNITS):
                if u + 2 <= LONG:
                    negative_max(u + 2)
                n, nk = heads_n(u), heads_keys(u)
                r = rs[0:n, u % 4:u % 4 + 1]
                dve.wait_ge(S["s_exp"], u + 1)
                o(v.reciprocal(r, r))
                o(TSC(sc[u % 2][0:n, 0:nk], sc[u % 2][0:n, 0:nk], r, None, ALU.mult), S["p_ready"])
                if LONG <= u < UNITS - 1:
                    negative_max(u + 1)
            dve.wait_ge(S["o_act"], UNITS)

            def begin_decays(k):
                i, m = divmod(k, 2)
                if m:
                    return
                n = TILES[i][1]
                dve.wait_ge(S["u_tr"], k + 1)
                Gb = bank4(1, n)
                STT(NB[0:n, :, 0:n], Gb, -1.0, bc_mid(C("neg_strict_l")[0:n, 0:n], 4), ALU.mult, ALU.add)
                mark(TT(DmT[0:n, :, 0:n], Gb, bc_mid(C("neg_incl_u")[0:n, 0:n], 4), ALU.add), S["u_mask"])

            def begin_matrices(k, q):
                i, m = divmod(k, 2)
                n, u = TILES[i][1], U[m]
                if m == 0:
                    dve.wait_ge(S["u_dexp"], i + 1)
                dve.wait_ge(S["u_A"], k + 1)
                if m == 0:
                    blk = ps[0:n, 2 + q, 0:4 * n].rearrange("p (k c t) -> p k c t", k=2, c=2)
                    STT(u["N"][0:n, q::2, 0:n], blk[:, 0], -1.0, NB[0:n, q::2, 0:n], ALU.mult, ALU.mult)
                    last = TT(u["BA"][0:n, q::2, P:P + n], blk[:, 1], DmT[0:n, q::2, 0:n], ALU.mult)
                else:
                    blk = ps[0:n, 4 + 2 * q, 0:4 * n].rearrange("p (k c t) -> p k c t", k=2, c=2)
                    blk2 = ps[0:n, 5 + 2 * q, 0:4 * n].rearrange("p (k c t) -> p k c t", k=2, c=2)
                    TT(u["N"][0:n, q::2, 0:n], blk[:, 0], bc_mid(C("strict_l")[0:n, 0:n], 2), ALU.mult)
                    TT(Aak[0:n, q::2, 0:n], blk[:, 1], bc_mid(C("strict_u")[0:n, 0:n], 2), ALU.mult)
                    TT(u["BA"][0:n, q::2, P:P + n], blk2[:, 0], bc_mid(C("incl_u")[0:n, 0:n], 2), ALU.mult)
                    last = TT(KA[0:n, q::2, P:P + n], blk2[:, 1], bc_mid(C("incl_u")[0:n, 0:n], 2), ALU.mult)
                if q:
                    mark(last, S["u_N"])

            def first_inverse(k):
                i, m = divmod(k, 2)
                n, u = TILES[i][1], U[m]
                dve.wait_ge(S["u_NTs"], k + 1)
                mark(TT(u["ED"][0:n, 0, :, 0:n], u["NT"][0:n, :, 0:n], bc_mid(C("first_u")[0:n, 0:n], 4), ALU.mult), S["u_E0"])
                if m:
                    dve.wait_ge(S["u_P"], i + 1)
                    mark(v.tensor_copy(u["QP"][0:n, :, 0:HD], ps[0:n, 4, 0:GW].rearrange("p (h t) -> p h t", h=4)), S["u_Pq"])

            def join_middle(k, s):
                i, m = divmod(k, 2)
                n, u = TILES[i][1], U[m]
                dve.wait_ge(S["u_T1p"], NJ * k + s + 1)
                mark(TT(u["T1"][0:n, :, 0:n], bank4(mixer_bank[m] + 2, n), bc_mid(C(JOINS[s])[0:n, 0:n], 4), ALU.mult), S["u_T1"])

            def join_sum(k, s):
                i, m = divmod(k, 2)
                n, u, b = TILES[i][1], U[m], mixer_bank[m]
                if s == 0:
                    dve.wait_ge(S["u_D0"], k + 1)
                    dve.wait_ge(S["u_E0"], k + 1)
                if s < NJ - 1:
                    dve.wait_ge(S["u_Dp"], (NJ - 1) * k + s + 1)
                    D_ = u["ED"][0:n, 1, :, 0:n]
                    mark(TT(D_, D_, bank4(b + 1, n), ALU.add), S["u_Dd"])
                dve.wait_ge(S["u_Ep"], NJ * k + s + 1)
                E_ = u["ED"][0:n, 0, :, 0:n]
                mark(TT(E_, E_, bank4(b, n), ALU.add), S["u_Es"])

            def end_decay(k):
                i, m = divmod(k, 2)
                n, u, b = TILES[i][1], U[m], mixer_bank[m]
                dve.wait_ge(S["u_OUTs"], k + 1)
                dve.wait_ge(S["u_DI"], k + 1)
                src = ps[TOP, b:b + 2, :].rearrange("p b (h t) -> p (b h) t", h=2)
                mark(TT(u["OUT"][TOP, :, 0:n], src[:, :, 0:n], u["DI"][TOP, :, 0:n], ALU.add), S["u_OUTv"])

            def end_state(k, c):
                i, m = divmod(k, 2)
                ch = 2 * i + c
                dve.wait_ge(S["u_Sp"], chunks_before(k) + c + 1)
                mark(v.tensor_copy(U[m]["IS"][TOP, 4 if ch == 8 else (ch + 1) % 3],
                                   ps[TOP, mixer_bank[m] + 2, c * GW:(c + 1) * GW].rearrange("p (h t) -> p h t", h=4)), S["u_S"])

            def norm_centre(x):
                t0, n = NORM_PIECES[x]
                dve.wait_ge(S["pe_stage"], AFTER[f"p_rsum{x}"])
                y = mixT[:, 4:6, t0:t0 + n]
                o(STT(y, norm_banks(x, 1), -1.0 / HD, y, ALU.mult, ALU.add), S["vec_stage"])

            def norm_mixer_b(x):
                t0, n = NORM_PIECES[x]
                ts, y = slice(t0, t0 + n), mixT[:, 2:4, t0:t0 + n]
                dve.wait_ge(S["act_stage"], AFTER[f"p_grs{x}"])
                o(TT(y, y, ta[:, :, ts], ALU.mult))
                o(STT(y, y, pp("gnorm"), gzs[:, :, ts], ALU.mult, ALU.mult))

            def norm_mixer_c(x):
                t0, n = NORM_PIECES[x]
                ts, y = slice(t0, t0 + n), mixT[:, 4:6, t0:t0 + n]
                dve.wait_ge(S["act_stage"], AFTER[f"p_rrs{x}"])
                for c in range(2):
                    o(STT(y[:, c], y[:, c], pp("lnx_g", c), tb[:, c, ts], ALU.mult, ALU.mult))
                    o(STT(y[:, c], y[:, c], pp("lnx_b", c), bonus[:, c, ts], ALU.add, ALU.add))
                o(TT(y, y, gate[:, :, ts], ALU.mult), S["vec_stage"])

            begin_decays(0)
            u = U[0]
            v.memset(u["BA"][:, :, 0:P], 0.0)
            v.memset(u["IS"][TOP, 0], 0.0)
            mark(v.tensor_copy(u["IS"][LOW].rearrange("p c h t -> p (c h) t"), bc_mid(ident[LOW, LOW], 20)), S["u_zero_B"])
            begin_matrices(0, 0)
            begin_matrices(0, 1)
            for k in range(JOBS + 1):
                joins, ends, begins = k < JOBS, k > 0, k + 1 < JOBS
                if joins:
                    first_inverse(k)
                    join_middle(k, 0)
                    join_sum(k, 0)
                if ends:
                    end_decay(k - 1)
                if joins:
                    join_middle(k, 1)
                    join_sum(k, 1)
                if ends:
                    end_state(k - 1, 0)
                if joins:
                    join_middle(k, 2)
                if ends and chunks_of(k - 1) == 2:
                    end_state(k - 1, 1)
                if joins:
                    join_sum(k, 2)
                if k == JOBS - 1:
                    norm_centre(0)
                if begins:
                    begin_decays(k + 1)
                if joins:
                    join_middle(k, 3)
                    join_sum(k, 3)
                if begins:
                    begin_matrices(k + 1, 0)
                if joins:
                    join_middle(k, 4)
                if begins:
                    begin_matrices(k + 1, 1)
                if joins:
                    join_sum(k, 4)
                if k == JOBS - 1:
                    norm_mixer_b(0)
                    norm_mixer_c(0)
            dve.wait_ge(S["ld_xtok"], 16 * NT)
            dve.wait_ge(S["ld_ln1"], 32)

            def layer_norm(x, n, i, out):
                for k in range(2):
                    o(v.bn_stats(bst[0:n, 6 * k:6 * k + 6], x[:, k * 512:(k + 1) * 512]))
                o(v.bn_aggr(stat[0:n, 20:22], bst[0:n, 0:12]), S["o_var"])
                dve.wait_ge(S["o_rstd"], i + 1)
                o(STT(x, x, stat[0:n, 20:21], lnp[0][0:n], ALU.subtract, ALU.mult))
                o(STT(out, x, stat[0:n, 24:25], lnp[1][0:n], ALU.mult, ALU.add), S["o_x1"])

            for i, (t0, n) in enumerate(TILES):
                dve.wait_ge(S["o_y"], i + 1)
                x = xtok[0:n, i]
                b = 2 * (i % 2)
                o(STT(x, x, ALPHA, ps[0:n, b:b + 2, :].rearrange("p b t -> p (b t)"), ALU.mult, ALU.add), S["o_x"])
                layer_norm(x, n, i, x1[0:n, i])
                if i == 0:
                    norm_centre(1)
                elif i == 1:
                    norm_mixer_b(1)
                elif i == 2:
                    norm_mixer_c(1)
            dve.wait_ge(S["ld_router"], 48)
            o(v.memset(logit, 0.0))
            o(v.tensor_copy(token_ids[:, :], slot_c[:, 2 * P + EXPERTS:]))
            dve.wait_ge(S["pe_stage"], AFTER["o_log"])
            lp = ps[:, 6, 0:NT * 20].rearrange("p (i r) -> p i r", r=20)
            bias = bc_mid(rt[:, 0:20], 4)
            TT(logit[:, 0:4], lp[:, 0:4], bias, ALU.add)
            o(TT(logit[LOW, 4], lp[LOW, 4], rt[LOW, 0:20], ALU.add))
            lg = logit[:, :, 0:4]
            at = 65

            def tmp(*shape):
                nonlocal at
                n = int(np.prod(shape))
                t = rt[:, at:at + n]
                at += n
                if len(shape) > 1:
                    names_ = "abc"[:len(shape)]
                    t = t.rearrange(f"p ({' '.join(names_)}) -> p {' '.join(names_)}", **dict(zip(names_[1:], shape[1:])))
                return t

            def groups(x):
                return x.rearrange("p i (g o) -> p i g o", o=1).to_broadcast([P, NT, 4, 4])

            def within(x):
                return x.rearrange("p i (o k) -> p i o k", o=1).to_broadcast([P, NT, 4, 4])

            def by_group(x):
                return x.rearrange("p i (g e) -> p i g e", e=4)

            def bc4(x):
                return x.rearrange("p (i o) -> p i o", o=1).to_broadcast([P, NT, 4])

            def first_max(values, best, hit):
                eq, n_eq = tmp(NT * 4), tmp(NT * 4)
                o(TT(eq.rearrange("p (i k) -> p i k", k=4), values, bc4(best), ALU.is_equal))
                o(SCAN(n_eq, starts, eq, 0.0, ALU.mult, ALU.add))
                o(STT(hit.rearrange("p i k -> p (i k)"), n_eq, 1.0, eq, ALU.is_equal, ALU.mult))

            starts = tmp(NT * 4)
            o(v.memset(starts, 1.0))
            o(v.memset(starts.rearrange("p (i k) -> p i k", k=4)[:, :, 0], 0.0))
            mg, hitg = tmp(NT), tmp(NT, 4)
            o(v.reduce_max(mg, lg, AX))
            eg = rt[:, 40:60].rearrange("p (i k) -> p i k", k=4)
            o(TT(eg, lg, bc4(mg), ALU.subtract), S["vec_stage"])
            first_max(lg, mg, hitg)
            le4 = tmp(NT, 4, 4)
            o(TT(le4, by_group(logit[:, :, 4:20]), groups(hitg), ALU.mult))
            le = tmp(NT, 4)
            o(v.reduce_sum(le, le4.rearrange("p i g e -> p i e g"), AX))
            m1, hit1, m2, hit2, le2 = tmp(NT), tmp(NT, 4), tmp(NT), tmp(NT, 4), tmp(NT, 4)
            o(v.reduce_max(m1, le, AX))
            first_max(le, m1, hit1)
            o(STT(le2, hit1, NEG, le, ALU.mult, ALU.add))
            o(v.reduce_max(m2, le2, AX))
            first_max(le2, m2, hit2)
            d21 = rt[:, 60:65]
            o(TT(d21, m2, m1, ALU.subtract), S["vec_stage"])
            for k, (M, hit) in enumerate(((M1, hit1), (M2, hit2))):
                o(TT(by_group(M), within(hit), groups(hitg), ALU.mult))
                o(v.memset(M[TOP, 4], 0.0))
            o(TT(Mx, M1, M2, ALU.add), S["vec_stage"])
            dve.wait_ge(S["o_eg"], 2)
            gs, w1, w2 = tmp(NT), tmp(NT), tmp(NT)
            o(v.reduce_sum(gs, eg, AX))
            o(STT(gs, d21, 1.0, gs, ALU.add, ALU.mult))
            o(v.reciprocal(w1, gs))
            o(TT(w2, w1, d21, ALU.mult))
            dve.wait_ge(S["pe_stage"], AFTER["r_rank"])
            o(v.tensor_copy(rank, ps[:, 7, 0:NT * EXPERTS].rearrange("p (i e) -> p i e", e=EXPERTS)))
            o(v.reduce_max(stat[:, 31:32], ps[:, 7, NT * EXPERTS:(NT + 1) * EXPERTS], AX))
            o(TSC(pos, rank, float(CAP), FAR, ALU.is_ge, ALU.mult))
            o(STT(pos, rank, float(EXPERTS), pos, ALU.mult, ALU.add))
            o(TT(pos, pos, bc_mid(slot_c[:, 2 * P:2 * P + EXPERTS], NT), ALU.add))
            for k, M in enumerate((M1, M2)):
                o(TT(M, M, pos, ALU.mult))
                o(v.reduce_sum(sl[:, k], M, AX))
            o(v.tensor_copy(idx[:, 2 * NT:], stat[:, 31:32]))
            o(v.tensor_copy(idx[:, 0:2 * NT], sl.rearrange("p k i -> p (k i)")), S["vec_stage"])
            o(TT(hit1, hit1, bc4(w1), ALU.mult))
            o(TT(hit2, hit2, bc4(w2), ALU.mult))
            o(TT(hit1, hit1, hit2, ALU.add))
            o(TT(le4, within(hit1), groups(hitg), ALU.mult))
            comb = le4.rearrange("p i g e -> p i (g e)")
            for i, (t0, n) in enumerate(TILES):
                o(TSC(yacc[0:n, i], x1[0:n, i], ALPHA, None, ALU.mult))
            most = dve.value_load(idx[0:1, 2 * NT:], min_val=0, max_val=T)
            for e in range(EXPERTS + 2):
                if e < EXPERTS:
                    dve.wait_ge(S["x_t"], e + 1)
                    v.tensor_copy(xbT[e % 2][:, 4:8], ps[:, 1].rearrange("p (k t) -> p k t", k=4)).then_inc(S["x_tv"], 1)
                if e >= 2:
                    d = e - 2
                    dve.wait_ge(S["x_ht"], d + 1)
                    v.tensor_copy(hTs, ps[:, 4, 0:FF].rearrange("p (f t) -> p f t", f=2)).then_inc(S["x_hT"], 1)
                if 1 <= e <= EXPERTS:
                    dve.wait_ge(S["x_silu"], e)
                    if e >= 2:
                        dve.wait_ge(S["x_ht"], e - 1)
                    TT(hrow, hs, ps[:, 2 + (e - 1) % 2, FF:], ALU.mult).then_inc(S["x_h"], 1)
                if e >= 2:
                    dve.wait_ge(S["x_dn"], d + 1)
                    if d >= 2:
                        dve.wait_ge(st_yb[d % 2], 16 * (d // 2))
                    v.tensor_copy(yb[d % 2][:, 512:], ps[:, 6]).then_inc(S["x_yv"], 1)
            for i, (t0, n) in enumerate(TILES):
                dve.wait_ge(ld_got[i], 32)
                o(STT(yacc[0:n, i], got[0:n, i, 0], w1[0:n, i:i + 1], yacc[0:n, i], ALU.mult, ALU.add))
                o(STT(yacc[0:n, i], got[0:n, i, 1], w2[0:n, i:i + 1], yacc[0:n, i], ALU.mult, ALU.add,
                      accum_out=f_mean[0:n, i:i + 1]), S["y_sum"])
            with dve.If(most > CAP):
                od, _ = own_order(dve, S["dense_step"])
                for i, (t0, n) in enumerate(TILES):
                    od(TSC(yacc[0:n, i], x1[0:n, i], ALPHA, None, ALU.mult))
                for e in range(EXPERTS):
                    for f in range(2):
                        dve.wait_ge(S["m_silu"], 2 * e + f + 1)
                        if e >= 1:
                            dve.wait_ge(S["m_dn"], NT * e)
                        mark(TT(halves(hT[:, f]), halves(hg[:, f]), two_banks(4 * f + 2, HALF), ALU.mult), S["m_h"])
                    for i, (t0, n) in enumerate(TILES):
                        dve.wait_ge(S["m_dn"], NT * e + i + 1)
                        b = 2 * (i % 2)
                        mark(STT(yacc[0:n, i], ps[0:n, b:b + 2, :].rearrange("p b t -> p (b t)"), comb[0:n, i, e:e + 1],
                                 yacc[0:n, i], ALU.mult, ALU.add, accum_out=f_mean[0:n, i:i + 1]), S["m_acc"])
                dve.wait_ge(S["m_acc"], NT * EXPERTS)
            dve.wait_ge(S["ld_ln2"], 32)
            for i, (t0, n) in enumerate(TILES):
                dve.wait_ge(S["f_rstd"], i + 1)
                o(STT(yacc[0:n, i], yacc[0:n, i], f_mean[0:n, i:i + 1], lnp[2][0:n], ALU.add, ALU.mult))
                o(STT(x1[0:n, i], yacc[0:n, i], f_rstd[0:n, i:i + 1], lnp[3][0:n], ALU.mult, ALU.add), S["f_y"])

        @block.tensor
        def _(pe):
            mm, tr = nc.tensor.matmul, nc.tensor.transpose
            def head_sums(b, src):
                for c in range(2):
                    for h in range(2):
                        last = mm(ps[:, b + 2 * c + h, 0:HALF], C("head_ones"), src[:, c, h * HALF:(h + 1) * HALF],
                                  start=True, stop=True)
                last.then_inc(S["pe_stage"], 1)

            def lora_product(rows):
                for c in range(2):
                    for h in range(2):
                        last = mm(ps[:, 4 + 2 * c + h, 0:HALF], lora[rows, c * P:(c + 1) * P],
                                  xm[rows, 6, h * HALF:(h + 1) * HALF], start=True, stop=True)
                last.then_inc(S["pe_stage"], 1)

            def per_token_rows():
                pe.wait_ge(S["ld_const"], 32)
                pe.wait_ge(S["vec_stage"], AFTER["rows_done"])
                for h in range(HEADS):
                    last = mm(ps[TOP, 4, h * 9:(h + 1) * 9], sel[ROWS, SEL_G + h, 0:64], rowG[ROWS, CHUNK - 1::CHUNK],
                              start=True, stop=True)
                last.then_inc(S["pe_stage"], 1)
                for i, (t0, n) in enumerate(TILES):
                    for k, rows in enumerate((rowy, rowG, rowGL)):
                        at = (3 * i + k) * 12
                        last = mm(ps[0:n, 5, at:at + 12], rows[ROWS, t0:t0 + n], ident[ROWS, ROWS], start=True, stop=True)
                last.then_inc(S["pe_stage"], 1)

            def decay_pairs():
                pe.wait_ge(S["act_stage"], AFTER["g_dec"])
                pe.wait_ge(S["vec_stage"], AFTER["g_tok"])
                for p_ in range(2):
                    for h in range(2):
                        last = mm(ps[:, 4 + 2 * p_ + h, 0:HALF], sel[ROWS, SEL_PAIR + p_, :],
                                  rowG[ROWS, h * HALF:(h + 1) * HALF], start=True, stop=True)
                last.then_inc(S["pe_stage"], 1)

            def conv_mean():
                pe.wait_ge(S["act_stage"], AFTER["g_eg"])
                pe.wait_ge(S["vec_stage"], AFTER["c_taps"])
                for dst, src in ((ps[:, 4, :], (0, TP)), (ps[:, 5, 0:TS], (CPAD + TP, TS))):
                    for c in range(2):
                        last = mm(dst, C("mean_ones"), cacc[:, c, src[0]:src[0] + src[1]], start=(c == 0), stop=(c == 1))
                last.then_inc(S["pe_stage"], 1)

            def conv_var():
                pe.wait_ge(S["act_stage"], AFTER["c_sq"])
                for h in range(2):
                    for c in range(2):
                        last = mm(ps[:, 6 + h, 0:HALF], C("mean_ones"), csq[:, c, h * HALF:(h + 1) * HALF],
                                  start=(c == 0), stop=(c == 1))
                last.then_inc(S["pe_stage"], 1)

            def gdn_q_sums():
                pe.wait_ge(S["act_stage"], AFTER["g_sq"])
                head_sums(4, gsq[:, 0:2])

            def gdn_k_sums():
                pe.wait_ge(S["act_stage"], AFTER["g_rsq"])
                head_sums(4, gsq[:, 2:4])

            def rwkv_w():
                pe.wait_ge(S["act_stage"], AFTER["g_rs"])
                lora_product(slice(0, 16))

            def rwkv_a():
                pe.wait_ge(S["act_stage"], AFTER["w_sg"])
                lora_product(slice(32, 48))

            def rwkv_gate():
                pe.wait_ge(S["act_stage"], AFTER["w_asig"])
                lora_product(slice(64, 96))

            def rwkv_k_sums():
                pe.wait_ge(S["act_stage"], AFTER["w_sq"])
                head_sums(4, tb)

            steps = {GATE + 1: per_token_rows, 7: decay_pairs, 12: conv_mean, 14: conv_var, 17: gdn_q_sums,
                     18: gdn_k_sums, 19: rwkv_w, 20: rwkv_a, 21: rwkv_gate, 23: rwkv_k_sums}
            for j in range(NCH):
                if j in steps:
                    steps[j]()
                pe.wait_ge(ld_w[j % RING], 16 * (j // RING + 1))
                if j >= 2:
                    pe.wait_ge(S["evac"], j - 1)
                for h in range(2):
                    if j == 0:
                        pe.wait_ge(ld_x[h], 16)
                    for k in range(KD):
                        last = mm(ps[:, 2 * (j % 2) + h, 0:HALF], wring[j % RING][:, k], xT[:, k, h * HALF:(h + 1) * HALF],
                                  start=(k == 0), stop=(k == KD - 1))
                last.then_inc(S["proj_done"], 1)
            pe.wait_ge(S["act_stage"], AFTER["w_krs"])
            pe.wait_ge(S["vec_stage"], AFTER["w_bon"])
            head_sums(4, wcum)
            pe.wait_ge(S["evac"], NCH)
            pe.wait_ge(S["vec_stage"], AFTER["w_prep"])
            for i, (t0, n) in enumerate(TILES):
                if i >= 2:
                    pe.wait_ge(S["vt_act"], i - 1)
                c0 = tile_cols(i)
                for pair in range(2):
                    last = tr(ps[0:n, 6 + i % 2, pair * P:(pair + 1) * P], hb[:, DV + pair, c0:c0 + n], ident)
                last.then_inc(S["vt_pe"], 1)
            def scores(u):
                i, h = divmod(u, HEADS)
                n, c0 = heads_n(u), tile_cols(i)
                pair, pb = HEADP[h]
                r = slice(pb, pb + HD)
                if u < LONG:
                    if u >= 4:
                        pe.wait_ge(S["s_exp"], u - 3)
                    segs = [(hb[r, DK + pair, PAD:PAD + P * (i + 1)], Fp[:, 0:P * (i + 1)])]
                    b = u % 4
                else:
                    if u == LONG:
                        pe.wait_ge(S["ld_cache"], 32)
                        pe.wait_ge(S["s_exp"], LONG - 1)
                    else:
                        pe.wait_ge(S["s_exp"], LONG)
                        pe.wait_ge(S["o_act"], LONG if u == LONG + 1 else u - 1)
                    segs = [(kcT[r, pair, 0:512], Fs[:, 0:512]), (kcT[r, pair, 512:PAST], Fs[:, 512:PAST]),
                            (hb[r, DK + pair, SCOL:SCOL + TS], Fs[:, PAST:])]
                    b = 3 * (u % 2)
                for k, (keys, f) in enumerate(segs):
                    nk = keys.shape[1]
                    diag = k == len(segs) - 1
                    mm(ps[0:n, b + k, 0:nk], hb[r, DQ + pair, c0:c0 + n], keys, start=True, stop=False,
                       skip_group_check=True)
                    last = mm(ps[0:n, b + k, 0:nk], sel[:, SEL_F + h, 0:n], f, start=False, stop=not diag,
                              skip_group_check=True)
                    if diag:
                        last = mm(ps[0:n, b + k, nk - n:nk], ident[:, 0:n], C("neg_causal")[:, 0:n],
                                  start=False, stop=True, skip_group_check=True)
                last.then_inc(S["s_done"], 1)

            def transposes(u):
                n, s = heads_n(u), sc[u % 2]
                pe.wait_ge(S["p_ready"], u + 1)
                if u >= 2:
                    pe.wait_ge(S["pt_copied"], u - 1)
                for k in range(heads_keys(u) // P):
                    last = tr(ps[:, 6 + u % 2, k * n:(k + 1) * n], s[0:n, k * P:(k + 1) * P], ident[0:n, 0:n])
                if u >= LONG:
                    last = tr(ps[LOW, out_bank(u) + 2, 64:128], s[0:n, PAST:], ident[0:n, 0:n])
                last.then_inc(S["t_done"], 1)

            def values(u):
                i, h = divmod(u, HEADS)
                n = heads_n(u)
                pair, pb = HEADP[h]
                hs = slice(h * HD, (h + 1) * HD)
                pe.wait_ge(S["pt_copied"], u + 1)
                if 2 <= u < LONG:
                    pe.wait_ge(S["o_act"], u - 1)
                out = ps[pb:pb + HD, out_bank(u), 0:n]
                if u < LONG:
                    for k in range(i + 1):
                        last = mm(out, vtok[:, k, hs], pT[:, u % 2, k * P:(k + 1) * P], start=(k == 0), stop=(k == i))
                else:
                    for k in range(8):
                        mm(out, vc[:, k, hs], pT[:, u % 2, k * n:(k + 1) * n], start=(k == 0), stop=False)
                    last = mm(out, vtok[LOW, 4, hs], pT[LOW, u % 2, 512:T], start=False, stop=True)
                last.then_inc(S["pv_done"], 1)

            for u in range(3):
                scores(u)
            for u in range(UNITS):
                if u + 3 < LONG:
                    scores(u + 3)
                if u == LONG - 2:
                    scores(LONG)
                transposes(u)
                if 1 <= u <= LONG:
                    values(u - 1)
                if LONG <= u < UNITS - 1:
                    scores(u + 1)
                if u >= LONG:
                    values(u)
            pe.wait_ge(S["o_act"], UNITS)
            def begin_operands(k):
                i, m = divmod(k, 2)
                t0, n = TILES[i]
                ts = slice(t0, t0 + n)
                if k >= 2:
                    pe.wait_ge(S["u_S"], chunks_before(k - 1))
                    pe.wait_ge(S["u_O"], k - 1)
                if m == 0:
                    for p_ in range(2):
                        tr(ps[0:n, 0, p_ * P:(p_ + 1) * P], gk[:, p_, ts], ident)
                        tr(ps[0:n, 0, GW + p_ * P:GW + (p_ + 1) * P], gv[:, p_, ts], ident)
                    for h in range(HEADS):
                        last = mm(ps[0:n, 1, h * n:(h + 1) * n], sel[ROWS, SEL_G + h, 0:n], rowG[ROWS, ts], start=True, stop=True)
                else:
                    for p_ in range(2):
                        for b, q, src in ((4, 0, Au), (4, 1, xmv), (5, 0, Bb), (5, 1, Kb)):
                            last = tr(ps[0:n, b, q * GW + p_ * P:q * GW + (p_ + 1) * P], src[:, p_, ts], ident)
                last.then_inc(S["u_tr"], 1)

            def begin_products(k):
                i, m = divmod(k, 2)
                t0, n = TILES[i]
                ts = slice(t0, t0 + n)
                if m == 0:
                    for h, (pair, pb) in enumerate(HEADP):
                        r = slice(pb, pb + HD)
                        kch = gk[r, pair, ts]
                        b = 2 + h % 2
                        mm(ps[0:n, b, pair * n:(pair + 1) * n], kch, kch, start=True, stop=True)
                        last = mm(ps[0:n, b, (2 + pair) * n:(3 + pair) * n], kch, gq[r, pair, ts], start=True, stop=True)
                else:
                    pe.wait_ge(S["u_tok"], i + 1)
                    for h in (1, 3, 0, 2):
                        pair, pb = HEADP[h]
                        r = slice(pb, pb + HD)
                        b = 4 + 2 * (h % 2)
                        for b_, q, lhs, rhs in ((b, 0, ac, bc), (b, 2, kc, ac), (b + 1, 0, bc, rc), (b + 1, 2, kc, rc)):
                            last = mm(ps[0:n, b_, (q + pair) * n:(q + pair + 1) * n], lhs[r, pair, ts], rhs[r, pair, ts],
                                      start=True, stop=True)
                last.then_inc(S["u_A"], 1)

            def begin_transposes(k):
                i, m = divmod(k, 2)
                n, u = TILES[i][1], U[m]
                pe.wait_ge(S["u_diag"], k + 1)
                for h in range(HEADS):
                    last = tr(ps[0:n, mixer_bank[m] + 1, h * n:(h + 1) * n], u["N"][0:n, h, 0:n], ident[0:n, 0:n])
                last.then_inc(S["u_NTp"], 1)
                if m:
                    for h in range(HEADS):
                        last = mm(ps[0:n, 4, h * HD:(h + 1) * HD], Aak[0:n, h, 0:n], V[0:n, h], start=True, stop=True)
                    last.then_inc(S["u_P"], 1)

            def join_middle(k, s):
                i, m = divmod(k, 2)
                n, u = TILES[i][1], U[m]
                if s:
                    pe.wait_ge(S["u_Dd"], (NJ - 1) * k + s)
                else:
                    pe.wait_ge(S["u_NTs"], k + 1)
                    pe.wait_ge(S["u_D0"], k + 1)
                for h in range(HEADS):
                    last = mm(ps[0:n, mixer_bank[m] + 2, h * n:(h + 1) * n], u["NT"][0:n, h, 0:n],
                              u["ED"][0:n, 1, h, 0:n], start=True, stop=True)
                last.then_inc(S["u_T1p"], 1)

            def join_sum(k, s):
                i, m = divmod(k, 2)
                n, u, b = TILES[i][1], U[m], mixer_bank[m]
                if s:
                    pe.wait_ge(S["u_Es"], NJ * k + s)
                else:
                    pe.wait_ge(S["u_E0"], k + 1)
                    if m:
                        pe.wait_ge(S["u_Pq"], i + 1)
                pe.wait_ge(S["u_T1"], NJ * k + s + 1)
                E_ = u["ED"][0:n, 0]
                if s < NJ - 1:
                    for h in range(HEADS):
                        last = mm(ps[0:n, b + 1, h * n:(h + 1) * n], E_[:, h, 0:n], u["T1"][0:n, h, 0:n], start=True, stop=True)
                    last.then_inc(S["u_Dp"], 1)
                for h in range(HEADS):
                    last = mm(ps[0:n, b, h * n:(h + 1) * n], u["T1"][0:n, h, 0:n], E_[:, h, 0:n], start=True, stop=True)
                last.then_inc(S["u_Ep"], 1)

            def end_solve(k):
                i, m = divmod(k, 2)
                n, u = TILES[i][1], U[m]
                pe.wait_ge(S["u_Es"], NJ * (k + 1))
                for h in range(HEADS):
                    last = mm(ps[0:n, mixer_bank[m] + 3, h * P:(h + 1) * P], u["ED"][0:n, 0, h, 0:n], u["QP"][0:n, h],
                              start=True, stop=True)
                last.then_inc(S["u_TPQp"], 1)

            def end_stack(k):
                i, m = divmod(k, 2)
                (t0, n), u, b = TILES[i], U[m], mixer_bank[m]
                pe.wait_ge(S["u_TPQ"], k + 1)
                R_ = (gR, Ru)[m]
                for h, (pair, pb) in enumerate(HEADP):
                    at = (h % 2) * 256
                    mm(ps[:, b + h // 2, at:at + P + n], u["TPQ"][0:n, h], u["BA"][0:n, h, 0:P + n], start=True, stop=False,
                       skip_group_check=True)
                    if m == 1:
                        mm(ps[LOW, b + h // 2, at:at + P + n], V[0:n, h], KA[0:n, h, 0:P + n], start=False, stop=False,
                           skip_group_check=True)
                    last = mm(ps[:, b + h // 2, at + P:at + P + n], C(f"shift{h % 2}"), R_[:, pair, t0:t0 + n],
                              start=False, stop=True, skip_group_check=True)
                last.then_inc(S["u_OUTp"], 1)

            def end_chunk(k, c):
                i, m = divmod(k, 2)
                n, u, b = TILES[i][1], U[m], mixer_bank[m]
                ch = 2 * i + c
                slot = 3 if ch == 8 else ch % 3
                if k >= 8:
                    pe.wait_ge(S["ld_state"], 48)
                if k < 2:
                    pe.wait_ge(S["u_zero_C"], 1)
                if c == 0:
                    pe.wait_ge(S["u_OUTs"], k + 1)
                    pe.wait_ge(S["u_OUTv"], k + 1)
                    if k >= 2:
                        pe.wait_ge(S["u_S"], chunks_before(k - 1))
                else:
                    pe.wait_ge(S["u_S"], chunks_before(k) + 1)
                for h in range(HEADS):
                    last = mm(ps[TOP, b + 2, c * GW + h * HD:c * GW + (h + 1) * HD], u["OUT"][:, h, c * CHUNK:(c + 1) * CHUNK],
                              u["IS"][:, slot, h], start=True, stop=True)
                last.then_inc(S["u_Sp"], 1)
                for h, (pair, pb) in enumerate(HEADP):
                    last = mm(ps[pb:pb + HD, b + 3, pair * n + c * CHUNK:pair * n + (c + 1) * CHUNK], u["IS"][:, slot, h],
                              u["OUT"][:, h, P + c * CHUNK:P + (c + 1) * CHUNK], start=True, stop=True)
                if c == chunks_of(k) - 1:
                    last.then_inc(S["u_Op"], 1)

            def piece_sums(x, m, src):
                t0, n = NORM_PIECES[x]
                for c in range(2):
                    last = mm(norm_banks(x, m)[:, c], C("head_ones"), src[:, c, t0:t0 + n], start=True, stop=True)
                last.then_inc(S["pe_stage"], 1)

            def norm_sums(x):
                pe.wait_ge(S["act_stage"], AFTER[f"p_gsq{x}"])
                piece_sums(x, 0, ta)
                piece_sums(x, 1, mixT[:, 4:6])

            def norm_variance(x):
                pe.wait_ge(S["act_stage"], AFTER[f"p_rsq{x}"])
                piece_sums(x, 1, tb)

            def project(i):
                t0, n = TILES[i]
                pe.wait_ge(S["vec_stage"], AFTER["p_done0" if i < 4 else "p_done1"])
                pe.wait_ge(S["act_stage"], AFTER["p_rrs0"])
                pe.wait_ge(S["ld_wout"], 16 * 8)
                if i >= 2:
                    pe.wait_ge(S["o_x"], i - 1)
                for q in range(2):
                    for k in range(KD):
                        last = mm(ps[0:n, 2 * (i % 2) + q, :], mixT[:, k, t0:t0 + n], wout[k][:, q * 512:(q + 1) * 512],
                                  start=(k == 0), stop=(k == KD - 1))
                last.then_inc(S["o_y"], 1)

            def x1_transposes(i):
                t0, n = TILES[i]
                pe.wait_ge(S["o_x1"], i + 1)
                if i:
                    pe.wait_ge(S["o_x1T"], i)
                for k in range(KD):
                    last = tr(ps[:, 4 + k // 4, (k % 4) * n:(k % 4 + 1) * n], x1[0:n, i, k * P:(k + 1) * P], ident[0:n, 0:n])
                last.then_inc(S["o_x1t"], 1)

            def logits(i):
                t0, n = TILES[i]
                pe.wait_ge(S["o_x1T"], i + 1)
                pe.wait_ge(S["ld_router"], 48)
                for k in range(KD):
                    last = mm(ps[0:n, 6, i * 20:(i + 1) * 20], x1T[:, k, t0:t0 + n], wr[:, k], start=(k == 0), stop=(k == KD - 1))
                if i == NT - 1:
                    last.then_inc(S["pe_stage"], 1)

            begin_operands(0)
            begin_products(0)
            begin_transposes(0)
            for k in range(JOBS + 1):
                joins, ends, begins = k < JOBS, k > 0, k + 1 < JOBS
                if ends:
                    end_solve(k - 1)
                if joins:
                    join_middle(k, 0)
                if ends:
                    end_stack(k - 1)
                if joins:
                    join_sum(k, 0)
                    join_middle(k, 1)
                    join_sum(k, 1)
                if k == JOBS:
                    project(0)
                if ends:
                    end_chunk(k - 1, 0)
                if joins:
                    join_middle(k, 2)
                if ends and chunks_of(k - 1) == 2:
                    end_chunk(k - 1, 1)
                if joins:
                    join_sum(k, 2)
                if k == JOBS - 1:
                    pe.wait_ge(S["u_O"], JOBS - 1)
                    pe.wait_ge(S["u_S"], 17)
                    norm_sums(0)
                if begins:
                    begin_operands(k + 1)
                if joins:
                    join_middle(k, 3)
                if begins:
                    begin_products(k + 1)
                if joins:
                    join_sum(k, 3)
                    join_middle(k, 4)
                    join_sum(k, 4)
                if k == JOBS - 1:
                    norm_variance(0)
                if begins:
                    begin_transposes(k + 1)
            for i in range(1, NT):
                project(i)
                if i == 1:
                    pe.wait_ge(S["u_S"], 18)
                    pe.wait_ge(S["u_O"], JOBS)
                x1_transposes(i - 1)
                if i == 1:
                    norm_sums(1)
                elif i == 2:
                    norm_variance(1)
                if i >= 2:
                    logits(i - 2)
            x1_transposes(NT - 1)
            logits(NT - 2)
            logits(NT - 1)
            pe.wait_ge(S["vec_stage"], AFTER["r_mask"])
            pe.wait_ge(S["ld_router"], 48)
            before, ones = slot_c[:, 0:P], slot_c[:, P:2 * P]
            r7 = ps[:, 7, 0:(NT + 1) * EXPERTS].rearrange("p (i e) -> p i e", e=EXPERTS)
            for j in range(NT):
                mm(r7[:, j + 1:], ones, bc_mid(Mx[:, j], NT - j), start=(j == 0), stop=False, skip_group_check=True)
            last = mm(r7[:, 1:NT], before, Mx[:, 1:NT], start=False, stop=True, skip_group_check=True)
            last = mm(r7[:, 0:1], before, Mx[:, 0:1], start=True, stop=True, skip_group_check=True)
            last.then_inc(S["pe_stage"], 1)
            pe.wait_ge(S["vec_stage"], AFTER["r_slots"])
            pe.wait_ge(S["o_x"], NT)

            def block_in(e):
                pe.wait_ge(ld_xb[e % 2], 16 * (e // 2 + 1))
                if e:
                    pe.wait_ge(S["x_ta"], e)
                    pe.wait_ge(S["x_tv"], e)
                for k in range(KD):
                    last = tr(ps[:, k // 4, (k % 4) * P:(k % 4 + 1) * P], xb[e % 2][:, k * P:(k + 1) * P], ident)
                last.then_inc(S["x_t"], 1)

            block_in(0)
            for e in range(EXPERTS + 1):
                if e + 1 < EXPERTS:
                    block_in(e + 1)
                if e:
                    pe.wait_ge(S["x_h"], e)
                    if e >= 2:
                        pe.wait_ge(S["x_hT"], e - 1)
                    for f in range(2):
                        last = tr(ps[:, 4, f * P:(f + 1) * P], hrow[:, f * P:(f + 1) * P], ident)
                    last.then_inc(S["x_ht"], 1)
                if e < EXPERTS:
                    pe.wait_ge(ld_e[e % 2], 16 * (e // 2 + 1))
                    pe.wait_ge(S["x_ta"], e + 1)
                    pe.wait_ge(S["x_tv"], e + 1)
                    if e >= 2:
                        pe.wait_ge(S["x_h"], e - 1)
                    for k in range(KD):
                        last = mm(ps[:, 2 + e % 2], xbT[e % 2][:, k], wgu[e % 2][:, k], start=(k == 0), stop=(k == KD - 1))
                    last.then_inc(S["x_gu"], 1)
                if e:
                    pe.wait_ge(S["x_hT"], e)
                    if e >= 2:
                        pe.wait_ge(S["x_ya"], e - 1)
                        pe.wait_ge(S["x_yv"], e - 1)
                    pe.wait_ge(ld_f[(e - 1) % 2], 16 * ((e - 1) // 2 + 1))
                    for q in range(2):
                        for f in range(2):
                            last = mm(ps[:, 5 + q], hTs[:, f], wdn[(e - 1) % 2][:, f, q * 512:(q + 1) * 512],
                                      start=(f == 0), stop=(f == 1))
                    last.then_inc(S["x_dn"], 1)
            pe.wait_ge(S["x_ya"], EXPERTS)
            pe.wait_ge(S["x_yv"], EXPERTS)
            most = pe.value_load(idx[0:1, 2 * NT:], min_val=0, max_val=T)
            with pe.If(most > CAP):
                for e in range(EXPERTS):
                    pe.wait_ge(ld_d[e % 2], 32 * (e // 2 + 1))
                    if e:
                        pe.wait_ge(S["m_acc"], NT * e)
                    for f in range(2):
                        for w_ in range(2):
                            for h in range(2):
                                for k in range(KD):
                                    last = mm(ps[:, 4 * f + 2 * w_ + h, 0:HALF], wgu[e % 2][:, k, w_ * FF + f * P:w_ * FF + (f + 1) * P],
                                              x1T[:, k, h * HALF:(h + 1) * HALF], start=(k == 0), stop=(k == KD - 1))
                        last.then_inc(S["m_gu"], 1)
                    pe.wait_ge(S["m_h"], 2 * e + 2)
                    for i, (t0, n) in enumerate(TILES):
                        if i >= 2:
                            pe.wait_ge(S["m_acc"], NT * e + i - 1)
                        for q in range(2):
                            for f in range(2):
                                last = mm(ps[0:n, 2 * (i % 2) + q, :], hT[:, f, t0:t0 + n], wdn[e % 2][:, f, q * 512:(q + 1) * 512],
                                          start=(f == 0), stop=(f == 1))
                        last.then_inc(S["m_dn"], 1)


OUTS = {"o_y": (T, D), "o_gconv": (P, 2, 6, PAD), "o_shift": (P, 2, 7), "o_kv": (P, 4, T), "o_logf": (HEADS, T),
        "o_conv": (P, 2, 2, CPAD), "o_state": (2, 2, HD, HEADS, HD)}


def square_constants():
    i, j = np.arange(P)[:, None], np.arange(P)[None, :]
    same = i // CHUNK == j // CHUNK
    lower = same & (i > j)
    c = {"ident": i == j, "strict_l": lower, "strict_u": lower.T, "incl_u": same & (i <= j),
         "neg_strict_l": np.where(lower, 0, NEG), "neg_incl_u": np.where(same & (i <= j), 0, NEG)}
    for b in (1, 2, 4, 8, 16, 32):
        join = (i // (2 * b) == j // (2 * b)) & (i // b % 2 == 1) & (j // b % 2 == 0)
        if b == 1:
            c["first_l"], c["first_u"] = join | (i == j), join.T | (i == j)
        else:
            c[f"join{b}"] = join
    c["neg_causal"] = np.where(j <= i, 0, NEG)
    c["head_ones"] = same
    c["mean_ones"] = np.full((P, P), 1.0 / GW)
    for q in range(2):
        c[f"shift{q}"] = (j >= HD) & (i == j - HD + q * HD)
    return np.stack([np.asarray(c[n], np.float32) for n in CONST], 1)


def row_selectors():
    s = np.zeros((P, NSEL, P), np.float32)
    for h in range(HEADS):
        s[96 + h, SEL_G + h, :] = 1.0
        s[104 + h, SEL_F + h, :] = -float(HD) ** 0.5
        s[96 + h, SEL_PAIR + h // 2, (h % 2) * HD:(h % 2 + 1) * HD] = 1.0
    return s


def layout(x):
    g = {k: np.asarray(v) for k, v in x.items()}
    z = np.zeros
    f32 = np.float32
    o = {}
    xx = np.concatenate([g["x_prompt"][0], g["x_sample"][0]], 0)
    o["x_tok"] = xx
    o["xT"] = xx.T.reshape(KD, P, T).transpose(1, 0, 2)
    w = g["w_in"][0]
    nA, nB = 2 * GW, 4 * GW + 2 * HEADS
    nC = 3 * GW + 64
    A, B, Cc, Dd = w[:, :nA], w[:, nA:nA + nB], w[:, nA + nB:nA + nB + nC], w[:, nA + nB + nC:]
    sm = z((D, P), f32)
    sm[:, 0:16], sm[:, 32:48], sm[:, 64:96] = Cc[:, 768:784], Cc[:, 784:800], Cc[:, 800:832]
    sm[:, 96:104], sm[:, 104:108] = B[:, 1024:1032], Dd[:, 768:772]
    cols = np.concatenate([sm, A, B[:, :1024], Cc[:, :768], Dd[:, :768]], 1)
    o["w_in"] = cols.reshape(KD, P, NCH, P).transpose(2, 1, 0, 3)
    pads = z((P, NCH, PAD), f32)
    pads[:, BQ:BQ + 6] = g["state_gdn_conv"][0, 0].T.reshape(6, P, PAD).transpose(1, 0, 2)
    sh = g["state_rwkv_shift"][0, 0]
    pads[:, CR:CR + 6, 2] = sh[:768].reshape(6, P).T
    pads[0:16, 0, 2], pads[32:48, 0, 2], pads[64:96, 0, 2] = sh[768:784], sh[784:800], sh[800:832]
    o["pads"] = pads
    o["conv_state"] = g["state_conv"][0, 0].T.reshape(2, P, CPAD).transpose(1, 0, 2)
    o["s_gdn"] = g["state_gdn"][0, 0].transpose(1, 0, 2)
    o["s_rwkv"] = g["state_rwkv"][0, 0].transpose(2, 0, 1)
    o["k_cache"] = g["cache_fox_k"][0, 0].transpose(1, 2, 0).reshape(2, P, PAST).transpose(1, 0, 2)
    o["v_cache"] = g["cache_fox_v"][0, 0].reshape(8, P, GW).transpose(1, 0, 2)
    fc = z((12, PAST), f32)
    fc[8:12] = g["cache_fox_logf"][0, 0].T
    o["f_cache"] = fc
    par = z((P, NPC), f32)

    def put(name, arr):
        arr = np.asarray(arr, f32)
        if arr.ndim == 1:
            arr = arr[:, None]
        k = arr.shape[1]
        a3 = arr.reshape(-1, P, k).transpose(1, 0, 2).reshape(P, -1)
        par[:, PCOL[name]:PCOL[name] + a3.shape[1]] = a3

    put("conv_w", g["conv_w"][0].T)
    put("conv_b", g["conv_b"][0]), put("conv_g", g["conv_ln_g"][0]), put("conv_lb", g["conv_ln_b"][0])
    put("gconv_w", g["gdn_conv_w"][0].T)
    put("gnorm", np.concatenate([g["gdn_norm_w"][0]] * 2))
    mu = g["rwkv_mu"][0]
    put("mu", mu[:768])
    c = PCOL["mu_s"]
    par[0:16, c], par[32:48, c], par[64:96, c] = mu[768:784], mu[784:800], mu[800:832]
    for n, k in (("w0", "rwkv_w0"), ("a0", "rwkv_a0"), ("k_k", "rwkv_k_k"), ("k_a", "rwkv_k_a"),
                 ("lnx_g", "rwkv_lnx_g"), ("lnx_b", "rwkv_lnx_b")):
        put(n, g[k][0])
    put("r_k", g["rwkv_r_k"][0].reshape(-1))
    par[96:100, PCOL["row_bias"]], par[104:108, PCOL["row_bias"]] = g["gdn_dt_bias"][0], g["fox_b_f"][0]
    par[96:100, PCOL["row_alog"]] = g["gdn_a_log"][0]
    par[96:100, PCOL["row_sign"]], par[100:108, PCOL["row_sign"]] = 1.0, -1.0
    o["params"] = par
    lo = z((P, GW), f32)
    lo[0:16], lo[32:48], lo[64:96] = g["rwkv_w_up"][0], g["rwkv_a_up"][0], g["rwkv_g_up"][0]
    o["lora"] = lo
    cm = np.ones((P, T), f32)
    cm[:, ::CHUNK] = 0
    o["ch_mask"] = cm
    o["consts"], o["sel"] = square_constants(), row_selectors()
    o["w_out"] = g["w_out"][0].reshape(8, P, D).transpose(1, 0, 2)
    o["ln"] = np.stack([g[k][0] for k in ("ln1_g", "ln1_b", "ln2_g", "ln2_b")])
    ij = np.arange(P)
    o["slot_c"] = np.concatenate([(ij[:, None] < ij[None, :]).astype(f32), np.ones((P, P), f32),
                                  np.tile(np.arange(EXPERTS, dtype=f32), (P, 1)),
                                  (ij[:, None] + P * np.arange(NT)[None, :]).astype(f32)], 1)
    o["w_router"] = np.concatenate([g["router_g_w"][0], g["router_e_w"][0]], 1).reshape(KD, P, 20).transpose(1, 0, 2)
    o["b_router"] = np.concatenate([g["router_g_b"][0], g["router_e_b"][0]])[None]
    gu = np.concatenate([g["exp_w_gate"][0], g["exp_w_up"][0]], 2)
    o["w_gu"] = gu.reshape(EXPERTS, KD, P, 2 * FF).transpose(0, 2, 1, 3)
    o["w_dn"] = g["exp_w_down"][0].reshape(EXPERTS, 2, P, D).transpose(0, 2, 1, 3)
    return {k: np.ascontiguousarray(v) for k, v in o.items()}


def restore(r):
    y = r["o_y"]
    out = [y[None, :TP], y[None, TP:]]
    for k in range(2):
        t = slice(0, TP) if k == 0 else slice(TP, T)
        n = TP if k == 0 else TS
        sh = r["o_shift"][:, k]
        shift = np.concatenate([sh[:, :6].T.reshape(-1), sh[0:16, 6], sh[32:48, 6], sh[64:96, 6]])
        kv = [r["o_kv"][:, c:c + 2, t].transpose(2, 1, 0).reshape(1, 1, n, HEADS, HD) for c in (0, 2)]
        out += [r["o_conv"][:, k].transpose(2, 1, 0).reshape(1, 1, CPAD, GW),
                r["o_gconv"][:, k].transpose(2, 1, 0).reshape(1, 1, PAD, 3 * GW),
                r["o_state"][0, k].transpose(1, 0, 2)[None, None],
                shift[None, None],
                r["o_state"][1, k].transpose(1, 2, 0)[None, None],
                kv[0], kv[1], r["o_logf"][:, t].T[None, None]]
    return tuple(np.ascontiguousarray(v) for v in out)


def kernel(**inputs):
    import concourse.bacc as _bacc
    from concourse.bass_utils import run_bass_kernel_spmd as _run

    nc = _bacc.Bacc("TRN2", target_bir_lowering=False, num_devices=1)
    arrays = {f"in_{k}": v for k, v in layout(inputs).items()}
    a = {k[3:]: nc.dram_tensor(k, v.shape, F32, kind="ExternalInput").ap() for k, v in arrays.items()}
    a.update({k: nc.dram_tensor(k, s, F32, kind="ExternalOutput").ap() for k, s in OUTS.items()})
    step_kernel(nc, a)
    r = _run(nc, [arrays], core_ids=[0])
    return restore(r.results[0])
```
